# Optimizing a Trainium2 kernel written in Bass

```python
import math
import jax
import jax.numpy as jnp
from jax import lax
import numpy as np

D_MODEL = 1024
BATCH = 1
SEQ = 512
DEPTH = 4

CHUNK = 64
N_META = 16
N_MIXERS = 4
EPS = 1e-6
NEG_INF = -1e30
ROPE_BASE = 10000.0
Q_BLOCK = 128

MLA_HEADS = 8
MLA_NOPE = 128
MLA_ROPE = 64
MLA_V = 128
MLA_QK = MLA_NOPE + MLA_ROPE
MLA_Q_LORA = 384
MLA_KV_LORA = 256

HGRN_EXPAND = 128
HGRN_HEADS = D_MODEL // HGRN_EXPAND
HGRN_DK = HGRN_EXPAND
HGRN_DV = D_MODEL // HGRN_HEADS
HGRN_CHUNK = 16

S5_GROUP = 16
S5_GROUPS = D_MODEL // S5_GROUP
S5_STATE = 64
S5_DT_MIN = 1e-3
S5_DT_MAX = 1e-1

RET_HEADS = 4
RET_DK = D_MODEL // RET_HEADS
RET_DV = 2 * RET_DK

FFN_HIDDEN = 2816
CONV_WIDTH = 3

N_MLA_L = (DEPTH + 3) // 4
N_HGRN_L = (DEPTH + 2) // 4
N_S5_L = (DEPTH + 1) // 4
N_RET_L = DEPTH // 4

kernel_name = "chunk_causal_hybrid_trunk"

F32 = jnp.float32

def rms_norm(x, g):
    xf = x.astype(F32)
    y = xf * lax.rsqrt(jnp.mean(xf * xf, axis=-1, keepdims=True) + EPS)
    return (y * g.astype(F32)).astype(x.dtype)

def rope_tables(n_pos, dim):
    inv_freq = 1.0 / (ROPE_BASE ** (jnp.arange(0, dim, 2, dtype=F32) / dim))
    ang = jnp.arange(n_pos, dtype=F32)[:, None] * inv_freq[None, :]
    return jnp.cos(ang), jnp.sin(ang)

def apply_rope(x, cos, sin):
    half = x.shape[-1] // 2
    x1, x2 = x[..., :half], x[..., half:]
    c = cos[None, :, None, :].astype(x.dtype)
    s = sin[None, :, None, :].astype(x.dtype)
    return jnp.concatenate([x1 * c - x2 * s, x1 * s + x2 * c], axis=-1)

def pad_front(t, n):
    return jnp.pad(t, [(0, 0), (n, 0)] + [(0, 0)] * (t.ndim - 2))

def chunk_ids(n_pos):
    real = 1 + jnp.arange(n_pos - N_META, dtype=jnp.int32) // CHUNK
    return jnp.concatenate([jnp.zeros((N_META,), jnp.int32), real])

def mla_mixer(a, w_down, g_cq, g_ckv, w_uq, w_ukv, g_qhead, g_khead, w_o, cos, sin, cid):
    B, L, _ = a.shape
    H = MLA_HEADS
    down = a @ w_down
    c_q = rms_norm(down[..., :MLA_Q_LORA], g_cq)
    c_kv = rms_norm(down[..., MLA_Q_LORA:MLA_Q_LORA + MLA_KV_LORA], g_ckv)
    k_pe = down[..., MLA_Q_LORA + MLA_KV_LORA:]
    q = (c_q @ w_uq).reshape(B, L, H, MLA_QK)
    kv = (c_kv @ w_ukv).reshape(B, L, H, MLA_NOPE + MLA_V)
    k = jnp.concatenate(
        [kv[..., :MLA_NOPE], jnp.broadcast_to(k_pe[:, :, None, :], (B, L, H, MLA_ROPE))], axis=-1)
    v = kv[..., MLA_NOPE:]
    q = rms_norm(q, g_qhead)
    k = rms_norm(k, g_khead)
    q = jnp.concatenate([q[..., :MLA_NOPE], apply_rope(q[..., MLA_NOPE:], cos, sin)], axis=-1)
    k = jnp.concatenate([k[..., :MLA_NOPE], apply_rope(k[..., MLA_NOPE:], cos, sin)], axis=-1)
    scale = MLA_QK ** -0.5

    def attend(qb, kb, vb, mask):
        s = jnp.einsum("bqhd,bkhd->bhqk", qb, kb).astype(F32) * scale
        s = jnp.where(mask[None, None], s, NEG_INF)
        p = jax.nn.softmax(s, axis=-1).astype(vb.dtype)
        return jnp.einsum("bhqk,bkhd->bqhd", p, vb)

    o_meta = attend(q[:, :N_META], k[:, :N_META], v[:, :N_META], jnp.ones((N_META, N_META), bool))
    n_real = L - N_META
    n_blk = n_real // Q_BLOCK
    q_blk = q[:, N_META:].reshape(B, n_blk, Q_BLOCK, H, MLA_QK).transpose(1, 0, 2, 3, 4)
    cid_blk = cid[N_META:].reshape(n_blk, Q_BLOCK)
    o_real = lax.map(lambda args: attend(args[0], k, v, cid[None, :] <= args[1][:, None]),
                     (q_blk, cid_blk))
    o_real = o_real.transpose(1, 0, 2, 3, 4).reshape(B, n_real, H, MLA_V)
    o = jnp.concatenate([o_meta, o_real], axis=1).reshape(B, L, H * MLA_V)
    return o @ w_o

def gla_chunkwise(q, k, v, log_f, chunk):
    B, L, H, DK = q.shape
    DV = v.shape[-1]
    n_pad = (-L) % chunk
    NC = (L + n_pad) // chunk

    def to_chunks(t):
        return pad_front(t, n_pad).reshape(B, NC, chunk, H, t.shape[-1]).transpose(1, 0, 3, 2, 4)

    qc, kc, vc, gc = map(to_chunks, (q, k, v, log_f))
    G = jnp.cumsum(gc, axis=3)
    G_last = G[..., -1:, :]
    q_dec = qc * jnp.exp(G)
    k_inv = kc * jnp.exp(-G)
    k_tail = kc * jnp.exp(G_last - G)
    causal = jnp.tril(jnp.ones((chunk, chunk), bool))
    attn = jnp.where(causal, jnp.einsum("nbhid,nbhjd->nbhij", q_dec, k_inv), 0.0)
    o_intra = jnp.einsum("nbhij,nbhjv->nbhiv", attn, vc)

    def step(state, xs):
        qd, kt, vv, gl = xs
        o_inter = jnp.einsum("bhid,bhdv->bhiv", qd, state)
        state = state * jnp.exp(gl)[:, :, 0, :, None] + jnp.einsum("bhjd,bhjv->bhdv", kt, vv)
        return state, o_inter

    _, o_inter = lax.scan(step, jnp.zeros((B, H, DK, DV), F32), (q_dec, k_tail, vc, G_last))
    o = (o_intra + o_inter).transpose(1, 0, 3, 2, 4).reshape(B, NC * chunk, H, DV)
    return o[:, n_pad:]

def hgrn2_mixer(a, w_in, lb, g_o, w_o):
    B, L, _ = a.shape
    H = HGRN_HEADS
    q, f, i_in, g = jnp.split(a @ w_in, 4, axis=-1)
    q = jax.nn.silu(q.astype(F32))
    forget = lb + (1.0 - lb) * jax.nn.sigmoid(f.astype(F32))
    log_f = jnp.log(forget)
    k = 1.0 - forget
    shp = (B, L, H, HGRN_DK)
    o = gla_chunkwise(q.reshape(shp), k.reshape(shp),
                      i_in.astype(F32).reshape(B, L, H, HGRN_DV), log_f.reshape(shp), HGRN_CHUNK)
    o = rms_norm(o, g_o).reshape(B, L, H * HGRN_DV) * jax.nn.silu(g.astype(F32))
    return o.astype(a.dtype) @ w_o

def _complex_affine_combine(e1, e2):
    a1r, a1i, b1r, b1i = e1
    a2r, a2i, b2r, b2i = e2
    return (a2r * a1r - a2i * a1i,
            a2r * a1i + a2i * a1r,
            a2r * b1r - a2i * b1i + b2r,
            a2r * b1i + a2i * b1r + b2i)

def s5_mixer(a, lam_re, lam_im, log_dt, b_re, b_im, c_re, c_im, d_skip, w_glu):
    B, L, D = a.shape
    G, P, K, C = S5_GROUPS, S5_STATE, S5_GROUP, CHUNK
    lam_re, lam_im = lam_re.astype(F32), lam_im.astype(F32)
    b_re, b_im = b_re.astype(F32), b_im.astype(F32)
    c_re, c_im = c_re.astype(F32), c_im.astype(F32)
    dt = jnp.exp(log_dt.astype(F32))[:, None]
    mag = jnp.exp(lam_re * dt)
    abar_re = mag * jnp.cos(lam_im * dt)
    abar_im = mag * jnp.sin(lam_im * dt)
    den = lam_re * lam_re + lam_im * lam_im
    zoh_re = ((abar_re - 1.0) * lam_re + abar_im * lam_im) / den
    zoh_im = (abar_im * lam_re - (abar_re - 1.0) * lam_im) / den
    bbar_re = zoh_re[..., None] * b_re - zoh_im[..., None] * b_im
    bbar_im = zoh_re[..., None] * b_im + zoh_im[..., None] * b_re
    steps = (jnp.arange(C, dtype=F32) + 1.0)[:, None, None] * dt[None]
    pmag = jnp.exp(lam_re[None] * steps)
    pow_re = pmag * jnp.cos(lam_im[None] * steps)
    pow_im = pmag * jnp.sin(lam_im[None] * steps)

    n_pad = (-L) % C
    NC = (L + n_pad) // C
    u = pad_front(a.astype(F32), n_pad).reshape(B, NC, C, G, K).transpose(1, 0, 2, 3, 4)

    def step(carry, uc):
        xr0, xi0 = carry
        bu_re = jnp.einsum("bcgk,gpk->bcgp", uc, bbar_re)
        bu_im = jnp.einsum("bcgk,gpk->bcgp", uc, bbar_im)
        ar = jnp.broadcast_to(abar_re, bu_re.shape)
        ai = jnp.broadcast_to(abar_im, bu_im.shape)
        _, _, xr, xi = lax.associative_scan(_complex_affine_combine, (ar, ai, bu_re, bu_im), axis=1)
        xr = xr + pow_re * xr0[:, None] - pow_im * xi0[:, None]
        xi = xi + pow_re * xi0[:, None] + pow_im * xr0[:, None]
        y = jnp.einsum("bcgp,gkp->bcgk", xr, c_re) - jnp.einsum("bcgp,gkp->bcgk", xi, c_im)
        return (xr[:, -1], xi[:, -1]), y

    zeros = jnp.zeros((B, G, P), F32)
    _, y = lax.scan(step, (zeros, zeros), u)
    y = y.transpose(1, 0, 2, 3, 4).reshape(B, NC * C, D)[:, n_pad:]
    y = jax.nn.gelu(y + d_skip.astype(F32) * a.astype(F32))
    val, gate = jnp.split(y.astype(a.dtype) @ w_glu, 2, axis=-1)
    return val * jax.nn.sigmoid(gate)

def retention_mixer(a, w_in, gn_g, w_o, cos, sin):
    B, L, _ = a.shape
    H, DK, DV, C = RET_HEADS, RET_DK, RET_DV, CHUNK
    qk_w = H * DK
    q, k, v, g = jnp.split(a @ w_in, [qk_w, 2 * qk_w, 2 * qk_w + H * DV], axis=-1)
    q = apply_rope(q.reshape(B, L, H, DK), cos, sin).astype(F32)
    k = apply_rope(k.reshape(B, L, H, DK), cos, sin).astype(F32) * (DK ** -0.5)
    v = v.reshape(B, L, H, DV).astype(F32)
    n_pad = (-L) % C
    NC = (L + n_pad) // C

    def to_chunks(t):
        return pad_front(t, n_pad).reshape(B, NC, C, H, t.shape[-1]).transpose(1, 0, 3, 2, 4)

    qc, kc, vc = map(to_chunks, (q, k, v))
    log_gamma = jnp.log(1.0 - jnp.exp2(-5.0 - jnp.arange(H, dtype=F32)))
    pos = jnp.arange(C, dtype=F32)
    diff = pos[:, None] - pos[None, :]
    decay = jnp.where(diff >= 0, jnp.exp(diff[None] * log_gamma[:, None, None]), 0.0)
    scores = jnp.einsum("nbhid,nbhjd->nbhij", qc, kc) * decay
    o_intra = jnp.einsum("nbhij,nbhjv->nbhiv", scores, vc)
    q_decay = jnp.exp((pos[None, :] + 1.0) * log_gamma[:, None])[..., None]
    k_decay = jnp.exp((C - 1.0 - pos[None, :]) * log_gamma[:, None])[..., None]
    chunk_decay = jnp.exp(C * log_gamma)[:, None, None]

    def step(state, xs):
        qi, ki, vi = xs
        o_inter = jnp.einsum("bhid,bhdv->bhiv", qi * q_decay, state)
        state = state * chunk_decay + jnp.einsum("bhjd,bhjv->bhdv", ki * k_decay, vi)
        return state, o_inter

    _, o_inter = lax.scan(step, jnp.zeros((B, H, DK, DV), F32), (qc, kc, vc))
    o = (o_intra + o_inter).transpose(1, 0, 3, 2, 4).reshape(B, NC * C, H, DV)[:, n_pad:]
    mu = jnp.mean(o, axis=-1, keepdims=True)
    var = jnp.mean(jnp.square(o - mu), axis=-1, keepdims=True)
    o = ((o - mu) * lax.rsqrt(var + EPS)).reshape(B, L, H * DV)
    o = o * gn_g.astype(F32) * jax.nn.silu(g.astype(F32))
    return o.astype(a.dtype) @ w_o

def conv_glu_ffn(a, w_up, conv_w, conv_b, w_down):
    u = a @ w_up
    u = lax.conv_general_dilated(
        u, conv_w[:, None, :].astype(u.dtype), window_strides=(1,),
        padding=[(CONV_WIDTH - 1, 0)], dimension_numbers=("NWC", "WIO", "NWC"),
        feature_group_count=u.shape[-1]) + conv_b.astype(u.dtype)
    gate, val = jnp.split(u, 2, axis=-1)
    return (jax.nn.silu(gate) * val) @ w_down

def setup_inputs(seed: int = 0) -> dict:
    key = jax.random.key(seed)
    ks = iter(jax.random.split(key, 40))
    D = D_MODEL

    def nrm(shape, scale):
        return jax.random.normal(next(ks), shape, F32) * scale

    def gain(shape):
        return 1.0 + 0.02 * jax.random.normal(next(ks), shape, F32)

    n_a, n_b, n_c, n_d = N_MLA_L, N_HGRN_L, N_S5_L, N_RET_L
    return {
        "x": nrm((BATCH, SEQ, D), 1.0),
        "meta_tokens": nrm((N_META, D), 1.0),
        "norm_mix_g": gain((DEPTH, D)),
        "norm_ffn_g": gain((DEPTH, D)),
        "mla_w_down": nrm((n_a, D, MLA_Q_LORA + MLA_KV_LORA + MLA_ROPE), D ** -0.5),
        "mla_cq_norm_g": gain((n_a, MLA_Q_LORA)),
        "mla_ckv_norm_g": gain((n_a, MLA_KV_LORA)),
        "mla_w_uq": nrm((n_a, MLA_Q_LORA, MLA_HEADS * MLA_QK), MLA_Q_LORA ** -0.5),
        "mla_w_ukv": nrm((n_a, MLA_KV_LORA, MLA_HEADS * (MLA_NOPE + MLA_V)), MLA_KV_LORA ** -0.5),
        "mla_q_head_g": gain((n_a, MLA_QK)),
        "mla_k_head_g": gain((n_a, MLA_QK)),
        "mla_w_o": nrm((n_a, MLA_HEADS * MLA_V, D), (MLA_HEADS * MLA_V) ** -0.5),
        "hgrn_w_in": nrm((n_b, D, 4 * D), D ** -0.5),
        "hgrn_lb_logits": nrm((DEPTH, HGRN_HEADS * HGRN_DK), 0.1),
        "hgrn_o_norm_g": gain((n_b, HGRN_DV)),
        "hgrn_w_o": nrm((n_b, D, D), D ** -0.5),
        "s5_lam_re": -0.5 + nrm((n_c, S5_GROUPS, S5_STATE), 0.01),
        "s5_lam_im": jnp.pi * jnp.arange(S5_STATE, dtype=F32)[None, None, :] + nrm((n_c, S5_GROUPS, S5_STATE), 0.01),
        "s5_log_dt": jax.random.uniform(next(ks), (n_c, S5_GROUPS), F32,
                                        minval=math.log(S5_DT_MIN), maxval=math.log(S5_DT_MAX)),
        "s5_b_re": nrm((n_c, S5_GROUPS, S5_STATE, S5_GROUP), (2 * S5_GROUP) ** -0.5),
        "s5_b_im": nrm((n_c, S5_GROUPS, S5_STATE, S5_GROUP), (2 * S5_GROUP) ** -0.5),
        "s5_c_re": nrm((n_c, S5_GROUPS, S5_GROUP, S5_STATE), (2 * S5_STATE) ** -0.5),
        "s5_c_im": nrm((n_c, S5_GROUPS, S5_GROUP, S5_STATE), (2 * S5_STATE) ** -0.5),
        "s5_d": nrm((n_c, D), 1.0),
        "s5_w_glu": nrm((n_c, D, 2 * D), D ** -0.5),
        "ret_w_in": nrm((n_d, D, 2 * RET_HEADS * RET_DK + 2 * RET_HEADS * RET_DV), D ** -0.5),
        "ret_gn_g": gain((n_d, RET_HEADS * RET_DV)),
        "ret_w_o": nrm((n_d, RET_HEADS * RET_DV, D), (RET_HEADS * RET_DV) ** -0.5),
        "ffn_w_up": nrm((DEPTH, D, 2 * FFN_HIDDEN), D ** -0.5),
        "ffn_conv_w": nrm((DEPTH, CONV_WIDTH, 2 * FFN_HIDDEN), CONV_WIDTH ** -0.5),
        "ffn_conv_b": nrm((DEPTH, 2 * FFN_HIDDEN), 0.01),
        "ffn_w_down": nrm((DEPTH, FFN_HIDDEN, D), FFN_HIDDEN ** -0.5),
    }

def reference(x, meta_tokens, norm_mix_g, norm_ffn_g,
              mla_w_down, mla_cq_norm_g, mla_ckv_norm_g, mla_w_uq, mla_w_ukv, mla_q_head_g, mla_k_head_g, mla_w_o,
              hgrn_w_in, hgrn_lb_logits, hgrn_o_norm_g, hgrn_w_o,
              s5_lam_re, s5_lam_im, s5_log_dt, s5_b_re, s5_b_im, s5_c_re, s5_c_im, s5_d, s5_w_glu,
              ret_w_in, ret_gn_g, ret_w_o,
              ffn_w_up, ffn_conv_w, ffn_conv_b, ffn_w_down):
    B = x.shape[0]
    L = x.shape[1] + N_META
    h = jnp.concatenate(
        [jnp.broadcast_to(meta_tokens[None].astype(x.dtype), (B, N_META, D_MODEL)), x], axis=1)
    cid = chunk_ids(L)
    cos_a, sin_a = rope_tables(L, MLA_ROPE)
    cos_d, sin_d = rope_tables(L, RET_DK)
    lb_cum = jnp.cumsum(jax.nn.softmax(hgrn_lb_logits.astype(F32), axis=0), axis=0)
    lb_all = lb_cum - lb_cum[0:1]

    for i in range(DEPTH):
        m, j = i % N_MIXERS, i // N_MIXERS
        a = rms_norm(h, norm_mix_g[i])
        if m == 0:
            y = mla_mixer(a, mla_w_down[j], mla_cq_norm_g[j], mla_ckv_norm_g[j], mla_w_uq[j], mla_w_ukv[j],
                          mla_q_head_g[j], mla_k_head_g[j], mla_w_o[j], cos_a, sin_a, cid)
        elif m == 1:
            y = hgrn2_mixer(a, hgrn_w_in[j], lb_all[i], hgrn_o_norm_g[j], hgrn_w_o[j])
        elif m == 2:
            y = s5_mixer(a, s5_lam_re[j], s5_lam_im[j], s5_log_dt[j], s5_b_re[j], s5_b_im[j],
                         s5_c_re[j], s5_c_im[j], s5_d[j], s5_w_glu[j])
        else:
            y = retention_mixer(a, ret_w_in[j], ret_gn_g[j], ret_w_o[j], cos_d, sin_d)
        h = h + y.astype(h.dtype)
        f = conv_glu_ffn(rms_norm(h, norm_ffn_g[i]), ffn_w_up[i], ffn_conv_w[i], ffn_conv_b[i], ffn_w_down[i])
        h = h + f.astype(h.dtype)
    return h[:, N_META:]


_drawn_inputs = setup_inputs


def setup_inputs(seed=0):
    import zlib

    import numpy as np

    out = dict(_drawn_inputs(seed))
    spreads = {}
    factors = {'mla_cq_norm_g': 8.0,
     'mla_ckv_norm_g': 8.0,
     'mla_q_head_g': 8.0,
     'mla_k_head_g': 8.0,
     'hgrn_lb_logits': 25.715,
     'hgrn_o_norm_g': 135.689,
     's5_lam_re': 64.0,
     's5_lam_im': 21.824,
     's5_log_dt': 22.536,
     's5_b_re': 30.56,
     's5_b_im': 31.184,
     's5_c_re': 30.6,
     's5_c_im': 30.824,
     'ret_gn_g': 200.0,
     'ffn_conv_b': 21.432,
     'norm_ffn_g': 8.0,
     's5_d': 8.0,
     's5_w_glu': 7.538}
    for name, (base, spread) in spreads.items():
        noise = np.random.default_rng([zlib.crc32(name.encode()), seed]).standard_normal(out[name].shape)
        drawn = base * np.exp(spread * noise) if base else spread * noise
        out[name] = jnp.asarray(drawn.astype(out[name].dtype))
    for name, factor in factors.items():
        out[name] = (out[name] * factor).astype(out[name].dtype)
    return out
```

```python
from contextlib import ExitStack

import concourse.bass as bass
from concourse import mybir

F32 = mybir.dt.float32
F32R = mybir.dt.float32r
ALU = mybir.AluOpType
ACT = mybir.ActivationFunctionType
AX = mybir.AxisListType

P = 128
D = 1024
DT = D // P
SEQ, META = 512, 16
T = SEQ + META
HALF = T // 2
DEPTH = 4
EPS = 1e-6
NEG = -1e30
BLK = 8
RING = 4
AHEAD = 3
QB = SEQ // P

HEADS = 8
NOPE, ROPE, VDIM = 128, 64, 128
QK = NOPE + ROPE
QL, KVL = 384, 256

FFN = 2816
KT = FFN // P
DOWN = (8, 7, 7)

RH, RDK, RDV = 4, 256, 512
S5P = 64

SUBLAYERS = ["mla", "ffn0", "hgrn", "ffn1", "s5", "ffn2", "ret", "ffn3"]
MLA_TILES = 6 + 2 + 7 + 22 * 7 + 15 + DT
HGRN_TILES = 16 * HEADS + DT
S5_TILES = 2 + 2 + 6 * 8 + 4 + 2 * DT
RET_TILES = 12 + 3 * (24 + DT) + 12 + DT
LAST_TILES = {"ffn": 1 + 2 * KT, "mla": 1 + MLA_TILES - DT, "hgrn": 1 + HGRN_TILES - DT, "s5": S5_TILES - DT, "ret": 1 + RET_TILES - DT}
CONSTS = 64


class Order:

    def __init__(self, sem, names, start=0):
        self.sem, self.names, self.start = sem, list(names), start
        self.index = {n: k for k, n in enumerate(self.names)}
        assert len(self.index) == len(self.names)
        self.at = 0

    def one(self, name):
        assert self.names[self.at] == name, (self.names[self.at], name)
        self.at = (self.at + 1) % len(self.names)
        return 1

    def done(self, name, round_=0):
        return round_ * len(self.names) + (self.start + self.index[name] + 1)


def plan(stages):
    units = {"mla": 30, "hgrn": 40, "s5": 2 * DT, "ret": 16 * RH, "ffn": 2 * KT + 3 * DT}
    tiles = {"mla": MLA_TILES, "hgrn": HGRN_TILES, "s5": S5_TILES, "ret": RET_TILES, "ffn": 2 * KT + DT}
    at, u, g = [], 0, 4
    for s in stages:
        kind = "ffn" if s[:3] == "ffn" else s
        at.append((kind, s, u, g))
        u += units[kind]
        g += 1 + tiles[kind]
    return at, u


def trunk(nc, a, stages):
    at, n_units = plan(stages)
    n_units += 4 * DEBUG
    first = SUBLAYERS.index(stages[0])

    layer0 = min(int(s[3]) for s in stages if s[:3] == "ffn") if any(s[:3] == "ffn" for s in stages) else 0
    ctx = ExitStack()
    with ctx:
        def sem(name):
            return ctx.enter_context(nc.semaphore(name))

        place = [nc.sbuf_base + (-nc.sbuf_base) % 32]

        def sb(name, shape, dt=F32, at=None):
            size = 4
            for n in shape[1:]:
                size *= n
            size += -size % 32
            if at is None:
                at = place[0]
                place[0] += size
            return nc.alloc_sbuf_tensor_at(name, shape, dt, offset=at)

        h = sb("h", [P, DT, T])
        xs_at = place[0]
        xs = sb("xs", [P, DT, 2, T], F32R)
        hid_at = place[0]
        hid = sb("hid", [P, KT, 2, T], F32R)
        raw = sb("raw", [P, RING, BLK * P])
        wr = sb("wr", [P, RING, 2, BLK, P], F32R)
        rstd = sb("rstd", [P, T])
        sqsum = sb("sqsum", [P, T])
        scr = sb("scr", [P, 4, T])
        ub = sb("ub", [P, 2, T + 2])
        ones = sb("ones", [P, P])
        ident = sb("ident", [P, P])
        gains = sb("gains", [P, 2 * DEPTH, DT])
        convp = sb("convp", [P, 2 * KT, 4])
        work_at = hid_at + 8 * 2 * T * 4
        NW = (KT - 8) * 2
        work = sb("work", [P, NW, T], at=work_at)
        work2 = sb("work2", [P, 2 * DT * T], at=xs_at)
        spare = sb("spare", [P, 2 * DT * T], at=hid_at)
        assert place[0] <= nc.sbuf_usable_end, place[0]
        ps = ctx.enter_context(nc.psum_tensor("ps", [P, 4, 2, 512], F32))

        raw_landed = [sem(f"raw_landed{s}") for s in range(RING)]
        hi_ready = sem("hi_ready")
        lo_ready = sem("lo_ready")
        unit_done = sem("unit_done")
        tile_free = sem("tile_free")
        consts = sem("consts")
        convp_landed = sem("convp_landed")
        norm_sum = sem("norm_sum")
        norm_act = sem("norm_act")
        norm_dve_done = Order(sem("norm_dve"), ["square", "times", "factor"])
        sum_cleared = sem("sum_cleared")
        tail_dve = Order(sem("tail_dve"), ["scaled", "summed"])
        tail_act = Order(sem("tail_act"), ["hi", "square"])
        tail_pool = Order(sem("tail_pool"), ["lo"])
        up_dve = Order(sem("up_dve"), [n for j in range(2) for n in
                                       [(n, j, s) for s in range(2) for n in ("tap0", "tap1", "conv")] + [("hidden", j)]])
        up_act = Order(sem("up_act"), [(n, j) for j in range(2) for n in ("silu", "hi")])
        up_pool = Order(sem("up_pool"), [("lo", j) for j in range(2)], start=1)
        pads = sem("pads")
        out_written = sem("out_written")
        def tile(g):
            return ps[:, g % 4, :, 0:HALF]

        def flat(g):
            return ps[:, g % 4].rearrange("p a b -> p (a b)")

        def halves(x):
            return x.rearrange("p (a b) -> p a b", a=2)

        def load_unit(sp, u0, i=0, per=0):
            if u0 >= RING or per:
                sp.wait_ge(lo_ready, u0 + i * per - RING + 1)
            sp.dma_start(raw[:, u0 % RING, :], a["stream"][bass.ds(u0 + i * per, 1)].rearrange("a p n -> p (a n)"))\
              .then_inc(raw_landed[u0 % RING], 16)

        def round_unit(act, u0, i=0, per=0):
            if u0 >= n_units and not per:
                return
            s = u0 % RING
            act.wait_ge(raw_landed[s], (i * (per // RING) + (u0 // RING + 1)) * 16)
            if u0 >= RING or per:
                act.wait_ge(unit_done, u0 + i * per - RING + 1)
            act.activation(wr[:, s, 0].rearrange("p a b -> p (a b)"), raw[:, s, :], ACT.Copy).then_inc(hi_ready, 1)

        def split_unit(pool, u0, i=0, per=0):
            if u0 >= n_units and not per:
                return
            s = u0 % RING
            pool.wait_ge(hi_ready, u0 + i * per + 1)
            pool.tensor_tensor(wr[:, s, 1].rearrange("p a b -> p (a b)"), raw[:, s, :],
                               wr[:, s, 0].rearrange("p a b -> p (a b)").bitcast(F32), ALU.subtract).then_inc(lo_ready, 1)

        def project(pe, out, slot, b0, x, start, stop, inc=None):
            n = len(x)
            for k in range(n):
                for p, (w, v) in enumerate(((0, 0), (0, 1), (1, 0))):
                    for q in range(2):
                        mm = pe.matmul(out[:, q], wr[:, slot, w, b0 + k], x[k][v][:, q * HALF:(q + 1) * HALF],
                                       start=start and k == 0 and p == 0, stop=stop and k == n - 1 and p == 2)
            if inc is not None:
                mm.then_inc(inc, 1)

        def split_tiles(t, ks):
            return [(t[:, k, 0], t[:, k, 1]) for k in ks]

        def newton(dve, y, x, t, o, names, r=0):
            dve.scalar_tensor_tensor(t, y, -0.5, y, ALU.mult, ALU.mult).then_inc(o.sem, o.one(names[0]))
            dve.wait_ge(o.sem, o.done(names[0], r))
            dve.tensor_tensor(t, t, x, ALU.mult).then_inc(o.sem, o.one(names[1]))
            dve.wait_ge(o.sem, o.done(names[1], r))
            dve.scalar_tensor_tensor(y, t, 1.5, y, ALU.add, ALU.mult).then_inc(o.sem, o.one(names[2]))
            dve.wait_ge(o.sem, o.done(names[2], r))

        def norm_pe(pe, n, g):
            pe.wait_ge(tail_dve.sem, tail_dve.done("summed", 8 * n + 7))
            if g >= 4:
                pe.wait_ge(tile_free, g - 3)
            if n == 0:
                pe.wait_ge(consts, CONSTS)
            for q in range(2):
                mm = pe.matmul(tile(g)[:, q], ones[:], sqsum[:, q * HALF:(q + 1) * HALF], start=True, stop=True)
            mm.then_inc(norm_sum, 1)
            pe.wait_ge(tail_pool.sem, tail_pool.done("lo", 8 * n + 7))

        def norm_dve(dve, n, g):
            dve.wait_ge(norm_sum, n + 1)
            dve.tensor_scalar(halves(sqsum[:]), tile(g), 1.0 / D, EPS, ALU.mult, ALU.add).then_inc(tile_free, 1)
            dve.wait_ge(norm_act, 2 * n + 2)
            newton(dve, rstd[:], sqsum[:], ub[:, 1, 2:], norm_dve_done, ("square", "times", "factor"), n)
            dve.memset(sqsum[:], 0.0).then_inc(sum_cleared, 1)

        def norm_act_(act, n, g):
            act.wait_ge(tile_free, g + 1)
            act.activation(rstd[:], sqsum[:], ACT.Ln).then_inc(norm_act, 1)
            act.wait_ge(norm_act, 2 * n + 1)
            act.activation(rstd[:], rstd[:], ACT.Exp, scale=-0.5).then_inc(norm_act, 1)

        def tail_dve_(dve, n, m, i=0):
            r = 8 * n + m
            if r >= 2:
                dve.wait_ge(tail_pool.sem, tail_pool.done("lo", r - 2 + 4 * i))
            dve.tensor_scalar(scr[:, m % 2], h[:, m + 4 * i], gains[:, first + n, bass.ds(m + 4 * i, 1)], None, ALU.mult)\
               .then_inc(tail_dve.sem, tail_dve.one("scaled"))
            dve.wait_ge(tail_act.sem, tail_act.done("square", r + 4 * i))
            dve.wait_ge(tail_dve.sem, tail_dve.done("scaled", r + 4 * i))
            dve.wait_ge(sum_cleared, n + 1)
            dve.tensor_tensor(sqsum[:], sqsum[:], scr[:, 2 + m % 2], ALU.add)\
               .then_inc(tail_dve.sem, tail_dve.one("summed"))

        def tail_act_(act, n, m, i=0):
            r = 8 * n + m
            act.wait_ge(tail_dve.sem, tail_dve.done("scaled", r + 4 * i))
            act.activation(xs[:, m + 4 * i, 0], scr[:, m % 2], ACT.Copy).then_inc(tail_act.sem, tail_act.one("hi"))
            act.activation(scr[:, 2 + m % 2], h[:, m + 4 * i], ACT.Square).then_inc(tail_act.sem, tail_act.one("square"))

        def tail_pool_(pool, n, m, i=0):
            r = 8 * n + m
            pool.wait_ge(tail_act.sem, tail_act.done("hi", r + 4 * i))
            pool.tensor_tensor(xs[:, m + 4 * i, 1], scr[:, m % 2], xs[:, m + 4 * i, 0].bitcast(F32), ALU.subtract)\
                .then_inc(tail_pool.sem, tail_pool.one("lo"))

        def last_stage_over(eng, n):
            eng.wait_ge(tail_dve.sem, tail_dve.done("summed", 8 * n + 7))
            eng.wait_ge(tail_pool.sem, tail_pool.done("lo", 8 * n + 7))

        def out_pe(pe, u0, g0, x):
            for m in range(DT):
                pe.wait_ge(lo_ready, u0 + m + 1)
                pe.wait_ge(tile_free, g0 + m - 3)
                project(pe, tile(g0 + m), (u0 + m) % RING, 0, x, True, True, unit_done)

        def out_dve(dve, n, u0, g0):
            for m in range(DT):
                dve.wait_ge(unit_done, u0 + m + 1)
                dve.tensor_tensor(halves(h[:, m]), tile(g0 + m), halves(h[:, m]), ALU.add).then_inc(tile_free, 1)
                dve.wait_ge(tile_free, g0 + m + 1)
                tail_dve_(dve, n, m)

        def out_act(act, n, u0):
            for m in range(DT):
                round_unit(act, u0 + m + AHEAD)
                tail_act_(act, n, m)

        def out_pool(pool, n, u0):
            for m in range(DT):
                split_unit(pool, u0 + m + AHEAD)
                tail_pool_(pool, n, m)

        def ffn_pe(pe, n, layer, u0, g0):
            norm_pe(pe, n, g0)
            x = split_tiles(xs, range(DT))
            ug, gg = u0, g0 + 1
            with pe.Fori(0, KT // 2) as i:
                for s in range(4):
                    pe.wait_ge(lo_ready, ug + s + 1 + i * 4)
                    pe.wait_ge(tile_free, gg + s - 3 + i * 4)
                    project(pe, tile(gg + s), (ug + s) % RING, 0, x, True, True, unit_done)
            ug, gg = u0 + 2 * KT, gg + 2 * KT
            pe.wait_ge(up_pool.sem, up_pool.done(("lo", 1), (layer + 1) * (KT // 2) - 1))
            with pe.Fori(0, DT // 4) as i:
                for m in range(4):
                    pe.wait_ge(tile_free, gg + m - 3 + i * 4)
                    k0 = 0
                    for j, nb in enumerate(DOWN):
                        u = ug + 3 * m + j
                        pe.wait_ge(lo_ready, u + 1 + i * 12)
                        project(pe, tile(gg + m), u % RING, 0, split_tiles(hid, range(k0, k0 + nb)),
                                j == 0, j == 2, unit_done)
                        k0 += nb

        def ffn_dve(dve, n, layer, u0, g0, last):
            norm_dve(dve, n, g0)
            gg = g0 + 1
            R = layer * (KT // 2)
            dve.wait_ge(convp_landed, 16 * (layer + 1))
            dve.wait_ge(pads, 1)
            with dve.Fori(0, KT // 2) as i:
                for j in range(2):
                    for s in range(2):
                        q = 2 * j + s
                        cp = lambda c, q=q: convp[:, bass.ds(q + 4 * i, 1), c]
                        dve.wait_ge(unit_done, u0 + q + 1 + i * 4)
                        dve.tensor_tensor(halves(ub[:, s, 2:]), tile(gg + q), halves(rstd[:]), ALU.mult)\
                           .then_inc(tile_free, 1)
                        dve.wait_ge(tile_free, gg + q + 1 + i * 4)
                        dve.tensor_scalar(scr[:, s], ub[:, s, 2:], cp(2), cp(3), ALU.mult, ALU.add)\
                           .then_inc(up_dve.sem, up_dve.one(("tap0", j, s)))
                        dve.wait_ge(up_dve.sem, up_dve.done(("tap0", j, s), R + i))
                        dve.scalar_tensor_tensor(scr[:, s], ub[:, s, 1:T + 1], cp(1), scr[:, s], ALU.mult, ALU.add)\
                           .then_inc(up_dve.sem, up_dve.one(("tap1", j, s)))
                        dve.wait_ge(up_dve.sem, up_dve.done(("tap1", j, s), R + i))
                        dve.scalar_tensor_tensor(scr[:, s], ub[:, s, 0:T], cp(0), scr[:, s], ALU.mult, ALU.add)\
                           .then_inc(up_dve.sem, up_dve.one(("conv", j, s)))
                    dve.wait_ge(up_dve.sem, up_dve.done(("conv", j, 1), R + i))
                    dve.wait_ge(up_act.sem, up_act.done(("silu", j), R + i))
                    dve.wait_ge(up_pool.sem, up_pool.done(("lo", j), R + i) - 1)
                    dve.tensor_tensor(scr[:, 3], scr[:, 2], scr[:, 1], ALU.mult)\
                       .then_inc(up_dve.sem, up_dve.one(("hidden", j)))
            ug, gg = u0 + 2 * KT, gg + 2 * KT
            dve.wait_ge(up_pool.sem, up_pool.done(("lo", 1), R + KT // 2 - 1))
            with dve.Fori(0, DT // 4) as i:
                for m in range(4):
                    dve.wait_ge(unit_done, ug + 3 * m + 3 + i * 12)
                    hm = h[:, m + 4 * i].rearrange("p (a b) -> p a b", a=2)
                    dve.tensor_tensor(hm, tile(gg + m), hm, ALU.add).then_inc(tile_free, 1)
                    if not last:
                        dve.wait_ge(tile_free, gg + m + 1 + i * 4)
                        tail_dve_(dve, n + 1, m, i)

        def ffn_act(act, n, layer, u0, g0, last):
            norm_act_(act, n, g0)
            R = layer * (KT // 2)
            with act.Fori(0, KT // 2) as i:
                for s in range(4):
                    round_unit(act, u0 + AHEAD + s, i, 4)
                    j = s // 2
                    if s % 2 == 0:
                        act.wait_ge(up_dve.sem, up_dve.done(("conv", j, 0), R + i))
                        act.activation(scr[:, 2], scr[:, 0], ACT.Silu).then_inc(up_act.sem, up_act.one(("silu", j)))
                    else:
                        act.wait_ge(up_dve.sem, up_dve.done(("hidden", j), R + i))
                        act.activation(hid[:, bass.ds(i * 2 + j, 1), 0], scr[:, 3], ACT.Copy)\
                           .then_inc(up_act.sem, up_act.one(("hi", j)))
            ug = u0 + 2 * KT
            if last:
                for u in range(ug + AHEAD, n_units):
                    round_unit(act, u)
                return
            with act.Fori(0, DT // 4) as i:
                for m in range(4):
                    for j in range(3):
                        round_unit(act, ug + AHEAD + 3 * m + j, i, 12)
                    tail_act_(act, n + 1, m, i)

        def ffn_pool(pool, n, layer, u0, g0, last):
            R = layer * (KT // 2)
            with pool.Fori(0, KT // 2) as i:
                for s in range(4):
                    split_unit(pool, u0 + AHEAD + s, i, 4)
                    j = s // 2
                    if s % 2 == 1:
                        pool.wait_ge(up_act.sem, up_act.done(("hi", j), R + i))
                        lo = hid[:, bass.ds(i * 2 + j, 1), 1].rearrange("p a b -> p (a b)")
                        hi = hid[:, bass.ds(i * 2 + j, 1), 0].rearrange("p a b -> p (a b)")
                        pool.tensor_tensor(lo, scr[:, 3], hi.bitcast(F32), ALU.subtract)\
                            .then_inc(up_pool.sem, up_pool.one(("lo", j)))
            ug = u0 + 2 * KT
            if last:
                for u in range(ug + AHEAD, n_units):
                    split_unit(pool, u)
                return
            with pool.Fori(0, DT // 4) as i:
                for m in range(4):
                    for j in range(3):
                        split_unit(pool, ug + AHEAD + 3 * m + j, i, 12)
                    tail_pool_(pool, n + 1, m, i)
        MIX = {}

        def mla(n, u0, g0):
            if "mla" not in stages:
                return {}
            SCALE = QK ** -0.5
            parity = lambda k: [work[:, 10 * j + k] for j in range(2)]
            qn, qr, kn, kr = (parity(k) for k in range(4))
            vt = [work[:, 10 * j + 4:10 * j + 6].rearrange("p a b -> p (a b)") for j in range(2)]
            krot, sqkr, tab, misc = (work[:, k] for k in (6, 7, 8, 9))
            par, stat = misc[:, 0:16], misc[:, 16:96]
            sqn, sqr, rg, rt, vfm, fac = (work[:, k] for k in range(20, 26))
            ms = work[:, 16]
            nt = work[:, 17]
            prob = [work[:, 26 + k] for k in range(2)]
            pt = [scr[:, 2 * k:2 * k + 2].rearrange("p a b -> p (a b)") for k in range(2)]
            lat = [work[:, 20 + k] for k in range(6)]
            lsq = [work[:, 10 + k] for k in range(5)]
            lfac = [work[:, 15], work[:, 18]]
            lms = [work[:, 16], work[:, 19]]
            groups = ((0, 3, QL), (3, 5, KVL))
            G_Q, G_QR, G_K, G_KR = 5, 6, 7, 8

            P_SEQ = ["qn", "qr", "sumq", "kn", "vv", "sumk", "vT"]
            A_SEQ = [("S", 0), ("S", 1), ("T", 0), ("O", 0), ("S", 2), ("T", 1), ("O", 1), ("S", 3),
                     ("T", 2), ("O", 2), ("S", 4), ("T", 3), ("O", 3), ("T", 4), ("O", 4)]
            X_SEQ, after = [], {1: "qn", 2: "qr", 4: "sumq", 6: "kn", 8: "vv", 10: "sumk", 13: "vT"}
            for k, s in enumerate(A_SEQ):
                X_SEQ.append(s)
                if k in after:
                    X_SEQ.append(after[k])
            gP = g0 + 1 + 6 + 2
            gX = gP + len(P_SEQ)
            uH = u0 + 6
            uO = uH + 2 * HEADS
            gO = gX + len(X_SEQ) * (HEADS - 1) + len(A_SEQ)
            assert gO + DT == g0 + 1 + MLA_TILES

            consts_in = sem("mla_consts")
            l_dve = Order(sem("mla_l_dve"), [("norm", t) for t in range(3)] and
                          ["t0", "t1", "factor0"] + [("norm", 0), ("norm", 1), ("norm", 2)] +
                          ["t2", "t3", "factor1"] + [("norm", 3), ("norm", 4)] + ["gain", "up", "down", "turned"])
            l_act = Order(sem("mla_l_act"), [("square", t) for t in range(6)] + ["ln0", "exp0", "ln1", "exp1"] +
                          [("hi", t) for t in range(5)])
            l_pool = Order(sem("mla_l_pool"), [("lo", t) for t in range(5)])
            l_pe = Order(sem("mla_l_pe"), ["sum0", "sum1"])
            p_dve = Order(sem("mla_p_dve"), ["up", "down", "turned", "q0", "q1", "facq", "qn", "qr",
                                             "k0", "k1", "fack", "kn", "kr", "vt"])
            p_act = Order(sem("mla_p_act"), ["sqqn", "sqqr", "lnq", "expq", "sqkn", "lnk", "expk"])
            p_pe = Order(sem("mla_p_pe"), ["sumq", "sumk", "vT"])
            a_dve = Order(sem("mla_a_dve"), [x for k, b in A_SEQ for x in
                                             {"S": ([("mask", b)] if b < QB else []) + [("max", b), ("bias", b)],
                                              "T": [], "O": []}[k] + ([("prob", b)] if k == "S" else [])])
            a_act = Order(sem("mla_a_act"), [({"S": "exp", "T": "copy", "O": "hi"}[k], b) for k, b in A_SEQ
                                             if (k, b) != ("T", QB)])
            a_pe = Order(sem("mla_a_pe"), A_SEQ)

            def rows(b):
                return P if b < QB else META

            def keys(b):
                return META + P * (b + 1) if b < QB else META

            def walk(head, project, attend, at_):
                for k, s in enumerate(P_SEQ):
                    project(s, 0, 0, 0, gP + k)
                with at_.Fori(0, (HEADS - 2) // 2) as i:
                    for j in range(2):
                        for k, s in enumerate(X_SEQ):
                            g = gX + len(X_SEQ) * j + k
                            if isinstance(s, tuple):
                                attend(s, j, j, i, g)
                            else:
                                project(s, 1 - j, j + 1, i, g)
                for k, s in enumerate(X_SEQ):
                    g = gX + len(X_SEQ) * (HEADS - 2) + k
                    if isinstance(s, tuple):
                        attend(s, 0, HEADS - 2, 0, g)
                    else:
                        project(s, 1, HEADS - 1, 0, g)
                for k, s in enumerate(A_SEQ):
                    attend(s, 1, HEADS - 1, 0, gX + len(X_SEQ) * (HEADS - 1) + k)

            W2 = 2 * len(X_SEQ)

            def pe_(pe):
                norm_pe(pe, n, g0)
                for t in range(6):
                    pe.wait_ge(lo_ready, u0 + t + 1)
                    pe.wait_ge(tile_free, g0 + 1 + t - 3)
                    project(pe, tile(g0 + 1 + t), (u0 + t) % RING, 0, split_tiles(xs, range(DT)), True, True, unit_done)
                for k, (a0, a1, _) in enumerate(groups):
                    g = g0 + 7 + k
                    pe.wait_ge(tile_free, g - 3)
                    pe.wait_ge(l_act.sem, l_act.done(("square", a1 - 1)))
                    for q in range(2):
                        for t in range(a0, a1):
                            mm = pe.matmul(tile(g)[:, q], ones[:], lsq[t][:, q * HALF:(q + 1) * HALF],
                                           start=t == a0, stop=t == a1 - 1)
                    mm.then_inc(l_pe.sem, l_pe.one(f"sum{k}"))
                pe.wait_ge(l_pool.sem, l_pool.done(("lo", 4)))
                cq, ckv = split_tiles(xs, range(3)), split_tiles(xs, range(3, 5))

                def proj(s, j, h0, i, g):
                    pe.wait_ge(tile_free, g - 3 + i * W2)
                    u = uH + 2 * h0
                    if s == "qn":
                        pe.wait_ge(lo_ready, u + 1 + i * 4)
                        project(pe, tile(g), u % RING, 0, cq, True, True)
                    elif s == "qr":
                        project(pe, tile(g), u % RING, 3, cq, True, True, unit_done)
                    elif s == "kn":
                        pe.wait_ge(lo_ready, u + 2 + i * 4)
                        project(pe, tile(g), (u + 1) % RING, 0, ckv, True, True)
                    elif s == "vv":
                        project(pe, tile(g), (u + 1) % RING, 2, ckv, True, True, unit_done)
                    elif s == "vT":
                        pe.wait_ge(tile_free, vv_at(g) + 1 + i * W2)
                        for b in range(QB):
                            pe.transpose(flat(g)[:, b * P:(b + 1) * P], vfm[:, META + b * P:META + (b + 1) * P], ident[:])
                        pe.transpose(flat(g)[0:META, 512:512 + P], vfm[:, 0:META], ident[:])\
                          .then_inc(p_pe.sem, p_pe.one("vT"))
                    else:
                        rope, rsq = ("sqqr", sqr) if s == "sumq" else ("sqkn", sqkr)
                        pe.wait_ge(p_act.sem, p_act.done(rope, h0) + i * 2 * len(p_act.names))
                        for q in range(2):
                            c = slice(q * HALF, (q + 1) * HALF)
                            pe.matmul(tile(g)[:, q], ones[:], sqn[:, c], start=True, stop=False)
                            mm = pe.matmul(tile(g)[:, q], ones[0:ROPE, :], rsq[0:ROPE, c], start=False, stop=True)
                        mm.then_inc(p_pe.sem, p_pe.one(s))

                def attend(s, j, h0, i, g):
                    k, b = s
                    pe.wait_ge(tile_free, g - 3 + i * W2)
                    R, K = rows(b), keys(b)
                    q0 = META + b * P if b < QB else 0
                    if k == "S":
                        pe.wait_ge(p_dve.sem, p_dve.done("kr", h0) + i * 2 * len(p_dve.names))
                        for c0, c1 in ((0, min(K, 512)), (512, K)):
                            if c0 < c1:
                                pe.matmul(flat(g)[0:R, c0:c1], qn[j][:, q0:q0 + R], kn[j][:, c0:c1], start=True, stop=False)
                                mm = pe.matmul(flat(g)[0:R, c0:c1], qr[j][0:ROPE, q0:q0 + R], kr[j][0:ROPE, c0:c1],
                                               start=False, stop=True)
                    elif k == "T":
                        pe.wait_ge(a_dve.sem, a_dve.done(("prob", b), h0) + i * 2 * len(a_dve.names))
                        for t in range(b + 1 if b < QB else 0):
                            pe.transpose(flat(g)[:, t * P:t * P + R], prob[b % 2][0:R, META + t * P:META + (t + 1) * P],
                                         ident[0:R, 0:R])
                        if b < QB:
                            mm = pe.transpose(flat(g)[0:META, 512:512 + R], prob[b % 2][0:R, 0:META], ident[0:R, 0:R])
                        else:
                            mm = pe.matmul(flat(g)[:, 512:512 + R], prob[b % 2][0:R, 0:P], ident[0:R, 0:R],
                                           start=True, stop=True)
                    else:
                        pe.wait_ge(p_dve.sem, p_dve.done("vt", h0) + i * 2 * len(p_dve.names))
                        pe.wait_ge(tile_free, t_at(g, b) + 1 + i * W2)
                        for t in range(b + 1 if b < QB else 0):
                            pe.matmul(flat(g)[:, 0:R], vt[j][:, t * P:(t + 1) * P], pt[b % 2][:, t * P:t * P + R],
                                      start=t == 0, stop=False)
                        mm = pe.matmul(flat(g)[:, 0:R], vt[j][0:META, 512:512 + P], pt[b % 2][0:META, 512:512 + R],
                                       start=b == QB, stop=True)
                    mm.then_inc(a_pe.sem, a_pe.one(s))

                walk(None, proj, attend, pe)
                pe.wait_ge(tile_free, gO)
                out_pe(pe, uO, gO, split_tiles(hid, range(HEADS)))

            def vv_at(g):
                if g < gX:
                    return g - 2
                return g - (X_SEQ.index("vT") - X_SEQ.index("vv"))

            def t_at(g, b):
                seq = X_SEQ if g < gX + len(X_SEQ) * (HEADS - 1) else A_SEQ
                return g - (seq.index(("O", b)) - seq.index(("T", b)))

            def dve_(dve):
                norm_dve(dve, n, g0)
                for t in range(6):
                    g = g0 + 1 + t
                    dve.wait_ge(unit_done, u0 + t + 1)
                    dve.tensor_tensor(halves(lat[t]), tile(g), halves(rstd[:]), ALU.mult).then_inc(tile_free, 1)
                dve.wait_ge(consts_in, 32)
                for k, (a0, a1, width) in enumerate(groups):
                    g = g0 + 7 + k
                    dve.wait_ge(l_pe.sem, l_pe.done(f"sum{k}"))
                    dve.tensor_scalar(halves(lms[k]), tile(g), 1.0 / width, EPS, ALU.mult, ALU.add).then_inc(tile_free, 1)
                    dve.wait_ge(l_act.sem, l_act.done(f"exp{k}"))
                    newton(dve, lfac[k], lms[k], nt, l_dve, (f"t{2 * k}", f"t{2 * k + 1}", f"factor{k}"))
                    for t in range(a0, a1):
                        dve.scalar_tensor_tensor(lat[t], lat[t], par[:, t:t + 1], lfac[k], ALU.mult, ALU.mult)\
                           .then_inc(l_dve.sem, l_dve.one(("norm", t)))
                dve.wait_ge(l_act.sem, l_act.done(("square", 5)))
                dve.tensor_scalar(lat[5], lat[5], par[:, G_KR:G_KR + 1], None, ALU.mult).then_inc(l_dve.sem, l_dve.one("gain"))
                dve.wait_ge(l_dve.sem, l_dve.done("gain"))
                turn(dve, krot, lat[5], scr[:, 1], l_dve, 0)
                dve.wait_ge(l_pool.sem, l_pool.done(("lo", 4)))

                def proj(s, j, h0, i, g):
                    D2 = len(p_dve.names) * 2
                    if s == "qn" or s == "kn":
                        a_ = "sqqn" if s == "qn" else "sqkn"
                        col = G_Q if s == "qn" else G_K
                        dst = qn[j] if s == "qn" else kn[j]
                        dve.wait_ge(p_act.sem, p_act.done(a_, h0) + i * 2 * len(p_act.names))
                        dve.tensor_scalar(halves(dst), tile(g), par[:, col:col + 1], None, ALU.mult).then_inc(tile_free, 1)
                    elif s == "qr":
                        dve.wait_ge(p_act.sem, p_act.done("sqqr", h0) + i * 2 * len(p_act.names))
                        dve.tensor_scalar(halves(rg), tile(g), par[:, G_QR:G_QR + 1], None, ALU.mult).then_inc(tile_free, 1)
                        dve.wait_ge(tile_free, g + 1 + i * W2)
                        turn(dve, qr[j], rg, rt, p_dve, h0, i * D2)
                    elif s == "vv":
                        dve.wait_ge(unit_done, uH + 2 * h0 + 2 + i * 4)
                        dve.tensor_copy(halves(vfm), tile(g)).then_inc(tile_free, 1)
                    elif s == "vT":
                        dve.wait_ge(p_pe.sem, p_pe.done("vT", h0) + i * 2 * len(p_pe.names))
                        dve.tensor_copy(vt[j][:, 0:512], flat(g)[:, 0:512]).then_inc(p_dve.sem, p_dve.one("vt"))
                        dve.tensor_copy(vt[j][0:META, 512:512 + P], flat(g)[0:META, 512:512 + P]).then_inc(tile_free, 1)
                    else:
                        c = s[3]
                        dve.wait_ge(p_pe.sem, p_pe.done(s, h0) + i * 2 * len(p_pe.names))
                        dve.tensor_scalar(halves(ms), tile(g), 1.0 / QK, EPS, ALU.mult, ALU.add).then_inc(tile_free, 1)
                        dve.wait_ge(p_act.sem, p_act.done("exp" + c, h0) + i * 2 * len(p_act.names))
                        newton(dve, fac, ms, nt, p_dve, (c + "0", c + "1", "fac" + c), h0 + 2 * i)
                        dst = qn[j] if c == "q" else kn[j]
                        dve.tensor_tensor(dst, dst, fac, ALU.mult).then_inc(p_dve.sem, p_dve.one(c + "n"))
                        if c == "q":
                            dve.tensor_tensor(qr[j][0:ROPE], qr[j][0:ROPE], fac[0:ROPE], ALU.mult)\
                               .then_inc(p_dve.sem, p_dve.one("qr"))
                        else:
                            dve.tensor_tensor(kr[j][0:ROPE], krot[0:ROPE], fac[0:ROPE], ALU.mult)\
                               .then_inc(p_dve.sem, p_dve.one("kr"))
                        dve.wait_ge(p_dve.sem, p_dve.done(c + "r", h0) + i * D2)

                def attend(s, j, h0, i, g):
                    k, b = s
                    R, K = rows(b), keys(b)
                    A2 = 2 * len(a_dve.names)
                    if k == "S":
                        st = stat[0:R, 8 * b:8 * b + 4]
                        dve.wait_ge(a_pe.sem, a_pe.done(s, h0) + i * 2 * len(a_pe.names))
                        if b < QB:
                            dve.memset(flat(g)[0:64, K - 64:K], NEG).then_inc(a_dve.sem, a_dve.one(("mask", b)))
                            dve.wait_ge(a_dve.sem, a_dve.done(("mask", b), h0) + i * A2)
                        dve.reduce_max(st[:, 0:1], flat(g)[0:R, 0:K], AX.X).then_inc(a_dve.sem, a_dve.one(("max", b)))
                        dve.wait_ge(a_dve.sem, a_dve.done(("max", b), h0) + i * A2)
                        dve.tensor_scalar(st[:, 1:2], st[:, 0:1], -SCALE, None, ALU.mult)\
                           .then_inc(a_dve.sem, a_dve.one(("bias", b)))
                        dve.wait_ge(a_act.sem, a_act.done(("exp", b), h0) + i * 2 * len(a_act.names))
                        dve.reciprocal(st[:, 3:4], st[:, 2:3]).then_inc(tile_free, 1)
                        dve.wait_ge(tile_free, g + 1 + i * W2)
                        dve.tensor_scalar(prob[b % 2][0:R, 0:K], prob[b % 2][0:R, 0:K], st[:, 3:4], None, ALU.mult)\
                           .then_inc(a_dve.sem, a_dve.one(("prob", b)))
                    elif k == "T":
                        dve.wait_ge(a_pe.sem, a_pe.done(s, h0) + i * 2 * len(a_pe.names))
                        if b < QB:
                            dve.wait_ge(a_act.sem, a_act.done(("copy", b), h0) + i * 2 * len(a_act.names))
                        dve.tensor_copy(pt[b % 2][0:META, 512:512 + R], flat(g)[0:META, 512:512 + R]).then_inc(tile_free, 1)
                    else:
                        q0 = META + b * P if b < QB else 0
                        dve.wait_ge(a_act.sem, a_act.done(("hi", b), h0) + i * 2 * len(a_act.names))
                        hi = hid[:, bass.ds(h0 + 2 * i, 1), 0, q0:q0 + R].rearrange("p a b -> p (a b)")
                        lo = hid[:, bass.ds(h0 + 2 * i, 1), 1, q0:q0 + R].rearrange("p a b -> p (a b)")
                        dve.tensor_tensor(lo, flat(g)[:, 0:R], hi.bitcast(F32), ALU.subtract).then_inc(tile_free, 1)

                walk(None, proj, attend, dve)
                out_dve(dve, n + 1, uO, gO)

            def turn(dve, dst, src, tmp, o, r, off=0):
                dve.tensor_tensor(tmp[0:ROPE], src[ROPE:P], tab[ROPE:P], ALU.mult).then_inc(o.sem, o.one("up"))
                dve.tensor_tensor(dst[0:ROPE], src[0:ROPE], tab[0:ROPE], ALU.mult).then_inc(o.sem, o.one("down"))
                dve.wait_ge(o.sem, o.done("down", r) + off)
                dve.tensor_tensor(dst[0:ROPE], dst[0:ROPE], tmp[0:ROPE], ALU.add).then_inc(o.sem, o.one("turned"))
                dve.wait_ge(o.sem, o.done("turned", r) + off)

            def act_(act):
                act.dma_start(tab, a["mla_tab"]).then_inc(consts_in, 16)
                act.dma_start(par[:, 0:9], a["mla_par"]).then_inc(consts_in, 16)
                norm_act_(act, n, g0)
                for t in range(6):
                    round_unit(act, u0 + t + AHEAD)
                    act.wait_ge(tile_free, g0 + 1 + t + 1)
                    if t < 5:
                        act.activation(lsq[t], lat[t], ACT.Square).then_inc(l_act.sem, l_act.one(("square", t)))
                    else:
                        act.activation(sqkr[0:ROPE], lat[t][0:ROPE], ACT.Square).then_inc(l_act.sem, l_act.one(("square", t)))
                for k in range(2):
                    act.wait_ge(tile_free, g0 + 7 + k + 1)
                    act.activation(lfac[k], lms[k], ACT.Ln).then_inc(l_act.sem, l_act.one(f"ln{k}"))
                    act.wait_ge(l_act.sem, l_act.done(f"ln{k}"))
                    act.activation(lfac[k], lfac[k], ACT.Exp, scale=-0.5).then_inc(l_act.sem, l_act.one(f"exp{k}"))
                for t in range(5):
                    act.wait_ge(l_dve.sem, l_dve.done(("norm", t)))
                    act.activation(xs[:, t, 0], lat[t], ACT.Copy).then_inc(l_act.sem, l_act.one(("hi", t)))

                def proj(s, j, h0, i, g):
                    u = uH + 2 * h0
                    A2 = 2 * len(p_act.names)
                    if s == "qn":
                        round_unit(act, u + AHEAD, i, 4)
                        act.wait_ge(unit_done, u + 1 + i * 4)
                        act.activation(halves(sqn), tile(g), ACT.Square).then_inc(p_act.sem, p_act.one("sqqn"))
                    elif s == "qr":
                        act.activation(sqr[0:ROPE].rearrange("p (a b) -> p a b", a=2), tile(g)[0:ROPE], ACT.Square)\
                            .then_inc(p_act.sem, p_act.one("sqqr"))
                    elif s == "kn":
                        round_unit(act, u + 1 + AHEAD, i, 4)
                        act.wait_ge(unit_done, u + 2 + i * 4)
                        act.wait_ge(p_pe.sem, p_pe.done("sumq", h0) + i * 2 * len(p_pe.names))
                        act.activation(halves(sqn), tile(g), ACT.Square).then_inc(p_act.sem, p_act.one("sqkn"))
                    elif s in ("sumq", "sumk"):
                        c = s[3]
                        act.wait_ge(tile_free, g + 1 + i * W2)
                        act.activation(fac, ms, ACT.Ln).then_inc(p_act.sem, p_act.one("ln" + c))
                        act.wait_ge(p_act.sem, p_act.done("ln" + c, h0) + i * A2)
                        act.activation(fac, fac, ACT.Exp, scale=-0.5).then_inc(p_act.sem, p_act.one("exp" + c))

                def attend(s, j, h0, i, g):
                    k, b = s
                    R, K = rows(b), keys(b)
                    if k == "S":
                        st = stat[0:R, 8 * b:8 * b + 4]
                        act.wait_ge(a_dve.sem, a_dve.done(("bias", b), h0) + i * 2 * len(a_dve.names))
                        act.wait_ge(a_pe.sem, PROB_READ(b, h0) + i * 2 * len(a_pe.names))
                        act.activation(prob[b % 2][0:R, 0:K], flat(g)[0:R, 0:K], ACT.Exp, bias=st[:, 1:2], scale=SCALE,
                                       accum_out=st[:, 2:3]).then_inc(a_act.sem, a_act.one(("exp", b)))
                    elif k == "T" and b < QB:
                        act.wait_ge(a_pe.sem, a_pe.done(s, h0) + i * 2 * len(a_pe.names))
                        act.activation(pt[b % 2][:, 0:P * (b + 1)], flat(g)[:, 0:P * (b + 1)], ACT.Copy)\
                            .then_inc(a_act.sem, a_act.one(("copy", b)))
                    elif k == "O":
                        q0 = META + b * P if b < QB else 0
                        act.wait_ge(a_pe.sem, a_pe.done(s, h0) + i * 2 * len(a_pe.names))
                        hi = hid[:, bass.ds(h0 + 2 * i, 1), 0, q0:q0 + R].rearrange("p a b -> p (a b)")
                        act.activation(hi, flat(g)[:, 0:R], ACT.Copy).then_inc(a_act.sem, a_act.one(("hi", b)))

                walk(None, proj, attend, act)
                out_act(act, n + 1, uO)

            def PROB_READ(b, h0):
                if b < 2:
                    v = a_pe.done(("T", b + 2 if b else 4), h0 - 1)
                    return max(v, 1)
                return a_pe.done(("T", b - 2), h0)

            def pool_(pool):
                for t in range(6):
                    split_unit(pool, u0 + t + AHEAD)
                for t in range(5):
                    pool.wait_ge(l_act.sem, l_act.done(("hi", t)))
                    pool.tensor_tensor(xs[:, t, 1], lat[t], xs[:, t, 0].bitcast(F32), ALU.subtract)\
                        .then_inc(l_pool.sem, l_pool.one(("lo", t)))
                for u in range(uH, uO):
                    split_unit(pool, u + AHEAD)
                out_pool(pool, n + 1, uO)

            return {"pe": pe_, "dve": dve_, "act": act_, "pool": pool_}

        def hgrn(n, u0, g0):
            C, NC = 16, T // 16
            names = ("q16", "kinv", "kt16", "q32", "k32", "q64", "k64", "q128", "k128", "vfm", "gate", "qraw", "sigq",
                     "fg", "kk", "G", "E", "Ei", "Et", "graw", "sigg", "o", "sqo", "ms", "fac", "masks")
            b_ = {x: work[:, k] for k, x in enumerate(names)}
            vt = work[:, 26:28].rearrange("p a b -> p (a b)")
            kt = scr[:, 0:2].rearrange("p a b -> p (a b)")
            mk = scr[:, 2, 0:512]
            misc = scr[:, 3]
            at_ = [misc[:, 0:128], ub[:, 1, 2:130]]
            state = misc[:, 128:256]
            us = [ub[:, 1, 130:258], ub[:, 1, 258:386]]
            d16, d32, d64, d128 = misc[:, 256:289], misc[:, 290:306], misc[:, 306:314], misc[:, 314:318]
            lb, lb1, g_o = misc[:, 320:328], misc[:, 328:336], misc[:, 336:337]
            lg, le, lm, ls = misc[:, 340:372], misc[:, 372:404], misc[:, 404:412], misc[:, 412:420]
            scan_mask = ub[:, 0, 2:]
            nt = b_["Et"]

            P_SEQ = ["f", "e1", "q", "e2", "i", "e3", "g", "e4"]
            A_SEQ = ["VK", "M", ("S", 0), "OM", ("S", 1), ("O", 0), ("S", 2), ("O", 1), ("S", 3), ("O", 2), ("O", 3),
                     "N", "F"]
            X_SEQ = ["VK", "M", ("S", 0), "f'", "OM", "e1'", ("S", 1), ("O", 0), "q'", "e2'", ("S", 2), ("O", 1), "i'",
                     ("S", 3), ("O", 2), "e3'", ("O", 3), "N", "g'", "F", "e4'"]
            NO_TILE = ("e1", "e2", "e3", "e4", "F")

            def numbered(seq, g):
                out = []
                for s in seq:
                    head = s.rstrip("'") if isinstance(s, str) else s
                    out.append((head, isinstance(s, str) and s.endswith("'"), g))
                    g += head not in NO_TILE
                return out, g
            prologue, gX = numbered(P_SEQ, g0 + 1)
            body, gX1 = numbered(X_SEQ, gX)
            PER = gX1 - gX
            assert PER % 4 == 0
            epilogue, gO = numbered(A_SEQ, gX + PER * (HEADS - 1))
            assert gO + DT == g0 + 1 + HGRN_TILES, (gO + DT - g0 - 1)
            uO = u0 + 4 * HEADS
            UNIT_OF = {"f": 0, "q": 1, "i": 2, "g": 3}

            def walk(eng, project_, attend):
                for s, _, g in prologue:
                    project_(s, 0, 0, g)
                with eng.Fori(0, HEADS - 1) as i:
                    for s, next_, g in body:
                        if next_:
                            project_(s, 1, i, g)
                        else:
                            attend(s, 0, i, g)
                for s, _, g in epilogue:
                    attend(s, HEADS - 1, 0, g)

            consts_in = sem("hgrn_consts")
            c_dve = Order(sem("hgrn_c_dve"), ["m1", "m2", "max", "sub0", "sub1", "sub2", "sub3", "s1", "s2", "sum", "rec",
                                              "lb", "lb1"])
            c_act = Order(sem("hgrn_c_act"), ["exp"])
            p_act = Order(sem("hgrn_p_act"), ["sigf", "ln", "sigq", "E", "Ei", "Et", "sigg", "q32", "k32", "q64", "k64",
                                              "q128", "k128", "k128m"])
            p_dve = Order(sem("hgrn_p_dve"), ["forget", "k", "G", "tail", "q", "q16", "kinv", "kt16",
                                              "gate", "d16", "d32", "d64", "d128", "q32", "k32", "q64", "k64", "q128", "k128"])
            a_pe = Order(sem("hgrn_a_pe"), A_SEQ[:-1])
            a_dve = Order(sem("hgrn_a_dve"),
                          ["vtm", "ktm", ("mk", 0), ("at", 0), "om", ("mk", 1), ("at", 1), ("st", 0), ("mk", 2), ("at", 2),
                           ("st", 1), ("at", 3), ("st", 2),
                           "nw0", "nw1", "fac", "scaled", "gated"])
            a_act = Order(sem("hgrn_a_act"), ["vt", "sqo", "ln", "exp", "hi"])
            a_pool = Order(sem("hgrn_a_pool"), ["lo"], start=1)

            def pe_(pe):
                norm_pe(pe, n, g0)
                x = split_tiles(xs, range(DT))
                pe.wait_ge(consts_in, 48)

                def proj(s, r, i, g):
                    if s in NO_TILE:
                        return
                    pe.wait_ge(lo_ready, u0 + 4 * r + UNIT_OF[s] + 1 + i * 4)
                    pe.wait_ge(tile_free, g - 3 + i * PER)
                    project(pe, tile(g), (u0 + UNIT_OF[s]) % RING, 0, x, True, True, unit_done)

                def attend(s, r, i, g):
                    if s == "F":
                        return
                    pe.wait_ge(tile_free, g - 3 + i * PER)
                    f = flat(g)
                    if s == "VK":
                        pe.wait_ge(p_dve.sem, p_dve.done("k128", r + i))
                        pe.wait_ge(p_act.sem, p_act.done("k128m", r + i))
                        for b in range(QB):
                            c = slice(META + b * P, META + (b + 1) * P)
                            pe.transpose(f[:, b * P:(b + 1) * P], b_["vfm"][:, c], ident[:])
                        for b in range(QB):
                            c = slice(META + b * P, META + (b + 1) * P)
                            mm = pe.transpose(f[:, 512 + b * P:512 + (b + 1) * P], b_["k128"][:, c], ident[:])
                    elif s == "M":
                        pe.transpose(f[0:META, 0:P], b_["vfm"][:, 0:META], ident[:])
                        pe.transpose(f[0:META, P:2 * P], b_["k128"][:, 0:META], ident[:])
                        mm = pe.matmul(f[0:META, 256:256 + META], b_["kinv"][:, 0:META], b_["q16"][:, 0:META],
                                       start=True, stop=True)
                    elif s == "OM":
                        pe.wait_ge(tile_free, g_of("M", g) + 1 + i * PER)
                        pe.matmul(f[:, 0:META], vt[0:META, 512:640], at_[1][0:META, 0:META], start=True, stop=True)
                        mm = pe.matmul(f[:, 512:640], kt[0:META, 512:640], vt[0:META, 512:640], start=True, stop=True)
                    elif s == "N":
                        pe.wait_ge(a_act.sem, a_act.done("sqo", r + i))
                        for q in range(2):
                            mm = pe.matmul(tile(g)[:, q], ones[:], b_["sqo"][:, q * HALF:(q + 1) * HALF], start=True, stop=True)
                    elif s[0] == "S":
                        b = s[1]
                        c = slice(META + b * P, META + (b + 1) * P)
                        for lv, (k_, q_) in enumerate((("kinv", "q16"), ("kt16", "q16"), ("k32", "q32"), ("k64", "q64"))):
                            mm = pe.matmul(f[:, lv * P:(lv + 1) * P], b_[k_][:, c], b_[q_][:, c], start=True, stop=True)
                        if b < QB - 1:
                            pe.wait_ge(tile_free, g_of("VK", g) + 1 + i * PER)
                            mm = pe.matmul(f[:, 512:640], kt[:, b * P:(b + 1) * P], vt[:, b * P:(b + 1) * P],
                                           start=True, stop=True)
                    else:
                        b = s[1]
                        c = slice(META + b * P, META + (b + 1) * P)
                        pe.wait_ge(a_dve.sem, a_dve.done(("at", b), r + i))
                        if b:
                            pe.wait_ge(a_dve.sem, a_dve.done(("st", b - 1), r + i))
                        else:
                            pe.wait_ge(tile_free, g_of("OM", g) + 1 + i * PER)
                        pe.matmul(f[:, 0:P], vt[:, b * P:(b + 1) * P], at_[b % 2], start=True, stop=False)
                        mm = pe.matmul(f[:, 0:P], state, b_["q128"][:, c], start=False, stop=True)
                    mm.then_inc(a_pe.sem, a_pe.one(s))

                walk(pe, proj, attend)
                pe.wait_ge(a_pool.sem, a_pool.done("lo", HEADS - 1))
                out_pe(pe, uO, gO, split_tiles(hid, range(HEADS)))

            def g_of(s, g):
                seq = epilogue if g >= gX + PER * (HEADS - 1) else body
                return [x for t, next_, x in seq if t == s and not next_][0]

            def dve_(dve):
                dve.wait_ge(consts_in, 48)
                L4 = [lg[:, 8 * k:8 * k + 8] for k in range(4)]
                E4 = [le[:, 8 * k:8 * k + 8] for k in range(4)]

                def small(name, a0, a1, op, out):
                    dve.tensor_tensor(out, a0, a1, op).then_inc(c_dve.sem, c_dve.one(name))
                    dve.wait_ge(c_dve.sem, c_dve.done(name))
                small("m1", L4[0], L4[1], ALU.max, lm)
                small("m2", lm, L4[2], ALU.max, lm)
                small("max", lm, L4[3], ALU.max, lm)
                for k in range(4):
                    small(f"sub{k}", L4[k], lm, ALU.subtract, L4[k])
                dve.wait_ge(c_act.sem, c_act.done("exp"))
                small("s1", E4[0], E4[1], ALU.add, ls)
                small("s2", ls, E4[2], ALU.add, ls)
                small("sum", ls, E4[3], ALU.add, ls)
                dve.reciprocal(ls, ls).then_inc(c_dve.sem, c_dve.one("rec"))
                dve.wait_ge(c_dve.sem, c_dve.done("rec"))
                small("lb", E4[1], ls, ALU.mult, lb)
                dve.tensor_scalar(lb1, lb, -1.0, 1.0, ALU.mult, ALU.add).then_inc(c_dve.sem, c_dve.one("lb1"))
                dve.wait_ge(c_dve.sem, c_dve.done("lb1"))
                norm_dve(dve, n, g0)

                def step(o, name, r):
                    return o.done(name, r)

                def tt(out, x, y, op, name, o=p_dve):
                    dve.tensor_tensor(out, x, y, op).then_inc(o.sem, o.one(name))

                def v(name, count):
                    return b_[name][:, META:].rearrange("p (a b c) -> p a b c", b=2, c=count)

                def proj(s, r, i, g):
                    R = r + i
                    if s in UNIT_OF:
                        dst = {"f": "fg", "q": "qraw", "i": "vfm", "g": "graw"}[s]
                        dve.wait_ge(unit_done, u0 + 4 * r + UNIT_OF[s] + 1 + i * 4)
                        dve.tensor_tensor(halves(b_[dst]), tile(g), halves(rstd[:]), ALU.mult).then_inc(tile_free, 1)
                    elif s == "e1":
                        dve.wait_ge(p_act.sem, p_act.done("sigf", R))
                        dve.tensor_scalar(b_["fg"], b_["fg"], lb1[:, bass.ds(R, 1)], lb[:, bass.ds(R, 1)], ALU.mult, ALU.add)\
                           .then_inc(p_dve.sem, p_dve.one("forget"))
                        dve.wait_ge(p_dve.sem, p_dve.done("forget", R))
                        dve.tensor_scalar(b_["kk"], b_["fg"], -1.0, 1.0, ALU.mult, ALU.add)\
                           .then_inc(p_dve.sem, p_dve.one("k"))
                    elif s == "e2":
                        dve.wait_ge(p_act.sem, p_act.done("ln", R))
                        dve.tensor_tensor_scan(b_["G"], scan_mask, b_["fg"], 0.0, ALU.mult, ALU.add)\
                           .then_inc(p_dve.sem, p_dve.one("G"))
                        dve.wait_ge(p_dve.sem, p_dve.done("G", R))
                        Gv = b_["G"].rearrange("p (a b) -> p a b", b=C)
                        tt(b_["Et"].rearrange("p (a b) -> p a b", b=C), Gv[:, :, C - 1:C].broadcast_to([P, NC, C]), Gv,
                           ALU.subtract, "tail")
                    elif s == "e3":
                        dve.wait_ge(p_act.sem, p_act.done("Et", R))
                        tt(b_["qraw"], b_["qraw"], b_["sigq"], ALU.mult, "q")
                        dve.wait_ge(p_dve.sem, p_dve.done("q", R))
                        tt(b_["q16"], b_["qraw"], b_["E"], ALU.mult, "q16")
                        tt(b_["kinv"], b_["kk"], b_["Ei"], ALU.mult, "kinv")
                        tt(b_["kt16"], b_["kk"], b_["Et"], ALU.mult, "kt16")
                    elif s == "e4":
                        dve.wait_ge(p_act.sem, p_act.done("sigg", R))
                        tt(b_["gate"], b_["graw"], b_["sigg"], ALU.mult, "gate")
                        dve.tensor_copy(d16, b_["E"].rearrange("p (a b) -> p a b", b=C)[:, :, C - 1])\
                           .then_inc(p_dve.sem, p_dve.one("d16"))
                        dve.wait_ge(p_dve.sem, p_dve.done("d16", R))
                        pair = lambda d: d.rearrange("p (a b) -> p a b", b=2)
                        dd = [pair(d16[:, 1:33]), pair(d32), pair(d64)]
                        for name, src, dst in (("d32", dd[0], d32), ("d64", dd[1], d64), ("d128", dd[2], d128)):
                            tt(dst, src[:, :, 0], src[:, :, 1], ALU.mult, name)
                            dve.wait_ge(p_dve.sem, p_dve.done(name, R))
                        for lv, (w, src, dst) in enumerate(((16, ("q16", "kt16"), ("q32", "k32")),
                                                            (32, ("q32", "k32"), ("q64", "k64")),
                                                            (64, ("q64", "k64"), ("q128", "k128")))):
                            nb = SEQ // (2 * w)
                            if lv:
                                dve.wait_ge(p_act.sem, p_act.done(src[1], R))
                                dve.wait_ge(p_dve.sem, p_dve.done(src[1], R))
                            tt(v(dst[0], w)[:, :, 1], v(src[0], w)[:, :, 1], dd[lv][:, :, 0:1].broadcast_to([P, nb, w]),
                               ALU.mult, dst[0])
                            tt(v(dst[1], w)[:, :, 0], v(src[1], w)[:, :, 0], dd[lv][:, :, 1:2].broadcast_to([P, nb, w]),
                               ALU.mult, dst[1])

                def attend(s, r, i, g):
                    R = r + i
                    f = flat(g)
                    if s == "VK":
                        dve.wait_ge(a_act.sem, a_act.done("vt", R))
                        dve.tensor_copy(kt[:, 0:512], f[:, 512:1024]).then_inc(tile_free, 1)
                    elif s == "M":
                        dve.wait_ge(a_pe.sem, a_pe.done(s, R))
                        dve.tensor_copy(vt[0:META, 512:640], f[0:META, 0:P]).then_inc(a_dve.sem, a_dve.one("vtm"))
                        dve.tensor_copy(kt[0:META, 512:640], f[0:META, P:2 * P]).then_inc(a_dve.sem, a_dve.one("ktm"))
                        dve.tensor_tensor(at_[1][0:META, 0:META], f[0:META, 256:256 + META], b_["masks"][0:META, 0:META],
                                          ALU.mult).then_inc(tile_free, 1)
                    elif s == "OM":
                        dve.wait_ge(a_pe.sem, a_pe.done(s, R))
                        dve.tensor_copy(b_["o"][:, 0:META], f[:, 0:META]).then_inc(a_dve.sem, a_dve.one("om"))
                        dve.tensor_copy(state, f[:, 512:640]).then_inc(tile_free, 1)
                    elif s == "N":
                        dve.wait_ge(a_pe.sem, a_pe.done(s, R))
                        dve.tensor_scalar(halves(b_["ms"]), tile(g), 1.0 / P, EPS, ALU.mult, ALU.add).then_inc(tile_free, 1)
                    elif s == "F":
                        dve.wait_ge(a_act.sem, a_act.done("exp", R))
                        newton(dve, b_["fac"], b_["ms"], b_["sqo"], a_dve, ("nw0", "nw1", "fac"), R)
                        dve.scalar_tensor_tensor(b_["o"], b_["o"], g_o, b_["fac"], ALU.mult, ALU.mult)\
                           .then_inc(a_dve.sem, a_dve.one("scaled"))
                        dve.wait_ge(a_dve.sem, a_dve.done("scaled", R))
                        tt(b_["fac"], b_["o"], b_["gate"], ALU.mult, "gated", a_dve)
                        dve.wait_ge(a_dve.sem, a_dve.done("gated", R))
                    elif s[0] == "S":
                        b = s[1]
                        dve.wait_ge(a_pe.sem, a_pe.done(s, R))
                        if b:
                            dve.wait_ge(a_dve.sem, a_dve.done(("at", b - 1), R))
                        masked = dve.tensor_tensor(mk, f[:, 0:512], b_["masks"][:, 0:512], ALU.mult)
                        if b < QB - 1:
                            masked.then_inc(a_dve.sem, a_dve.one(("mk", b)))
                            dve.wait_ge(a_dve.sem, a_dve.done(("mk", b), R))
                            dve.tensor_copy(us[b % 2], f[:, 512:640]).then_inc(tile_free, 1)
                        else:
                            masked.then_inc(tile_free, 1)
                            dve.wait_ge(tile_free, g + 1 + i * PER)
                        dve.tensor_reduce(at_[b % 2], mk.rearrange("p (l t) -> p t l", t=P), AX.X, ALU.add)\
                           .then_inc(a_dve.sem, a_dve.one(("at", b)))
                    else:
                        b = s[1]
                        c = slice(META + b * P, META + (b + 1) * P)
                        dve.wait_ge(a_pe.sem, a_pe.done(s, R))
                        if b < QB - 1:
                            dve.scalar_tensor_tensor(state, state, d128[:, b:b + 1], us[b % 2], ALU.mult, ALU.add)\
                               .then_inc(a_dve.sem, a_dve.one(("st", b)))
                        dve.tensor_copy(b_["o"][:, c], f[:, 0:P]).then_inc(tile_free, 1)

                walk(dve, proj, attend)
                out_dve(dve, n + 1, uO, gO)

            def act_(act):
                last_stage_over(act, n)
                act.dma_start(b_["masks"][:, 0:512], a["hgrn_masks"]).then_inc(consts_in, 16)
                act.dma_start(scan_mask, a["hgrn_scan"]).then_inc(consts_in, 16)
                act.dma_start(misc[:, 336:372], a["hgrn_par"]).then_inc(consts_in, 16)
                act.wait_ge(c_dve.sem, c_dve.done("sub3"))
                act.activation(le, lg, ACT.Exp).then_inc(c_act.sem, c_act.one("exp"))
                norm_act_(act, n, g0)

                def f(out, x, func, name, o=p_act, **kw):
                    act.activation(out, x, func, **kw).then_inc(o.sem, o.one(name))

                def v(name, count):
                    return b_[name][:, META:].rearrange("p (a b c) -> p a b c", b=2, c=count)

                def proj(s, r, i, g):
                    R = r + i
                    if s in UNIT_OF:
                        round_unit(act, u0 + 4 * r + UNIT_OF[s] + AHEAD, i, 4)
                    if s in ("f", "q", "g"):
                        act.wait_ge(tile_free, g + 1 + i * PER)
                        src = {"f": "fg", "q": "qraw", "g": "graw"}[s]
                        dst = {"f": "fg", "q": "sigq", "g": "sigg"}[s]
                        f(b_[dst], b_[src], ACT.Sigmoid, "sig" + s)
                    elif s == "e1":
                        act.wait_ge(p_dve.sem, p_dve.done("k", R))
                        f(b_["fg"], b_["fg"], ACT.Ln, "ln")
                    elif s == "e2":
                        act.wait_ge(p_dve.sem, p_dve.done("tail", R))
                        f(b_["E"], b_["G"], ACT.Exp, "E")
                        f(b_["Ei"], b_["G"], ACT.Exp, "Ei", scale=-1.0)
                        f(b_["Et"], b_["Et"], ACT.Exp, "Et")
                    elif s == "e4":
                        act.wait_ge(p_dve.sem, p_dve.done("kt16", R))
                        for w, src, dst in ((16, ("q16", "kt16"), ("q32", "k32")), (32, ("q32", "k32"), ("q64", "k64")),
                                            (64, ("q64", "k64"), ("q128", "k128"))):
                            if w > 16:
                                act.wait_ge(p_dve.sem, p_dve.done(src[1], R))
                                act.wait_ge(p_act.sem, p_act.done(src[1], R))
                            f(v(dst[0], w)[:, :, 0], v(src[0], w)[:, :, 0], ACT.Copy, dst[0])
                            f(v(dst[1], w)[:, :, 1], v(src[1], w)[:, :, 1], ACT.Copy, dst[1])
                        f(b_["k128"][:, 0:META], b_["kt16"][:, 0:META], ACT.Copy, "k128m")

                def attend(s, r, i, g):
                    R = r + i
                    if s == "VK":
                        act.wait_ge(a_pe.sem, a_pe.done(s, R))
                        f(vt[:, 0:512], flat(g)[:, 0:512], ACT.Copy, "vt", a_act)
                    elif s == "N":
                        act.wait_ge(tile_free, g + i * PER)
                        f(b_["sqo"], b_["o"], ACT.Square, "sqo", a_act)
                    elif s == "F":
                        act.wait_ge(tile_free, g_of("N", g) + 1 + i * PER)
                        act.wait_ge(a_pool.sem, a_pool.done("lo", R) - 1)
                        f(b_["fac"], b_["ms"], ACT.Ln, "ln", a_act)
                        act.wait_ge(a_act.sem, a_act.done("ln", R))
                        f(b_["fac"], b_["fac"], ACT.Exp, "exp", a_act, scale=-0.5)
                        act.wait_ge(a_dve.sem, a_dve.done("gated", R))
                        hi = hid[:, bass.ds(R, 1), 0].rearrange("p a b -> p (a b)")
                        f(hi, b_["fac"], ACT.Copy, "hi", a_act)

                walk(act, proj, attend)
                out_act(act, n + 1, uO)

            def pool_(pool):
                pool.sem_inc(a_pool.sem, 1)

                def proj(s, r, i, g):
                    if s in UNIT_OF:
                        split_unit(pool, u0 + 4 * r + UNIT_OF[s] + AHEAD, i, 4)

                def attend(s, r, i, g):
                    if s == "F":
                        pool.wait_ge(a_act.sem, a_act.done("hi", r + i))
                        hi = hid[:, bass.ds(r + i, 1), 0].rearrange("p a b -> p (a b)")
                        lo = hid[:, bass.ds(r + i, 1), 1].rearrange("p a b -> p (a b)")
                        pool.tensor_tensor(lo, b_["fac"], hi.bitcast(F32), ALU.subtract)\
                            .then_inc(a_pool.sem, a_pool.one("lo"))

                walk(pool, proj, attend)
                out_pool(pool, n + 1, uO)

            return {"pe": pe_, "dve": dve_, "act": act_, "pool": pool_}

        def s5(n, u0, g0):
            if "s5" not in stages:
                return {}
            NPAIR, CH = D // 32, 64
            HP = NPAIR // 2
            NCH = 1 + SEQ // CH
            av = work[:, 0:8]
            flat_work = work[:].rearrange("p a b -> p (a b)")
            cols = [8 * T]

            def take(k):
                cols[0] += k
                return flat_work[:, cols[0] - k:cols[0]]
            Tc, Ts, R0 = (take(NPAIR * CH).rearrange("p (a b) -> p a b", b=CH) for _ in range(3))
            Bl = take(2 * DT * P).rearrange("p (f c s) -> p f c s", c=2, s=P)
            Cl = take(2 * NPAIR * 32).rearrange("p (a c s) -> p a c s", c=2, s=32)
            lre, lim, ldt, mag, zre, zim, xr, xi, cr, ci = (take(NPAIR) for _ in range(10))
            assert cols[0] <= NW * T
            tmp = [work2[:, 1024 * k:1024 * (k + 1)] for k in range(8)]
            pairs = lambda t: t.rearrange("p (a b) -> p a b", a=NPAIR)
            chunk = [spare[:, 2048 * k:2048 * (k + 1)].rearrange("p (f q s) -> p f q s", q=4, s=CH) for k in range(2)]
            braw, bbar = [tmp[0], tmp[1]], [tmp[2], tmp[3]]
            scr_ = scr[:].rearrange("p a b -> p (a b)")
            zr, zi, dcol = scr_[:, 0:1024], scr_[:, 1024:2048], scr_[:, 2048:2056]
            R0m = ub[:, 0, 2:514].rearrange("p (a b) -> p a b", b=META)
            dt, ang, sn, sh, cs, are, kk, rr, pp, t0, t1 = (tmp[4][:, 32 * k:32 * k + 32] for k in range(11))

            LOG2E, LN2_A, LN2_B = 1.4426950408889634, 0.693359375, -2.12194440e-4
            TWO_PI, TWO_PI_A, PI_BELOW = 6.283185307179586, 6.28125, 3.1415925
            ROUND = 12582912.0

            gB = g0 + 1
            gM = gB + 2
            gS = gM + 2
            gO = gS + 6 * (NCH - 1) + 4
            assert gO + 2 * DT == g0 + 1 + S5_TILES, gO + 2 * DT - g0 - 1

            consts_in = sem("s5_consts")
            EXP = ["k", "int", "ra", "rb", "clamp", "two"] + [f"p{k}" for k in range(8)]
            SETUP = [("dt", x) for x in EXP] + ["x"] + [("mag", x) for x in EXP] + \
                ["ang", "turns", "int", "ra", "rb", "clamp", "s2", "cs", "are", "aim", "are1", "m1", "m2", "num_re",
                 "m3", "m4", "num_im", "d1", "d2", "den", "rden", "zre", "zim"] + \
                [("bb", k) for k in range(6)] + ["T0c", "T0s"] + [(x, m) for m in range(6) for x in range(6)] + \
                ["R0", "R0z", "R0m", "R0mz", "x0r", "x0i"] + [("a", m) for m in range(DT)]
            c_dve = Order(sem("s5_c_dve"), SETUP)
            c_act = Order(sem("s5_c_act"), ["sin", "sinh"])
            c_pe = Order(sem("s5_c_pe"), ["B0", "B1"])
            HALFN = ["t1", "t2", "wr", "wi", "c0", "c1", "c2", "c3", "zr", "zi", "p1", "p2", "p3", "p4", "xr", "xi"]
            h_dve = [Order(sem(f"s5_half{hf}"), HALFN) for hf in range(2)]
            bu_pe = [sem(f"s5_bu{hf}") for hf in range(2)]
            y_pe = [sem(f"s5_y{hf}") for hf in range(2)]
            y_read = Order(sem("s5_y_read"), [(hf, f) for hf in range(2) for f in range(3)])
            g_act = Order(sem("s5_g_act"), [(x, m) for m in range(DT) for x in ("gelu", "hi")])
            g_pool = Order(sem("s5_g_pool"), [("lo", m) for m in range(DT)])
            chunk_in = sem("s5_chunk_in")
            chunk_zero = sem("s5_chunk_zero")
            o_act = sem("s5_gate")

            def inputs(t, k, i):
                if k == 0:
                    return av[:, t, 0:META]
                at_ = META + CH * (k - 1)
                return av[:, t, at_:at_ + CH] if isinstance(i, int) else av[:, t, bass.ds(i * (2 * CH) + at_, CH)]

            def walk(eng, bu, y):
                def step(k, i, g):
                    bu(1, k, i, g)
                    if k < NCH - 1:
                        bu(0, k + 1, i, g + 2)
                        g += 2
                    y(0, k, i, g + 2)
                    y(1, k, i, g + 3)
                bu(0, 0, 0, gM)
                step(0, 0, gS)
                with eng.Fori(0, (NCH - 3) // 2) as i:
                    for k in (1, 2):
                        step(k, i, gS + 6 * k)
                for k in (NCH - 2, NCH - 1):
                    step(k, 0, gS + 6 * k)

            def pe_(pe):
                norm_pe(pe, n, g0)
                pe.wait_ge(c_dve.sem, c_dve.done(("bb", 5)))
                for x in range(2):
                    pe.wait_ge(tile_free, gB + x - 3)
                    for f in range(DT):
                        mm = pe.transpose(flat(gB + x)[:, f * P:(f + 1) * P], bbar[x][:, f * P:(f + 1) * P], ident[:])
                    mm.then_inc(c_pe.sem, c_pe.one(f"B{x}"))
                pe.wait_ge(tile_free, gB + 2)
                pe.wait_ge(c_dve.sem, c_dve.done(("a", DT - 1)))
                pe.wait_ge(consts_in, 64)

                def bu(hf, k, i, g):
                    N = META if k == 0 else CH
                    pe.wait_ge(chunk_in, 4 * k + 4 + i * 8)
                    for part in range(2):
                        pe.wait_ge(tile_free, g + part - 3 + i * 12)
                        for f in range(4):
                            out = flat(g + part)[:, f * 256:(f + 1) * 256].rearrange("p (a b) -> p a b", b=CH)
                            mm = pe.matmul(out[:, :, 0:N], Bl[:, hf * 4 + f, part, :], chunk[k % 2][:, hf * 4 + f, :, 0:N],
                                           start=True, stop=True)
                    mm.then_inc(bu_pe[hf], 1)

                def y(hf, k, i, g):
                    N = META if k == 0 else CH
                    pe.wait_ge(tile_free, g - 3 + i * 12)
                    pe.wait_ge(h_dve[hf].sem, h_dve[hf].done("p4", k + i * 2))
                    for q in range(HP):
                        pair = hf * HP + q
                        r0 = 32 * (pair % 4)
                        for x in range(4):
                            mm = pe.matmul(flat(g)[r0:r0 + 32, (q // 4) * CH:(q // 4) * CH + N],
                                           Cl[:, pair, x // 2, :], tmp[4 * hf + x][:, q * N:(q + 1) * N],
                                           start=x == 0, stop=x == 3, tile_position=(0, r0))
                    mm.then_inc(y_pe[hf], 1)

                walk(pe, bu, y)
                pe.wait_ge(g_pool.sem, g_pool.done(("lo", DT - 1)))
                for m in range(2 * DT):
                    pe.wait_ge(lo_ready, u0 + m + 1)
                    pe.wait_ge(tile_free, gO + m - 3)
                    project(pe, tile(gO + m), (u0 + m) % RING, 0, split_tiles(hid, range(DT)), True, True, unit_done)

            def dve_(dve):
                def did(name, ins):
                    ins.then_inc(c_dve.sem, c_dve.one(name))
                    dve.wait_ge(c_dve.sem, c_dve.done(name))

                def tt(name, out, x, y, op):
                    did(name, dve.tensor_tensor(out, x, y, op))

                def ts(name, out, x, s1, s2, op1, op2):
                    did(name, dve.tensor_scalar(out, x, s1, s2, op1, *([op2] if op2 else [])))

                def stt(name, out, x, s, y, op1, op2):
                    did(name, dve.scalar_tensor_tensor(out, x, s, y, op1, op2))

                def exp(v, out, x):
                    ts((v, "k"), kk, x, LOG2E, ROUND, ALU.mult, ALU.add)
                    ts((v, "int"), kk, kk, ROUND, None, ALU.subtract, None)
                    stt((v, "ra"), rr, kk, -LN2_A, x, ALU.mult, ALU.add)
                    stt((v, "rb"), rr, kk, -LN2_B, rr, ALU.mult, ALU.add)
                    ts((v, "clamp"), kk, kk, -127.0, 128.0, ALU.max, ALU.min)
                    ts((v, "two"), t0.bitcast(mybir.dt.int32), kk, 2.0 ** 23, 127 * 2.0 ** 23, ALU.mult, ALU.add)
                    c, fact = [], 1.0
                    for k in range(1, 8):
                        fact *= k
                        c.append(1.0 / fact)
                    ts((v, "p0"), pp, rr, c[6], None, ALU.mult, None)
                    for k in range(1, 7):
                        stt((v, f"p{k}"), pp, pp, c[6 - k], rr, ALU.add, ALU.mult)
                    stt((v, "p7"), out, pp, 1.0, t0, ALU.add, ALU.mult)

                dve.wait_ge(consts_in, 64)
                exp("dt", dt, ldt)
                tt("x", t1, lre, dt, ALU.mult)
                exp("mag", mag, t1)
                tt("ang", ang, lim, dt, ALU.mult)
                ts("turns", kk, ang, 1.0 / TWO_PI, ROUND, ALU.mult, ALU.add)
                ts("int", kk, kk, ROUND, None, ALU.subtract, None)
                stt("ra", ang, kk, -TWO_PI_A, ang, ALU.mult, ALU.add)
                stt("rb", ang, kk, -(TWO_PI - TWO_PI_A), ang, ALU.mult, ALU.add)
                ts("clamp", ang, ang, -PI_BELOW, PI_BELOW, ALU.max, ALU.min)
                dve.wait_ge(c_act.sem, c_act.done("sinh"))
                tt("s2", cs, sh, sh, ALU.mult)
                ts("cs", cs, cs, -2.0, 1.0, ALU.mult, ALU.add)
                tt("are", are, mag, cs, ALU.mult)
                tt("aim", t1, mag, sn, ALU.mult)
                ts("are1", are, are, 1.0, None, ALU.subtract, None)
                tt("m1", zre, are, lre, ALU.mult)
                tt("m2", t0, t1, lim, ALU.mult)
                tt("num_re", zre, zre, t0, ALU.add)
                tt("m3", zim, t1, lre, ALU.mult)
                tt("m4", t0, are, lim, ALU.mult)
                tt("num_im", zim, zim, t0, ALU.subtract)
                tt("d1", t0, lre, lre, ALU.mult)
                tt("d2", t1, lim, lim, ALU.mult)
                tt("den", t0, t0, t1, ALU.add)
                did("rden", dve.reciprocal(t0, t0))
                tt("zre", zre, zre, t0, ALU.mult)
                tt("zim", zim, zim, t0, ALU.mult)
                wide = lambda v, k: v.rearrange("p (a b) -> p a b", b=1).broadcast_to([P, NPAIR, k])
                for x in range(2):
                    tt(("bb", 3 * x), pairs(bbar[x]), pairs(braw[x]), wide(zre, 32), ALU.mult)
                    tt(("bb", 3 * x + 1), pairs(tmp[5]), pairs(braw[1 - x]), wide(zim, 32), ALU.mult)
                    tt(("bb", 3 * x + 2), bbar[x], bbar[x], tmp[5], ALU.add if x else ALU.subtract)
                did("T0c", dve.tensor_copy(Tc[:, :, 0], cs))
                did("T0s", dve.tensor_copy(Ts[:, :, 0], sn))
                for m in range(6):
                    N = 1 << m
                    a_, b_, c_, d_ = (pairs(tmp[x])[:, :, 0:N] for x in (5, 6, 7, 4))
                    cN, sN = (t[:, :, N - 1:N].broadcast_to([P, NPAIR, N]) for t in (Tc, Ts))
                    tt((0, m), a_, Tc[:, :, 0:N], cN, ALU.mult)
                    tt((1, m), b_, Ts[:, :, 0:N], sN, ALU.mult)
                    tt((2, m), c_, Ts[:, :, 0:N], cN, ALU.mult)
                    tt((3, m), d_, Tc[:, :, 0:N], sN, ALU.mult)
                    tt((4, m), Tc[:, :, N:2 * N], a_, b_, ALU.subtract)
                    tt((5, m), Ts[:, :, N:2 * N], c_, d_, ALU.add)
                norm_dve(dve, n, g0)
                did("R0", dve.tensor_copy(R0, wide(mag, CH)))
                did("R0z", dve.memset(R0[:, :, 0], 0.0))
                did("R0m", dve.tensor_copy(R0m, wide(mag, META)))
                did("R0mz", dve.memset(R0m[:, :, 0], 0.0))
                did("x0r", dve.memset(xr, 0.0))
                did("x0i", dve.memset(xi, 0.0))
                dve.wait_ge(c_pe.sem, c_pe.done("B0"))
                dve.tensor_copy(Bl[:, :, 0, :], flat(gB).rearrange("p (f s) -> p f s", s=P)).then_inc(tile_free, 1)
                dve.wait_ge(c_pe.sem, c_pe.done("B1"))
                dve.tensor_copy(Bl[:, :, 1, :], flat(gB + 1).rearrange("p (f s) -> p f s", s=P)).then_inc(tile_free, 1)
                dve.wait_ge(tile_free, gB + 2)
                for m in range(DT):
                    dve.scalar_tensor_tensor(av[:, m], h[:, m], gains[:, first + n, m:m + 1], rstd[:], ALU.mult, ALU.mult)\
                       .then_inc(c_dve.sem, c_dve.one(("a", m)))
                dve.wait_ge(c_dve.sem, c_dve.done(("a", DT - 1)))

                def bu(hf, k, i, g):
                    o, r, N = h_dve[hf], k + i * 2, META if k == 0 else CH
                    e = HP * N
                    v3 = lambda x: x.rearrange("p (a b) -> p a b", b=N)
                    T1, T2, T3, T4 = (v3(tmp[4 * hf + x][:, 0:e]) for x in range(4))
                    wr, wi = zr[:, 0:e], zi[:, 0:e]
                    hs = slice(hf * HP, (hf + 1) * HP)
                    tc, ts_ = Tc[:, hs, 0:N], Ts[:, hs, 0:N]
                    re, im = (flat(g + x).rearrange("p (a b) -> p a b", b=CH)[:, :, 0:N] for x in range(2))
                    decay = (R0m if k == 0 else R0)[:, hs].rearrange("p a b -> p (a b)")

                    def one(ins, name):
                        ins.then_inc(o.sem, o.one(name))
                    dve.wait_ge(bu_pe[hf], k + 1 + i * 2)
                    if k > 0:
                        dve.wait_ge(y_pe[hf], k + i * 2)
                    one(dve.tensor_tensor(T1, re, tc, ALU.mult), "t1")
                    dve.tensor_tensor(T4, re, ts_, ALU.mult).then_inc(tile_free, 1)
                    one(dve.tensor_tensor(T2, im, ts_, ALU.mult), "t2")
                    dve.tensor_tensor(T3, im, tc, ALU.mult).then_inc(tile_free, 1)
                    dve.wait_ge(o.sem, o.done("t2", r))
                    one(dve.tensor_tensor(v3(wr), T1, T2, ALU.add), "wr")
                    dve.wait_ge(tile_free, g + 2 + i * 12)
                    one(dve.tensor_tensor(v3(wi), T3, T4, ALU.subtract), "wi")
                    one(dve.tensor_tensor(cr[:, hs], xr[:, hs], mag[:, hs], ALU.mult), "c0")
                    one(dve.tensor_tensor(ci[:, hs], xi[:, hs], mag[:, hs], ALU.mult), "c1")
                    dve.wait_ge(o.sem, o.done("c1", r))
                    one(dve.tensor_tensor(v3(wr)[:, :, 0], v3(wr)[:, :, 0], cr[:, hs], ALU.add), "c2")
                    one(dve.tensor_tensor(v3(wi)[:, :, 0], v3(wi)[:, :, 0], ci[:, hs], ALU.add), "c3")
                    dve.wait_ge(o.sem, o.done("c3", r))
                    one(dve.tensor_tensor_scan(wr, decay, wr, 0.0, ALU.mult, ALU.add), "zr")
                    one(dve.tensor_tensor_scan(wi, decay, wi, 0.0, ALU.mult, ALU.add), "zi")
                    dve.wait_ge(o.sem, o.done("zi", r))
                    one(dve.tensor_tensor(T1, tc, v3(wr), ALU.mult), "p1")
                    one(dve.scalar_tensor_tensor(T2, ts_, -1.0, v3(wi), ALU.mult, ALU.mult), "p2")
                    one(dve.scalar_tensor_tensor(T3, ts_, -1.0, v3(wr), ALU.mult, ALU.mult), "p3")
                    one(dve.scalar_tensor_tensor(T4, tc, -1.0, v3(wi), ALU.mult, ALU.mult), "p4")
                    dve.wait_ge(o.sem, o.done("p4", r))
                    one(dve.tensor_tensor(xr[:, hs], T1[:, :, N - 1], T2[:, :, N - 1], ALU.add), "xr")
                    one(dve.scalar_tensor_tensor(xi[:, hs], T3[:, :, N - 1], -1.0, T4[:, :, N - 1], ALU.mult,
                                                 ALU.subtract), "xi")
                    dve.wait_ge(o.sem, o.done("xi", r))

                def y(hf, k, i, g):
                    N = META if k == 0 else CH
                    dve.wait_ge(y_pe[hf], k + 1 + i * 2)
                    for f in range(4):
                        t = hf * 4 + f
                        ins = dve.scalar_tensor_tensor(inputs(t, k, i), inputs(t, k, i), dcol[:, t:t + 1],
                                                       flat(g)[:, f * CH:f * CH + N], ALU.mult, ALU.add)
                        if f < 3:
                            ins.then_inc(y_read.sem, y_read.one((hf, f)))
                        else:
                            ins.then_inc(tile_free, 1)

                walk(dve, bu, y)
                for m in range(DT):
                    val, gate = gO + 2 * m, gO + 2 * m + 1
                    gated = work[:, 10]
                    dve.wait_ge(o_act, m + 1)
                    if m >= 1:
                        dve.wait_ge(tile_free, val)
                    dve.tensor_tensor(halves(gated), tile(val), halves(work[:, 8 + m % 2]), ALU.mult).then_inc(tile_free, 1)
                    dve.wait_ge(tile_free, val + 1)
                    dve.tensor_tensor(h[:, m], h[:, m], gated, ALU.add).then_inc(tile_free, 1)
                    dve.wait_ge(tile_free, gate + 1)
                    tail_dve_(dve, n + 1, m)

            def act_(act):
                last_stage_over(act, n)
                act.dma_start(flat_work[:, cols[0] - 10 * NPAIR:cols[0] - 7 * NPAIR], a["s5_lam"]).then_inc(consts_in, 16)
                act.dma_start(work2[:, 0:2048], a["s5_b"]).then_inc(consts_in, 16)
                act.dma_start(Cl.rearrange("p a c s -> p (a c s)"), a["s5_c"]).then_inc(consts_in, 16)
                act.dma_start(dcol, a["s5_d"]).then_inc(consts_in, 16)
                act.wait_ge(c_dve.sem, c_dve.done("clamp"))
                act.activation(sn, ang, ACT.Sin).then_inc(c_act.sem, c_act.one("sin"))
                act.activation(sh, ang, ACT.Sin, scale=0.5).then_inc(c_act.sem, c_act.one("sinh"))
                norm_act_(act, n, g0)

                def bu(hf, k, i, g):
                    if hf == 1:
                        return
                    if k == 0:
                        act.wait_ge(c_dve.sem, c_dve.done(("a", DT - 1)))
                        act.wait_ge(chunk_zero, 1)
                    if k >= 2:
                        act.wait_ge(bu_pe[1], k - 1 + i * 2)
                    N = META if k == 0 else CH
                    at_ = META + CH * (k - 1) if k else 0
                    for q in range(4):
                        rows = slice(32 * q, 32 * q + 32)
                        src = av[rows, :, at_:at_ + N] if isinstance(i, int) else \
                            av[rows, :, bass.ds(i * (2 * CH) + at_, N)]
                        act.activation(chunk[k % 2][rows, :, q, 0:N], src, ACT.Copy).then_inc(chunk_in, 1)

                walk(act, bu, lambda *_: None)
                act.wait_ge(tile_free, gO)
                for m in range(DT):
                    if m == 4:
                        act.wait_ge(y_read.sem, y_read.done((1, 2), NCH - 1))
                    elif m == 0:
                        act.wait_ge(y_read.sem, y_read.done((0, 2), NCH - 1))
                    act.activation(av[:, m], av[:, m], ACT.Gelu_apprx_tanh).then_inc(g_act.sem, g_act.one(("gelu", m)))
                    act.wait_ge(g_act.sem, g_act.done(("gelu", m)))
                    act.activation(hid[:, m, 0], av[:, m], ACT.Copy).then_inc(g_act.sem, g_act.one(("hi", m)))
                for m in range(DT):
                    round_unit(act, u0 + 2 * m + AHEAD)
                    if m >= 2:
                        act.wait_ge(tile_free, gO + 2 * m - 3)
                    act.wait_ge(unit_done, u0 + 2 * m + 2)
                    act.activation(halves(work[:, 8 + m % 2]), tile(gO + 2 * m + 1), ACT.Sigmoid).then_inc(o_act, 1)
                    round_unit(act, u0 + 2 * m + 1 + AHEAD)
                    tail_act_(act, n + 1, m)

            def pool_(pool):
                last_stage_over(pool, n)
                pool.memset(spare[:, 0:4096], 0.0).then_inc(chunk_zero, 1)
                for m in range(DT):
                    pool.wait_ge(g_act.sem, g_act.done(("hi", m)))
                    pool.tensor_tensor(hid[:, m, 1], av[:, m], hid[:, m, 0].bitcast(F32), ALU.subtract)\
                        .then_inc(g_pool.sem, g_pool.one(("lo", m)))
                for m in range(DT):
                    split_unit(pool, u0 + 2 * m + AHEAD)
                    split_unit(pool, u0 + 2 * m + 1 + AHEAD)
                    tail_pool_(pool, n + 1, m)

            return {"pe": pe_, "dve": dve_, "act": act_, "pool": pool_}

        def ret(n, u0, g0):
            if "ret" not in stages:
                return {}
            flat_work = work[:].rearrange("p a b -> p (a b)")
            qrot, krot = [work[:, 0], work[:, 1]], [work[:, 2], work[:, 3]]
            ra, rb, rc, rd = (work[:, k] for k in range(4, 8))
            tab = work[:, 8:12]
            vfm = [work[:, 12 + t] for t in range(4)]
            vtok = flat_work[:, 16 * T:16 * T + 2560].rearrange("p (b d) -> p b d", d=RDV)
            gn = flat_work[:, 16 * T + 2560:16 * T + 2576]
            st_ = flat_work[:, 21 * T:25 * T]
            starts = (0, 512, 896, 1152)
            st = [st_[:, s:s + SEQ - b * P] for b, s in enumerate(starts)]
            stm = st_[0:META, 1280:1280 + T]
            mask = work[:, 25]
            fac, mu = work[:, 26], work[:, 27]
            o = [spare[:, (8 + t) * T:(9 + t) * T] for t in range(4)]
            gate = [spare[:, (12 + t) * T:(13 + t) * T] for t in range(4)]
            ms, nt = scr[:, 1], ub[:, 1, 2:]
            PROJ = ["q0", "q1", "k0", "k1"] + [f"v{t}" for t in range(4)] + [f"g{t}" for t in range(4)]
            UNIT = {s: k for k, s in enumerate(PROJ)}
            HEAD = ["VA", "VB", "VM", "SM", "S01", "S23", "q0'", "q1'", "O0", "O1", "O2", "O3", "k0'", "k1'", "MEAN",
                    "v0'", "v1'", "VAR", "v2'", "v3'", "g0'", "g1'", "g2'", "g3'"]
            ALONE = [s for s in HEAD if s[-1] != "'"]
            PER = len(HEAD) + DT
            assert PER % 4 == 0
            gX = g0 + 1 + len(PROJ)
            gE = gX + PER * (RH - 1)
            gO = gE + len(ALONE)
            assert gO + DT == g0 + 1 + RET_TILES, gO + DT - g0 - 1
            uX, uO = u0 + 12, u0 + 12 + 16 * (RH - 1)

            def walk(eng, project_, attend, out):
                for k, s in enumerate(PROJ):
                    project_(s, 0, 0, u0 + k, g0 + 1 + k)
                with eng.Fori(0, RH - 1) as i:
                    for k, s in enumerate(HEAD):
                        if s[-1] == "'":
                            project_(s[:-1], 1, i, uX + UNIT[s[:-1]], gX + k)
                        else:
                            attend(s, 0, i, gX + k, HEAD)
                    for m in range(DT):
                        out(m, 0, i, uX + 12 + m // 2, gX + len(HEAD) + m)
                for k, s in enumerate(ALONE):
                    attend(s, RH - 1, 0, gE + k, ALONE)
                for m in range(DT):
                    out(m, RH - 1, 0, uO + m // 2, gO + m)

            consts_in, tab_in = sem("ret_consts"), sem("ret_tab")
            p_dve = Order(sem("ret_p_dve"), [c + x for c in "qk" for x in ("c", "d", "1", "a", "b", "2")])
            p_act = Order(sem("ret_p_act"), [f"silu{t}" for t in range(4)])
            a_pe = Order(sem("ret_a_pe"), ALONE)
            a_act = Order(sem("ret_a_act"), ["VA", "VB"] + [f"sq{t}" for t in range(4)] + ["ln", "exp"] +
                          [f"hi{t}" for t in range(4)])
            a_dve = Order(sem("ret_a_dve"), ["SM", "S0", "S2"] + [f"o{t}" for t in range(4)] + ["s0", "s1", "s2"] +
                          [f"d{t}" for t in range(4)] + ["v0", "v1", "v2", "nw0", "nw1", "fac"] +
                          [f"{x}{t}" for t in range(4) for x in ("n", "z")])
            a_pool = Order(sem("ret_a_pool"), [f"lo{t}" for t in range(4)])
            out_even = sem("ret_out_even")

            def pe_(pe):
                norm_pe(pe, n, g0)
                x = split_tiles(xs, range(DT))

                def proj(s, r, i, u, g):
                    pe.wait_ge(lo_ready, u + 1 + i * 16)
                    pe.wait_ge(tile_free, g - 3 + i * PER)
                    project(pe, tile(g), u % RING, 0, x, True, True, unit_done)

                def attend(s, r, i, g, seq):
                    R = r + i
                    pe.wait_ge(tile_free, g - 3 + i * PER)
                    f = flat(g)
                    if s in ("VA", "VB"):
                        for b in range(2):
                            blk = b + 2 * (s == "VB")
                            for t in range(4):
                                mm = pe.transpose(f[:, b * 512 + t * P:b * 512 + (t + 1) * P],
                                                  vfm[t][:, META + blk * P:META + (blk + 1) * P], ident[:])
                    elif s == "VM":
                        for t in range(4):
                            mm = pe.transpose(f[0:META, t * P:(t + 1) * P], vfm[t][:, 0:META], ident[:])
                    elif s == "SM":
                        pe.wait_ge(p_dve.sem, p_dve.done("k2", R))
                        for c, q0, q1 in ((0, META, T), (512, 0, META)):
                            for t in range(2):
                                mm = pe.matmul(f[0:META, c:c + q1 - q0], krot[t][:, 0:META], qrot[t][:, q0:q1],
                                               start=t == 0, stop=t == 1)
                    elif s[0] == "S":
                        for j in range(2):
                            b = int(s[1 + j])
                            k0 = META + b * P
                            for t in range(2):
                                mm = pe.matmul(f[:, j * 512:j * 512 + T - k0], krot[t][:, k0:k0 + P], qrot[t][:, k0:T],
                                               start=t == 0, stop=t == 1)
                    elif s[0] == "O":
                        t = int(s[1])
                        d = slice(t * P, (t + 1) * P)
                        if t == 0:
                            pe.wait_ge(tile_free, g_of("S23", g, seq) + 1 + i * PER)
                        pe.matmul(f[:, 512:512 + META], vtok[0:META, 4, d], stm[:, SEQ:T], start=True, stop=True)
                        pe.matmul(f[:, 0:SEQ], vtok[0:META, 4, d], stm[:, 0:SEQ], start=True, stop=False)
                        for b in range(QB):
                            mm = pe.matmul(f[:, b * P:SEQ], vtok[:, b, d], st[b], start=False, stop=b == QB - 1)
                    else:
                        pe.wait_ge(a_dve.sem, a_dve.done("s2" if s == "MEAN" else "v2", R))
                        src = fac if s == "MEAN" else scr[:, 0]
                        for q in range(2):
                            mm = pe.matmul(tile(g)[:, q], ones[:], src[:, q * HALF:(q + 1) * HALF], start=True, stop=True)
                    mm.then_inc(a_pe.sem, a_pe.one(s))

                def out(m, r, i, u, g):
                    if m == 0:
                        pe.wait_ge(a_pool.sem, a_pool.done("lo3", r + i))
                    if m % 2 == 0:
                        pe.wait_ge(lo_ready, u + 1 + i * 16)
                    pe.wait_ge(tile_free, g - 3 + i * PER)
                    project(pe, tile(g), u % RING, 4 * (m % 2), split_tiles(hid, range(4)), True, True,
                            unit_done if m % 2 else out_even)

                walk(pe, proj, attend, out)

            def g_of(s, g, seq):
                return g - (seq.index("O0") - seq.index(s))

            def dve_(dve):
                norm_dve(dve, n, g0)

                def one(order, name, ins):
                    ins.then_inc(order.sem, order.one(name))

                def rope(c, out, r):
                    j = 2 * (c == "k")
                    one(p_dve, c + "c", dve.tensor_tensor(rc, ra, tab[:, j], ALU.mult))
                    one(p_dve, c + "d", dve.tensor_tensor(rd, rb, tab[:, j + 1], ALU.mult))
                    dve.wait_ge(p_dve.sem, p_dve.done(c + "d", r))
                    one(p_dve, c + "1", dve.tensor_tensor(out[0], rc, rd, ALU.subtract))
                    one(p_dve, c + "a", dve.tensor_tensor(ra, ra, tab[:, j + 1], ALU.mult))
                    one(p_dve, c + "b", dve.tensor_tensor(rb, rb, tab[:, j], ALU.mult))
                    dve.wait_ge(p_dve.sem, p_dve.done(c + "b", r))
                    one(p_dve, c + "2", dve.tensor_tensor(out[1], ra, rb, ALU.add))
                    dve.wait_ge(p_dve.sem, p_dve.done(c + "2", r))

                def proj(s, r, i, u, g):
                    R = r + i
                    dst = {"q0": ra, "q1": rb, "k0": ra, "k1": rb}.get(s)
                    if dst is None:
                        dst = (vfm if s[0] == "v" else gate)[int(s[1])]
                    dve.wait_ge(unit_done, u + 1 + i * 16)
                    if s == "q0":
                        dve.wait_ge(tab_in, 16 * r + 16 + i * 16)
                    dve.tensor_tensor(halves(dst), tile(g), halves(rstd[:]), ALU.mult).then_inc(tile_free, 1)
                    if s in ("q1", "k1"):
                        dve.wait_ge(tile_free, g + 1 + i * PER)
                    if s == "q1":
                        rope("q", qrot, R)
                    elif s == "k1" and r == 0:
                        rope("k", krot, R)

                def attend(s, r, i, g, seq):
                    R = r + i
                    f = flat(g)
                    dve.wait_ge(a_pe.sem, a_pe.done(s, R))
                    if s in ("VA", "VB"):
                        dve.wait_ge(a_act.sem, a_act.done(s, R))
                        dve.tensor_copy(vtok[:, 1 + 2 * (s == "VB")], f[:, 512:1024]).then_inc(tile_free, 1)
                    elif s == "VM":
                        dve.tensor_copy(vtok[0:META, 4], f[0:META, 0:512]).then_inc(tile_free, 1)
                    elif s == "SM":
                        one(a_dve, "SM", dve.tensor_copy(stm[:, 0:SEQ], f[0:META, 0:512]))
                        dve.tensor_tensor(stm[:, SEQ:T], f[0:META, 512:512 + META], mask[0:META, 0:META], ALU.mult)\
                           .then_inc(tile_free, 1)
                    elif s[0] == "S":
                        b = int(s[1])
                        w = SEQ - b * P
                        one(a_dve, f"S{b}", dve.tensor_tensor(st[b], f[:, 0:w], mask[:, 0:w], ALU.mult))
                        dve.tensor_tensor(st[b + 1], f[:, 512:512 + w - P], mask[:, 0:w - P], ALU.mult).then_inc(tile_free, 1)
                    elif s[0] == "O":
                        t = int(s[1])
                        one(a_dve, f"o{t}", dve.tensor_copy(o[t][:, 0:META], f[:, 512:512 + META]))
                        dve.tensor_copy(o[t][:, META:], f[:, 0:SEQ]).then_inc(tile_free, 1)
                        if t == 3:
                            dve.wait_ge(tile_free, g + 1 + i * PER)
                            for k in range(3):
                                one(a_dve, f"s{k}", dve.tensor_tensor(fac, o[0] if k == 0 else fac, o[k + 1], ALU.add))
                                dve.wait_ge(a_dve.sem, a_dve.done(f"s{k}", R))
                    elif s == "MEAN":
                        dve.tensor_scalar(halves(mu), tile(g), 1.0 / RDV, None, ALU.mult).then_inc(tile_free, 1)
                        dve.wait_ge(tile_free, g + 1 + i * PER)
                        for t in range(4):
                            one(a_dve, f"d{t}", dve.tensor_tensor(o[t], o[t], mu, ALU.subtract))
                        if r == 0:
                            rope("k", krot, 1 + i)
                    else:
                        dve.tensor_scalar(halves(ms), tile(g), 1.0 / RDV, EPS, ALU.mult, ALU.add).then_inc(tile_free, 1)
                        if r:
                            finish(dve, R)

                def squares(R):
                    for k in range(3):
                        dve.wait_ge(a_act.sem, a_act.done(f"sq{k + 1}", R))
                        one(a_dve, f"v{k}", dve.tensor_tensor(scr[:, 0], scr[:, 0], scr[:, k + 1], ALU.add))
                        dve.wait_ge(a_dve.sem, a_dve.done(f"v{k}", R))

                def finish(dve, R):
                    dve.wait_ge(a_act.sem, a_act.done("exp", R))
                    newton(dve, fac, ms, nt, a_dve, ("nw0", "nw1", "fac"), R)
                    dve.wait_ge(p_act.sem, p_act.done("silu3", R))
                    for t in range(4):
                        col = gn[:, 4 * R + t:4 * R + t + 1] if isinstance(R, int) else gn[:, bass.ds(R * 4 + t, 1)]
                        one(a_dve, f"n{t}", dve.scalar_tensor_tensor(o[t], o[t], col, fac, ALU.mult, ALU.mult))
                        dve.wait_ge(a_dve.sem, a_dve.done(f"n{t}", R))
                        one(a_dve, f"z{t}", dve.tensor_tensor(o[t], o[t], gate[t], ALU.mult))
                        dve.wait_ge(a_dve.sem, a_dve.done(f"z{t}", R))

                def out(m, r, i, u, g):
                    if m % 2:
                        dve.wait_ge(unit_done, u + 1 + i * 16)
                    else:
                        dve.wait_ge(out_even, 4 * r + m // 2 + 1 + i * 4)
                    dve.tensor_tensor(halves(h[:, m]), tile(g), halves(h[:, m]), ALU.add).then_inc(tile_free, 1)
                    if r:
                        dve.wait_ge(tile_free, g + 1)
                        tail_dve_(dve, n + 1, m)

                def proj_(s, r, i, u, g):
                    proj(s, r, i, u, g)
                    if r and s == "v1":
                        squares(i)
                    if r and s == "v3":
                        finish(dve, i)

                def attend_(s, r, i, g, seq):
                    if r and s == "VAR":
                        squares(r)
                    attend(s, r, i, g, seq)

                dve.wait_ge(consts_in, 32)
                walk(dve, proj_, attend_, out)

            def act_(act):
                last_stage_over(act, n)
                act.dma_start(mask, a["ret_mask"]).then_inc(consts_in, 16)
                act.dma_start(gn, a["ret_gn"]).then_inc(consts_in, 16)
                act.dma_start(tab, a["ret_tab"][0]).then_inc(tab_in, 16)
                norm_act_(act, n, g0)

                def f(out, x, func, name, order=a_act, **kw):
                    act.activation(out, x, func, **kw).then_inc(order.sem, order.one(name))

                def proj(s, r, i, u, g):
                    round_unit(act, u + AHEAD, i, 16)
                    if s[0] == "g":
                        t = int(s[1])
                        act.wait_ge(tile_free, g + 1 + i * PER)
                        f(gate[t], gate[t], ACT.Silu, f"silu{t}", p_act)
                    if r and s == "v3":
                        factor(i, gX + HEAD.index("VAR") + 1, i)

                def factor(R, done, i):
                    act.wait_ge(tile_free, done + i * PER)
                    f(fac, ms, ACT.Ln, "ln")
                    act.wait_ge(a_act.sem, a_act.done("ln", R))
                    f(fac, fac, ACT.Exp, "exp", scale=-0.5)
                    for t in range(4):
                        act.wait_ge(a_dve.sem, a_dve.done(f"z{t}", R))
                        f(hid[:, t, 0], o[t], ACT.Copy, f"hi{t}")

                def attend(s, r, i, g, seq):
                    R = r + i
                    if s in ("VA", "VB"):
                        act.wait_ge(a_pe.sem, a_pe.done(s, R))
                        f(vtok[:, 2 * (s == "VB")], flat(g)[:, 0:512], ACT.Copy, s)
                        if s == "VA" and r == 0:
                            act.wait_ge(p_dve.sem, p_dve.done("k2", R))
                            act.dma_start(tab, a["ret_tab"][bass.ds(i + 1, 1)].rearrange("a p c t -> p (a c) t"))\
                               .then_inc(tab_in, 16)
                    elif s == "MEAN":
                        for t in range(4):
                            act.wait_ge(a_dve.sem, a_dve.done(f"d{t}", R))
                            f(scr[:, t], o[t], ACT.Square, f"sq{t}")
                    elif s == "VAR" and r:
                        factor(R, g + 1, 0)

                def out(m, r, i, u, g):
                    if m % 2 == 0:
                        round_unit(act, u + AHEAD, i, 16)
                    if r:
                        tail_act_(act, n + 1, m)

                walk(act, proj, attend, out)

            def pool_(pool):
                def lows(R):
                    for t in range(4):
                        pool.wait_ge(a_act.sem, a_act.done(f"hi{t}", R))
                        pool.tensor_tensor(hid[:, t, 1], o[t], hid[:, t, 0].bitcast(F32), ALU.subtract)\
                            .then_inc(a_pool.sem, a_pool.one(f"lo{t}"))

                def proj(s, r, i, u, g):
                    split_unit(pool, u + AHEAD, i, 16)
                    if r and s == "v3":
                        lows(i)

                def attend(s, r, i, g, seq):
                    if s == "VAR" and r:
                        lows(r)

                def out(m, r, i, u, g):
                    if m % 2 == 0:
                        split_unit(pool, u + AHEAD, i, 16)
                    if r:
                        tail_pool_(pool, n + 1, m)

                walk(pool, proj, attend, out)

            return {"pe": pe_, "dve": dve_, "act": act_, "pool": pool_}
        makers = {"mla": mla, "hgrn": hgrn, "s5": s5, "ret": ret}
        mixer = {n: makers[kind](n, u0, g0) for n, (kind, name, u0, g0) in enumerate(at) if kind != "ffn"}

        block = ctx.enter_context(nc.Block())

        @block.sync
        def _(sp):
            for name, t in (("ones", ones), ("ident", ident), ("gains", gains)):
                sp.dma_start(t[:], a[name]).then_inc(consts, 16)
            sp.dma_start(h[:], a["h0"].rearrange("(m p) t -> p m t", p=P)).then_inc(consts, 16)
            for u in range(RING):
                load_unit(sp, u)
            laps = n_units // RING
            with sp.Fori(1, laps) as i:
                for s in range(RING):
                    load_unit(sp, s, i, RING)
            for u in range(laps * RING, n_units):
                load_unit(sp, u)
            kind, name, u0, g0 = at[-1]
            for m in range(DT):
                sp.wait_ge(tile_free, g0 + LAST_TILES[kind] + m + 1)
                if kind != "ffn" or DEBUG:
                    sp.wait_ge(tail_pool.sem, tail_pool.done("lo", 8 * len(at) + m))
                sp.dma_start(a["out"][m * P:(m + 1) * P], h[:, m, META if a["out"].shape[1] == SEQ else 0:]).then_inc(out_written, 16)
            sp.wait_ge(out_written, 16 * DT)

        @block.tensor
        def _(pe):
            for n, (kind, name, u0, g0) in enumerate(at):
                if kind == "ffn":
                    ffn_pe(pe, n, int(name[3]) - layer0, u0, g0)
                else:
                    mixer[n]["pe"](pe)

        @block.vector
        def _(dve):
            dve.sem_inc(tile_free, 4)
            dve.memset(sqsum[:], 0.0).then_inc(sum_cleared, 1)
            dve.memset(ub[:, :, 0:2], 0.0).then_inc(pads, 1)
            dve.wait_ge(consts, CONSTS)
            for m in range(DT):
                tail_dve_(dve, 0, m)
            for n, (kind, name, u0, g0) in enumerate(at):
                last = n == len(at) - 1 and not DEBUG
                if kind == "ffn":
                    ffn_dve(dve, n, int(name[3]) - layer0, u0, g0, last)
                else:
                    mixer[n]["dve"](dve)

        @block.scalar
        def _(act):
            act.dma_start(convp[:], a["convp"][layer0]).then_inc(convp_landed, 16)
            for u in range(AHEAD):
                round_unit(act, u)
            act.wait_ge(consts, CONSTS)
            for m in range(DT):
                tail_act_(act, 0, m)
            seen = 0
            for n, (kind, name, u0, g0) in enumerate(at):
                last = n == len(at) - 1 and not DEBUG
                if kind == "ffn":
                    ffn_act(act, n, int(name[3]) - layer0, u0, g0, last)
                    seen += 1
                    if not last and n + 1 < len(at):
                        act.dma_start(convp[:], a["convp"][int(name[3]) + 1]).then_inc(convp_landed, 16)
                else:
                    mixer[n]["act"](act)

        @block.gpsimd
        def _(pool):
            pool.sem_inc(up_pool.sem, 1)
            for u in range(AHEAD):
                split_unit(pool, u)
            for m in range(DT):
                tail_pool_(pool, 0, m)
            for n, (kind, name, u0, g0) in enumerate(at):
                last = n == len(at) - 1 and not DEBUG
                if kind == "ffn":
                    ffn_pool(pool, n, int(name[3]) - layer0, u0, g0, last)
                else:
                    mixer[n]["pool"](pool)

def _mla_units(z):
    import numpy as np
    down = np.asarray(z["mla_w_down"][0])
    k1, k2 = np.split(down[:, QL + KVL:], 2, 1)
    down = _blocks(np.concatenate([down[:, :QL + KVL], k1, k2, k2, k1], 1))
    out = [_unit(b) for b in down]
    uq = np.asarray(z["mla_w_uq"][0]).reshape(QL, HEADS, QK)
    ukv = np.asarray(z["mla_w_ukv"][0]).reshape(KVL, HEADS, NOPE + VDIM)
    for h in range(HEADS):
        q1, q2 = np.split(uq[:, h, NOPE:], 2, 1)
        q = _blocks(np.concatenate([uq[:, h, :NOPE], q1, q2, q2, q1], 1))
        out.append(_unit(list(q[0]) + list(q[1])))
        kv = _blocks(ukv[:, h])
        out.append(_unit(list(kv[0]) + list(kv[1])))
    return out + [_unit(b) for b in _blocks(z["mla_w_o"][0])]


def _rope(dim):
    import numpy as np
    inv = (1.0 / (np.float32(10000.0) ** (np.arange(0, dim, 2, dtype=np.float32) / np.float32(dim)))).astype(np.float32)
    ang = inv[:, None] * np.arange(T, dtype=np.float32)[None]
    return np.cos(ang.astype(np.float64)), np.sin(ang.astype(np.float64))


def _mla_arrays(z):
    import numpy as np
    c, s = _rope(ROPE)

    def head(g):
        g1, g2 = np.split(np.asarray(g)[NOPE:], 2)
        return [np.asarray(g)[:NOPE], np.concatenate([g1, g2, g2, g1])]

    cols = [_cols(z["mla_cq_norm_g"][0]), _cols(z["mla_ckv_norm_g"][0])]
    cols += [v[:, None] for v in head(z["mla_q_head_g"][0]) + head(z["mla_k_head_g"][0])]
    return {"mla_tab": np.concatenate([c, c, -s, s]), "mla_par": np.concatenate(cols, 1)}


def _hgrn_units(z):
    import numpy as np
    q, f, i, g = (_blocks(w) for w in np.split(np.asarray(z["hgrn_w_in"][0]), 4, 1))
    out = []
    for h in range(HEADS):
        out += [_unit(f[h]), _unit(q[h]), _unit(i[h]), _unit(g[h])]
    return out + [_unit(b) for b in _blocks(z["hgrn_w_o"][0])]


def _hgrn_arrays(z):
    import numpy as np
    j, i = np.arange(P)[:, None], np.arange(P)[None]
    masks = [(j // 16 == i // 16) & (j <= i)]
    for w in (16, 32, 64):
        masks.append((j // (2 * w) == i // (2 * w)) & (j // w + 1 == i // w))
    scan = np.broadcast_to((np.arange(T) % 16 != 0)[None], (P, T))
    logits = np.asarray(z["hgrn_lb_logits"]).reshape(DEPTH, HEADS, P).transpose(2, 0, 1).reshape(P, -1)
    par = np.concatenate([_cols(z["hgrn_o_norm_g"][0]), np.zeros((P, 3)), logits], 1)
    return {"hgrn_masks": np.concatenate(masks, 1), "hgrn_scan": scan, "hgrn_par": par}



def _s5_units(z):
    w = _blocks(z["s5_w_glu"][0])
    return [_unit(w[m + DT * x]) for m in range(DT) for x in range(2)]


def _s5_arrays(z):
    import numpy as np
    G, NPAIR, K = D // 16, D // 32, 16

    def states(v):
        v = np.asarray(v)
        v = v.reshape((NPAIR, 2) + v.shape[1:])
        return np.moveaxis(v, 0, 2).reshape((P, NPAIR) + v.shape[3:])

    def paired(v):
        v, out = states(v), np.zeros((P, NPAIR, 2, K), np.float32)
        for g in range(2):
            out[g * S5P:(g + 1) * S5P, :, g] = v[g * S5P:(g + 1) * S5P]
        return out.reshape(P, NPAIR, 2 * K)

    dt = np.broadcast_to(np.asarray(z["s5_log_dt"][0])[:, None], (G, S5P))
    lam = np.concatenate([states(v) for v in (z["s5_lam_re"][0], z["s5_lam_im"][0], dt)], 1)
    b = np.concatenate([paired(z[k][0]).reshape(P, -1) for k in ("s5_b_re", "s5_b_im")], 1)
    c = np.stack([paired(np.asarray(z[k][0]).transpose(0, 2, 1)) for k in ("s5_c_re", "s5_c_im")], 2)
    return {"s5_lam": lam, "s5_b": b, "s5_c": c.reshape(P, -1), "s5_d": _cols(z["s5_d"][0])}



def _ret_units(z):
    import numpy as np
    w = np.asarray(z["ret_w_in"][0])
    q, k, v, g = (_blocks(x) for x in np.split(w, [RH * RDK, 2 * RH * RDK, 2 * RH * RDK + RH * RDV], 1))
    wo = _blocks(z["ret_w_o"][0])
    proj = [[_unit(b) for b in list(q[2 * h:2 * h + 2]) + list(k[2 * h:2 * h + 2]) +
             list(v[4 * h:4 * h + 4]) + list(g[4 * h:4 * h + 4])] for h in range(RH)]
    outs = [[_unit(list(wo[m, 4 * h:4 * h + 4]) + list(wo[m + 1, 4 * h:4 * h + 4])) for m in range(0, DT, 2)]
            for h in range(RH)]
    out = proj[0]
    for h in range(RH):
        out = out + (proj[h + 1] if h + 1 < RH else []) + outs[h]
    return out


def _ret_arrays(z):
    import numpy as np
    c, s = _rope(RDK)
    t = np.arange(T, dtype=np.float64)
    tabs = []
    for h in range(RH):
        up = (1.0 - 2.0 ** (-5 - h)) ** t
        down = RDK ** -0.5 / up
        tabs.append(np.stack([c * up, s * up, c * down, s * down], 1))
    mask = np.arange(T)[None] >= np.arange(P)[:, None]
    return {"ret_tab": np.stack(tabs), "ret_mask": mask, "ret_gn": _cols(z["ret_gn_g"][0])}


HOST_UNITS = {"mla": _mla_units, "hgrn": _hgrn_units, "s5": _s5_units,
              "ret": _ret_units}
HOST_ARRAYS = {"mla": _mla_arrays, "hgrn": _hgrn_arrays, "s5": _s5_arrays,
               "ret": _ret_arrays}
DEBUG = False


def _blocks(w):
    import numpy as np
    K, M = w.shape
    return np.asarray(w).reshape(K // P, P, M // P, P).transpose(2, 0, 1, 3)


def _unit(blocks):
    import numpy as np
    u = np.zeros((P, BLK * P), np.float32)
    for k, b in enumerate(blocks):
        u[:, k * P:(k + 1) * P] = b
    return u


def _cols(v):
    import numpy as np
    return np.ascontiguousarray(np.asarray(v).reshape(-1, P).T)


def _stream(stages, z):
    out = []
    for s in stages:
        kind = "ffn" if s[:3] == "ffn" else s
        if kind == "ffn":
            n = int(s[3])
            up, down = _blocks(z["ffn_w_up"][n]), _blocks(z["ffn_w_down"][n])
            for k in range(KT):
                out += [_unit(up[k]), _unit(up[KT + k])]
            for m in range(DT):
                k0 = 0
                for nb in DOWN:
                    out.append(_unit(down[m][k0:k0 + nb]))
                    k0 += nb
        else:
            out += HOST_UNITS[kind](z)
    return out


def arrays(z, stages, h0):
    import numpy as np
    f = lambda v: np.ascontiguousarray(v, dtype=np.float32)
    r = {"stream": f(np.stack(_stream(stages, z))), "h0": f(h0),
         "ones": f(np.ones((P, P))), "ident": f(np.eye(P))}
    g = [_cols(np.asarray(z[k])[n]) for n in range(DEPTH) for k in ("norm_mix_g", "norm_ffn_g")]
    r["gains"] = f(np.stack(g, 1))
    cw, cb = np.asarray(z["ffn_conv_w"]), np.asarray(z["ffn_conv_b"])
    cp = np.stack([cw[:, 0], cw[:, 1], cw[:, 2], cb], -1)
    cp = cp.reshape(DEPTH, 2, KT, P, 4).transpose(0, 3, 2, 1, 4).reshape(DEPTH, P, 2 * KT, 4)
    r["convp"] = f(cp)
    for s in stages:
        kind = "ffn" if s[:3] == "ffn" else s
        if kind != "ffn":
            r.update({k: f(v) for k, v in HOST_ARRAYS[kind](z).items()})
    return r


def kernel(**inputs):
    import numpy as _np
    import concourse.bacc as _bacc
    from concourse import mybir as _mybir
    from concourse.bass_utils import run_bass_kernel_spmd as _run

    z = {k: _np.asarray(v) for k, v in inputs.items()}
    h0 = _np.concatenate([z["meta_tokens"], z["x"][0]], 0).T
    given = arrays(z, SUBLAYERS, h0)
    nc = _bacc.Bacc("TRN2", target_bir_lowering=False, num_devices=1)
    a = {k: nc.dram_tensor("in_" + k, v.shape, _mybir.dt.from_np(v.dtype), kind="ExternalInput").ap()
         for k, v in given.items()}
    a["out"] = nc.dram_tensor("out_0", (D, SEQ), F32, kind="ExternalOutput").ap()
    trunk(nc, a, SUBLAYERS)
    r = _run(nc, [{"in_" + k: v for k, v in given.items()}], core_ids=[0])
    return _np.ascontiguousarray(r.results[0]["out_0"].T)[None]
```

```python
from contextlib import ExitStack

import concourse.bass as bass
from concourse import mybir

F32 = mybir.dt.float32
F32R = mybir.dt.float32r
ALU = mybir.AluOpType
ACT = mybir.ActivationFunctionType
AX = mybir.AxisListType

P = 128
D = 1024
DT = D // P
SEQ, META = 512, 16
T = SEQ + META
HALF = T // 2
DEPTH = 4
EPS = 1e-6
NEG = -1e30
BLK = 8
RING = 4
AHEAD = 3
QB = SEQ // P

QUARTER = T // 4
SUMS = 848
NEWTON = ["bits", "y0", "a0", "b0", "y1", "a1", "b1", "y2", "a2", "b2"]
RSQRT = ["mean"] + NEWTON + [("q", 0, q) for q in range(4)]
LAST = ("q", 0, 3)

HEADS = 8
NOPE, ROPE, VDIM = 128, 64, 128
QK = NOPE + ROPE
QL, KVL = 384, 256

FFN = 2816
KT = FFN // P
DOWN = (8, 7, 7)

RH, RDK, RDV = 4, 256, 512
S5P = 64

SUBLAYERS = ["mla", "ffn0", "hgrn", "ffn1", "s5", "ffn2", "ret", "ffn3"]
MLA_TILES = 6 + 2 + 7 + 22 * 7 + 15 + DT
HGRN_TILES = 16 * HEADS + DT
S5_TILES = 2 + 2 + 6 * 8 + 4 + 2 * DT
RET_TILES = 12 + 3 * (24 + DT) + 12 + DT
LAST_TILES = {"ffn": 1 + 2 * KT, "mla": 1 + MLA_TILES - DT, "hgrn": 1 + HGRN_TILES - DT, "s5": S5_TILES - DT, "ret": 1 + RET_TILES - DT}
CONSTS = 48


class Order:

    def __init__(self, sem, names, start=0):
        self.sem, self.names, self.start = sem, list(names), start
        self.index = {n: k for k, n in enumerate(self.names)}
        assert len(self.index) == len(self.names)
        self.at = 0

    def one(self, name):
        assert self.names[self.at] == name, (self.names[self.at], name)
        self.at = (self.at + 1) % len(self.names)
        return 1

    def step(self, name):
        self.one(name)
        return self.sem

    def done(self, name, round_=0):
        return round_ * len(self.names) + (self.start + self.index[name] + 1)


def plan(stages):
    units = {"mla": 30, "hgrn": 40, "s5": 2 * DT, "ret": 16 * RH, "ffn": 2 * KT + 3 * DT}
    tiles = {"mla": MLA_TILES, "hgrn": HGRN_TILES, "s5": S5_TILES, "ret": RET_TILES, "ffn": 2 * KT + DT}
    at, u, g = [], 0, 4
    for s in stages:
        kind = "ffn" if s[:3] == "ffn" else s
        at.append((kind, s, u, g))
        u += units[kind]
        g += 1 + tiles[kind]
    return at, u


def trunk(nc, a, stages):
    at, n_units = plan(stages)
    n_units += 4 * DEBUG
    first = SUBLAYERS.index(stages[0])

    layer0 = min(int(s[3]) for s in stages if s[:3] == "ffn") if any(s[:3] == "ffn" for s in stages) else 0
    ctx = ExitStack()
    with ctx:
        def sem(name):
            return ctx.enter_context(nc.semaphore(name))

        place = [nc.sbuf_base + (-nc.sbuf_base) % 32]

        def sb(name, shape, dt=F32, at=None):
            size = 4
            for n in shape[1:]:
                size *= n
            size += -size % 32
            if at is None:
                at = place[0]
                place[0] += size
            return nc.alloc_sbuf_tensor_at(name, shape, dt, offset=at)

        h = sb("h", [P, DT, T])
        xs_at = place[0]
        xs = sb("xs", [P, DT, 2, T], F32R)
        hid_at = place[0]
        hid = sb("hid", [P, KT, 2, T], F32R)
        raw = sb("raw", [P, RING, BLK * P])
        wr = sb("wr", [P, RING, 2, BLK, P], F32R)
        rstd = sb("rstd", [P, T])
        sqsum = sb("sqsum", [P, T])
        scr = sb("scr", [P, 4, T])
        ub = sb("ub", [P, 2, T + 2])
        pick = sb("pick", [P, P])
        ones = sb("ones", [P, P])
        ident = sb("ident", [P, P])
        gains = sb("gains", [P, 2 * DEPTH, DT])
        convp = sb("convp", [P, 2 * KT, 4])
        work_at = hid_at + 8 * 2 * T * 4
        NW = (KT - 8) * 2
        work = sb("work", [P, NW, T], at=work_at)
        work2 = sb("work2", [P, 2 * DT * T], at=xs_at)
        spare = sb("spare", [P, 2 * DT * T], at=hid_at)
        assert place[0] <= nc.sbuf_usable_end, place[0]
        ps = ctx.enter_context(nc.psum_tensor("ps", [P, 4, 2, 512], F32))

        raw_landed = [sem(f"raw_landed{s}") for s in range(RING)]
        hi_ready = sem("hi_ready")
        lo_ready = sem("lo_ready")
        unit_done = sem("unit_done")
        tile_free = sem("tile_free")
        consts = sem("consts")
        gains_in = sem("gains_in")
        h_in = [sem(f"h_in{m}") for m in range(DT)]
        convp_landed = sem("convp_landed")
        norm_pe_done = Order(sem("norm_pe"), ["sums", "spread"])
        norm_dve_done = Order(sem("norm_dve"), ["clear"] + [("n", s) for s in RSQRT])
        sum_cleared = sem("sum_cleared")
        tail_dve = Order(sem("tail_dve"), ["scaled", "summed"])
        tail_act = Order(sem("tail_act"), ["hi", "square"])
        tail_pool = Order(sem("tail_pool"), ["lo"])
        up_dve = Order(sem("up_dve"), [n for j in range(2) for n in
                                       [(n, j, s) for s in range(2) for n in ("tap0", "tap1", "conv")] + [("hidden", j)]])
        up_act = Order(sem("up_act"), [(n, j) for j in range(2) for n in ("silu", "hi")])
        up_pool = Order(sem("up_pool"), [("lo", j) for j in range(2)], start=1)
        pads = sem("pads")
        out_written = sem("out_written")
        def tile(g):
            return ps[:, g % 4, :, 0:HALF]

        def flat(g):
            return ps[:, g % 4].rearrange("p a b -> p (a b)")

        def halves(x):
            return x.rearrange("p (a b) -> p a b", a=2)

        def load_unit(sp, u0, i=0, per=0):
            if u0 >= RING or per:
                sp.wait_ge(lo_ready, u0 + i * per - RING + 1)
            sp.dma_start(raw[:, u0 % RING, :], a["stream"][bass.ds(u0 + i * per, 1)].rearrange("a p n -> p (a n)"))\
              .then_inc(raw_landed[u0 % RING], 16)

        def round_unit(act, u0, i=0, per=0):
            if u0 >= n_units and not per:
                return
            s = u0 % RING
            act.wait_ge(raw_landed[s], (i * (per // RING) + (u0 // RING + 1)) * 16)
            if u0 >= RING or per:
                act.wait_ge(unit_done, u0 + i * per - RING + 1)
            act.activation(wr[:, s, 0].rearrange("p a b -> p (a b)"), raw[:, s, :], ACT.Copy).then_inc(hi_ready, 1)

        def split_unit(pool, u0, i=0, per=0):
            if u0 >= n_units and not per:
                return
            s = u0 % RING
            pool.wait_ge(hi_ready, u0 + i * per + 1)
            pool.tensor_tensor(wr[:, s, 1].rearrange("p a b -> p (a b)"), raw[:, s, :],
                               wr[:, s, 0].rearrange("p a b -> p (a b)").bitcast(F32), ALU.subtract).then_inc(lo_ready, 1)

        def project(pe, out, slot, b0, x, start, stop, inc=None, before={}):
            n = len(x)
            for k in range(n):
                if k in before:
                    pe.wait_ge(*before[k])
                for p, (w, v) in enumerate(((0, 0), (0, 1), (1, 0))):
                    for q in range(2):
                        mm = pe.matmul(out[:, q], wr[:, slot, w, b0 + k], x[k][v][:, q * HALF:(q + 1) * HALF],
                                       start=start and k == 0 and p == 0, stop=stop and k == n - 1 and p == 2)
            if inc is not None:
                mm.then_inc(inc, 1)

        def split_tiles(t, ks):
            return [(t[:, k, 0], t[:, k, 1]) for k in ks]

        def sums_pe(pe, g, col, srcs):
            for q in range(4):
                for j, (src, rows) in enumerate(srcs):
                    mm = pe.matmul(flat(g)[32 * q:32 * q + 32, col:col + QUARTER], ones[0:rows, 0:32],
                                   src[0:rows, q * QUARTER:(q + 1) * QUARTER],
                                   start=j == 0, stop=j == len(srcs) - 1, tile_position=(0, 32 * q))
            return mm

        def spread_pe(pe, g, quarters):
            for q in range(2):
                mm = pe.matmul(tile(g)[:, q], pick[:], quarters[:, q * HALF:(q + 1) * HALF], start=True, stop=True)
            return mm

        def mean_rsqrt(dve, g, cols, width, quarters, scratch, o, pre, r=0, free=None):
            n = len(cols) * QUARTER
            x, t, y = (scratch[:, k * n:(k + 1) * n] for k in range(3))

            def one(name, ins, wait=True):
                ins.then_inc(o.sem, o.one((pre, name)))
                if wait:
                    dve.wait_ge(o.sem, o.done((pre, name), r))
            for k, c in enumerate(cols):
                ins = dve.tensor_scalar(x[:, k * QUARTER:(k + 1) * QUARTER], flat(g)[:, c:c + QUARTER], 1.0 / width, EPS,
                                        ALU.mult, ALU.add)
                if k < len(cols) - 1:
                    one(f"mean{k}", ins, False)
            if free is not None:
                ins.then_inc(tile_free, 1)
                dve.wait_ge(tile_free, free)
            else:
                one("mean", ins)
            one("bits", dve.tensor_copy(y, x.bitcast(mybir.dt.int32)))
            one("y0", dve.tensor_scalar(y.bitcast(mybir.dt.int32), y, -0.5, 1597463007.0, ALU.mult, ALU.add))
            for k in range(3):
                one(f"a{k}", dve.scalar_tensor_tensor(t, y, -0.5, y, ALU.mult, ALU.mult))
                one(f"b{k}", dve.tensor_tensor(t, t, x, ALU.mult))
                if k < 2:
                    one(f"y{k + 1}", dve.scalar_tensor_tensor(y, t, 1.5, y, ALU.add, ALU.mult))
            for k, dst in enumerate(quarters):
                for q in range(4):
                    rows, c = slice(32 * q, 32 * q + 32), slice(k * QUARTER, (k + 1) * QUARTER)
                    one(("q", k, q), dve.scalar_tensor_tensor(dst[rows, q * QUARTER:(q + 1) * QUARTER], t[rows, c], 1.5,
                                                              y[rows, c], ALU.add, ALU.mult), False)

        def norm_sum_pe(pe, n, g):
            pe.wait_ge(tail_dve.sem, tail_dve.done("summed", 8 * n + 7))
            pe.wait_ge(tile_free, g - 3)
            if n == 0:
                pe.wait_ge(consts, CONSTS)
            sums_pe(pe, g, SUMS, [(sqsum[:], P)]).then_inc(norm_pe_done.sem, norm_pe_done.one("sums"))

        def norm_spread_pe(pe, n, g):
            pe.wait_ge(norm_dve_done.sem, norm_dve_done.done(("n", LAST), n))
            spread_pe(pe, g, rstd).then_inc(norm_pe_done.sem, norm_pe_done.one("spread"))

        def first_tiles_pe(pe, n, u0, g):
            for t in range(2):
                pe.wait_ge(lo_ready, u0 + t + 1)
                pe.wait_ge(tile_free, g + t - 2)
                project(pe, tile(g + 1 + t), (u0 + t) % RING, 0, split_tiles(xs, range(DT)), True, True, unit_done,
                        before={k: (tail_pool.sem, tail_pool.done("lo", 8 * n + k)) for k in range(DT) if t == 0})
                (norm_sum_pe if t == 0 else norm_spread_pe)(pe, n, g)

        def norm_dve(dve, n, g):
            dve.memset(rstd[:], 0.0).then_inc(norm_dve_done.sem, norm_dve_done.one("clear"))
            dve.wait_ge(norm_pe_done.sem, norm_pe_done.done("sums", n))
            dve.wait_ge(norm_dve_done.sem, norm_dve_done.done("clear", n))
            mean_rsqrt(dve, g, [SUMS], D, [rstd], ub[:, 1, 2:], norm_dve_done, "n", n)
            dve.memset(sqsum[:], 0.0).then_inc(sum_cleared, 1)
            dve.wait_ge(norm_pe_done.sem, norm_pe_done.done("spread", n))
            dve.tensor_copy(halves(rstd[:]), tile(g)).then_inc(tile_free, 1)
            dve.wait_ge(tile_free, g + 1)

        def tail_dve_(dve, n, m, i=0):
            r = 8 * n + m
            if r >= 2:
                dve.wait_ge(tail_pool.sem, tail_pool.done("lo", r - 2 + 4 * i))
            dve.tensor_scalar(scr[:, m % 2], h[:, m + 4 * i], gains[:, first + n, bass.ds(m + 4 * i, 1)], None, ALU.mult)\
               .then_inc(tail_dve.sem, tail_dve.one("scaled"))
            dve.wait_ge(tail_act.sem, tail_act.done("square", r + 4 * i))
            dve.wait_ge(tail_dve.sem, tail_dve.done("scaled", r + 4 * i))
            dve.wait_ge(sum_cleared, n + 1)
            dve.tensor_tensor(sqsum[:], sqsum[:], scr[:, 2 + m % 2], ALU.add)\
               .then_inc(tail_dve.sem, tail_dve.one("summed"))

        def tail_act_(act, n, m, i=0):
            r = 8 * n + m
            act.wait_ge(tail_dve.sem, tail_dve.done("scaled", r + 4 * i))
            act.activation(xs[:, m + 4 * i, 0], scr[:, m % 2], ACT.Copy).then_inc(tail_act.sem, tail_act.one("hi"))
            act.activation(scr[:, 2 + m % 2], h[:, m + 4 * i], ACT.Square).then_inc(tail_act.sem, tail_act.one("square"))

        def tail_pool_(pool, n, m, i=0):
            r = 8 * n + m
            pool.wait_ge(tail_act.sem, tail_act.done("hi", r + 4 * i))
            pool.tensor_tensor(xs[:, m + 4 * i, 1], scr[:, m % 2], xs[:, m + 4 * i, 0].bitcast(F32), ALU.subtract)\
                .then_inc(tail_pool.sem, tail_pool.one("lo"))

        def last_stage_over(eng, n):
            eng.wait_ge(tail_dve.sem, tail_dve.done("summed", 8 * n + 7))
            eng.wait_ge(tail_pool.sem, tail_pool.done("lo", 8 * n + 7))

        def out_pe(pe, u0, g0, x):
            for m in range(DT):
                pe.wait_ge(lo_ready, u0 + m + 1)
                pe.wait_ge(tile_free, g0 + m - 3)
                project(pe, tile(g0 + m), (u0 + m) % RING, 0, x, True, True, unit_done)

        def out_dve(dve, n, u0, g0):
            for m in range(DT):
                dve.wait_ge(unit_done, u0 + m + 1)
                dve.tensor_tensor(halves(h[:, m]), tile(g0 + m), halves(h[:, m]), ALU.add).then_inc(tile_free, 1)
                dve.wait_ge(tile_free, g0 + m + 1)
                tail_dve_(dve, n, m)

        def out_act(act, n, u0):
            for m in range(DT):
                round_unit(act, u0 + m + AHEAD)
                tail_act_(act, n, m)

        def out_pool(pool, n, u0):
            for m in range(DT):
                split_unit(pool, u0 + m + AHEAD)
                tail_pool_(pool, n, m)

        def setup_of(n):
            return mixer[n].get("setup") if n in mixer else None

        def ffn_pe(pe, n, layer, u0, g0):
            x = split_tiles(xs, range(DT))
            ug, gg = u0, g0 + 1

            def up(s, i):
                pe.wait_ge(lo_ready, ug + s + 1 + i * 4)
                pe.wait_ge(tile_free, gg + s - 3 + i * 4)
                project(pe, tile(gg + s), (ug + s) % RING, 0, x, True, True, unit_done)
            first_tiles_pe(pe, n, u0, g0)
            for s in range(2, 4):
                up(s, 0)
            with pe.Fori(1, KT // 2) as i:
                for s in range(4):
                    up(s, i)
            ug, gg = u0 + 2 * KT, gg + 2 * KT
            end = (layer + 1) * (KT // 2) - 1
            pe.wait_ge(up_pool.sem, up_pool.done(("lo", 1), end - 1))
            late = {KT - 2 + j: (up_pool.sem, up_pool.done(("lo", j), end)) for j in range(2)}
            with pe.Fori(0, DT // 4) as i:
                for m in range(4):
                    pe.wait_ge(tile_free, gg + m - 3 + i * 4)
                    k0 = 0
                    for j, nb in enumerate(DOWN):
                        u = ug + 3 * m + j
                        pe.wait_ge(lo_ready, u + 1 + i * 12)
                        project(pe, tile(gg + m), u % RING, 0, split_tiles(hid, range(k0, k0 + nb)),
                                j == 0, j == 2, unit_done, {k - k0: w for k, w in late.items()})
                        k0 += nb

        def ffn_dve(dve, n, layer, u0, g0, last):
            norm_dve(dve, n, g0)
            gg = g0 + 1
            R = layer * (KT // 2)
            dve.wait_ge(convp_landed, 16 * (layer + 1))
            dve.wait_ge(pads, 1)
            with dve.Fori(0, KT // 2) as i:
                for j in range(2):
                    for s in range(2):
                        q = 2 * j + s
                        cp = lambda c, q=q: convp[:, bass.ds(q + 4 * i, 1), c]
                        dve.wait_ge(unit_done, u0 + q + 1 + i * 4)
                        dve.tensor_tensor(halves(ub[:, s, 2:]), tile(gg + q), halves(rstd[:]), ALU.mult)\
                           .then_inc(tile_free, 1)
                        dve.wait_ge(tile_free, gg + q + 1 + i * 4)
                        dve.tensor_scalar(scr[:, s], ub[:, s, 2:], cp(2), cp(3), ALU.mult, ALU.add)\
                           .then_inc(up_dve.sem, up_dve.one(("tap0", j, s)))
                        dve.wait_ge(up_dve.sem, up_dve.done(("tap0", j, s), R + i))
                        dve.scalar_tensor_tensor(scr[:, s], ub[:, s, 1:T + 1], cp(1), scr[:, s], ALU.mult, ALU.add)\
                           .then_inc(up_dve.sem, up_dve.one(("tap1", j, s)))
                        dve.wait_ge(up_dve.sem, up_dve.done(("tap1", j, s), R + i))
                        dve.scalar_tensor_tensor(scr[:, s], ub[:, s, 0:T], cp(0), scr[:, s], ALU.mult, ALU.add)\
                           .then_inc(up_dve.sem, up_dve.one(("conv", j, s)))
                    dve.wait_ge(up_dve.sem, up_dve.done(("conv", j, 1), R + i))
                    dve.wait_ge(up_act.sem, up_act.done(("silu", j), R + i))
                    dve.wait_ge(up_pool.sem, up_pool.done(("lo", j), R + i) - 1)
                    dve.tensor_tensor(scr[:, 3], scr[:, 2], scr[:, 1], ALU.mult)\
                       .then_inc(up_dve.sem, up_dve.one(("hidden", j)))
            ug, gg = u0 + 2 * KT, gg + 2 * KT
            setup = setup_of(n + 1)
            if setup:
                setup[2](dve)
            dve.wait_ge(up_pool.sem, up_pool.done(("lo", 1), R + KT // 2 - 1))
            with dve.Fori(0, DT // 4) as i:
                for m in range(4):
                    dve.wait_ge(unit_done, ug + 3 * m + 3 + i * 12)
                    hm = h[:, m + 4 * i].rearrange("p (a b) -> p a b", a=2)
                    dve.tensor_tensor(hm, tile(gg + m), hm, ALU.add).then_inc(tile_free, 1)
                    if not last:
                        dve.wait_ge(tile_free, gg + m + 1 + i * 4)
                        tail_dve_(dve, n + 1, m, i)

        def ffn_act(act, n, layer, u0, g0, last):
            R = layer * (KT // 2)
            with act.Fori(0, KT // 2) as i:
                for s in range(4):
                    round_unit(act, u0 + AHEAD + s, i, 4)
                    j = s // 2
                    if s % 2 == 0:
                        act.wait_ge(up_dve.sem, up_dve.done(("conv", j, 0), R + i))
                        act.activation(scr[:, 2], scr[:, 0], ACT.Silu).then_inc(up_act.sem, up_act.one(("silu", j)))
                    else:
                        act.wait_ge(up_dve.sem, up_dve.done(("hidden", j), R + i))
                        act.activation(hid[:, bass.ds(i * 2 + j, 1), 0], scr[:, 3], ACT.Copy)\
                           .then_inc(up_act.sem, up_act.one(("hi", j)))
            ug = u0 + 2 * KT
            setup = setup_of(n + 1)
            if setup:
                setup[0](act)
                setup[1](act)
            if last:
                for u in range(ug + AHEAD, n_units):
                    round_unit(act, u)
                return
            with act.Fori(0, DT // 4) as i:
                for m in range(4):
                    for j in range(3):
                        round_unit(act, ug + AHEAD + 3 * m + j, i, 12)
                    tail_act_(act, n + 1, m, i)

        def ffn_pool(pool, n, layer, u0, g0, last):
            R = layer * (KT // 2)
            with pool.Fori(0, KT // 2) as i:
                for s in range(4):
                    split_unit(pool, u0 + AHEAD + s, i, 4)
                    j = s // 2
                    if s % 2 == 1:
                        pool.wait_ge(up_act.sem, up_act.done(("hi", j), R + i))
                        lo = hid[:, bass.ds(i * 2 + j, 1), 1].rearrange("p a b -> p (a b)")
                        hi = hid[:, bass.ds(i * 2 + j, 1), 0].rearrange("p a b -> p (a b)")
                        pool.tensor_tensor(lo, scr[:, 3], hi.bitcast(F32), ALU.subtract)\
                            .then_inc(up_pool.sem, up_pool.one(("lo", j)))
            ug = u0 + 2 * KT
            if last:
                for u in range(ug + AHEAD, n_units):
                    split_unit(pool, u)
                return
            with pool.Fori(0, DT // 4) as i:
                for m in range(4):
                    for j in range(3):
                        split_unit(pool, ug + AHEAD + 3 * m + j, i, 12)
                    tail_pool_(pool, n + 1, m, i)

        def mla(n, u0, g0):
            if "mla" not in stages:
                return {}
            SCALE = QK ** -0.5
            parity = lambda k: [work[:, 10 * j + k] for j in range(2)]
            qn, qr, kn, kr = (parity(k) for k in range(4))
            vt = [work[:, 10 * j + 4:10 * j + 6].rearrange("p a b -> p (a b)") for j in range(2)]
            krot, sqkr, tab, misc = (work[:, k] for k in (6, 7, 8, 9))
            par, stat = misc[:, 0:16], misc[:, 16:96]
            sqn, sqr, rg, rt, vfm = (work[:, k] for k in range(20, 25))
            sqk = work[:, 17]
            fac = work[:, 16]
            scratch = work[:, 18:20].rearrange("p a b -> p (a b)")
            quarters = [work2[:, (10 + k) * T:(11 + k) * T] for k in range(2)]
            prob = [work[:, 26 + k] for k in range(2)]
            pt = [scr[:, 2 * k:2 * k + 2].rearrange("p a b -> p (a b)") for k in range(2)]
            lat = [work[:, 20 + k] for k in range(6)]
            lsq = [work[:, 10 + k] for k in range(5)]
            lquarters = [work[:, 15], work[:, 17]]
            groups = ((0, 3, QL), (3, 5, KVL))
            SUM_Q, SUM_K = 512 + P, 512 + P + QUARTER
            G_Q, G_QR, G_K, G_KR = 5, 6, 7, 8

            P_SEQ = ["qn", "qr", "kn", "vv", "sum", "spreadq", "spreadk"]
            A_SEQ = [("S", 0), ("S", 1), ("T", 0), ("S", 2), ("O", 0), ("T", 1), ("S", 3), ("T", 2), ("S", 4),
                     ("O", 1), ("T", 3), ("O", 2), ("T", 4), ("O", 3), ("O", 4)]
            X_SEQ = [("S", 0), ("S", 1), "qn", ("T", 0), ("S", 2), "qr", ("O", 0), "kn", ("T", 1), ("S", 3),
                     "vv", ("T", 2), ("S", 4), ("O", 1), "sum", ("T", 3), ("O", 2), ("T", 4), "spreadq",
                     "spreadk", ("O", 3), ("O", 4)]
            gP = g0 + 1 + 6 + 2
            gX = gP + len(P_SEQ)
            uH = u0 + 6
            uO = uH + 2 * HEADS
            gO = gX + len(X_SEQ) * (HEADS - 1) + len(A_SEQ)
            assert gO + DT == g0 + 1 + MLA_TILES

            consts_in = sem("mla_consts")
            l_dve = Order(sem("mla_l_dve"), ["clear0", "clear1"] + [(k, s) for k in range(2) for s in RSQRT] +
                          [("norm", t) for t in (0, 1, 3)] + ["gain", "up", "down", "turned", "clearq", "cleark"])
            l_act = Order(sem("mla_l_act"), [("square", t) for t in range(6)] + [("hi", t) for t in range(5)])
            l_pool = Order(sem("mla_l_pool"), [("lo", t) for t in range(5)])
            l_pe = Order(sem("mla_l_pe"), ["sum0", "sum1", "spread0", "spread1"])
            p_dve = Order(sem("mla_p_dve"), ["up", "down", "turned", "vt", "vtm"] +
                          [("f", s) for s in ["mean0"] + NEWTON + [("q", k, q) for k in range(2) for q in range(4)]] +
                          ["qr", "kn", "kr"])
            p_act = Order(sem("mla_p_act"), ["sqqn", "sqqr", "sqkn"])
            p_pe = Order(sem("mla_p_pe"), ["qn", "kn", "sum", "spreadq", "spreadk"])
            a_dve = Order(sem("mla_a_dve"), [x for k, b in A_SEQ for x in
                                             {"S": ([("mask", b)] if b < QB else []) + [("max", b), ("bias", b)],
                                              "T": [], "O": []}[k] + ([("prob", b)] if k == "S" else [])])
            a_act = Order(sem("mla_a_act"), [({"S": "exp", "T": "copy", "O": "hi"}[k], b) for k, b in A_SEQ
                                             if (k, b) != ("T", QB)])
            a_pe = Order(sem("mla_a_pe"), A_SEQ)

            def rows(b):
                return P if b < QB else META

            def keys(b):
                return META + P * (b + 1) if b < QB else META

            def walk(head, project, attend, at_):
                for k, s in enumerate(P_SEQ):
                    project(s, 0, 0, 0, gP + k)
                with at_.Fori(0, (HEADS - 2) // 2) as i:
                    for j in range(2):
                        for k, s in enumerate(X_SEQ):
                            g = gX + len(X_SEQ) * j + k
                            if isinstance(s, tuple):
                                attend(s, j, j, i, g)
                            else:
                                project(s, 1 - j, j + 1, i, g)
                for k, s in enumerate(X_SEQ):
                    g = gX + len(X_SEQ) * (HEADS - 2) + k
                    if isinstance(s, tuple):
                        attend(s, 0, HEADS - 2, 0, g)
                    else:
                        project(s, 1, HEADS - 1, 0, g)
                for k, s in enumerate(A_SEQ):
                    attend(s, 1, HEADS - 1, 0, gX + len(X_SEQ) * (HEADS - 1) + k)

            W2 = 2 * len(X_SEQ)

            def pe_(pe):
                first_tiles_pe(pe, n, u0, g0)
                for t in range(2, 6):
                    pe.wait_ge(lo_ready, u0 + t + 1)
                    pe.wait_ge(tile_free, g0 + 1 + t - 3)
                    project(pe, tile(g0 + 1 + t), (u0 + t) % RING, 0, split_tiles(xs, range(DT)), True, True, unit_done)
                for k, (a0, a1, _) in enumerate(groups):
                    g = g0 + 7 + k
                    pe.wait_ge(tile_free, g - 3)
                    pe.wait_ge(l_act.sem, l_act.done(("square", a1 - 1)))
                    sums_pe(pe, g, SUMS, [(lsq[t], P) for t in range(a0, a1)]).then_inc(l_pe.sem, l_pe.one(f"sum{k}"))
                for k in range(2):
                    pe.wait_ge(l_dve.sem, l_dve.done((k, LAST)))
                    spread_pe(pe, g0 + 7 + k, lquarters[k]).then_inc(l_pe.sem, l_pe.one(f"spread{k}"))
                pe.wait_ge(l_pool.sem, l_pool.done(("lo", 4)))
                cq, ckv = split_tiles(xs, range(3)), split_tiles(xs, range(3, 5))

                def proj(s, j, h0, i, g):
                    pe.wait_ge(tile_free, g - 3 + i * W2)
                    u = uH + 2 * h0
                    if s == "qn":
                        pe.wait_ge(lo_ready, u + 1 + i * 4)
                        project(pe, tile(g), u % RING, 0, cq, True, True, p_pe.step(s))
                    elif s == "qr":
                        project(pe, tile(g), u % RING, 3, cq, True, True, unit_done)
                    elif s == "kn":
                        pe.wait_ge(lo_ready, u + 2 + i * 4)
                        project(pe, tile(g), (u + 1) % RING, 0, ckv, True, True, p_pe.step(s))
                    elif s == "vv":
                        project(pe, tile(g), (u + 1) % RING, 2, ckv, True, True, unit_done)
                    elif s == "sum":
                        pe.wait_ge(tile_free, vv_at(g) + 1 + i * W2)
                        for b in range(QB):
                            pe.transpose(flat(g)[:, b * P:(b + 1) * P], vfm[:, META + b * P:META + (b + 1) * P], ident[:])
                        pe.transpose(flat(g)[0:META, 512:512 + P], vfm[:, 0:META], ident[:])
                        pe.wait_ge(p_act.sem, p_act.done("sqkn", h0) + i * 2 * len(p_act.names))
                        sums_pe(pe, g, SUM_Q, [(sqn, P), (sqr, ROPE)])
                        sums_pe(pe, g, SUM_K, [(sqk, P), (sqkr, ROPE)]).then_inc(p_pe.sem, p_pe.one("sum"))
                    else:
                        k = int(s == "spreadk")
                        pe.wait_ge(p_dve.sem, p_dve.done(("f", ("q", k, 3)), h0) + i * 2 * len(p_dve.names))
                        spread_pe(pe, g, quarters[k]).then_inc(p_pe.sem, p_pe.one(s))

                def attend(s, j, h0, i, g):
                    k, b = s
                    pe.wait_ge(tile_free, g - 3 + i * W2)
                    R, K = rows(b), keys(b)
                    q0 = META + b * P if b < QB else 0
                    if k == "S":
                        pe.wait_ge(p_dve.sem, p_dve.done("kr", h0) + i * 2 * len(p_dve.names))
                        for c0, c1 in ((0, min(K, 512)), (512, K)):
                            if c0 < c1:
                                pe.matmul(flat(g)[0:R, c0:c1], qn[j][:, q0:q0 + R], kn[j][:, c0:c1], start=True, stop=False)
                                mm = pe.matmul(flat(g)[0:R, c0:c1], qr[j][0:ROPE, q0:q0 + R], kr[j][0:ROPE, c0:c1],
                                               start=False, stop=True)
                    elif k == "T":
                        pe.wait_ge(a_dve.sem, a_dve.done(("prob", b), h0) + i * 2 * len(a_dve.names))
                        for t in range(b + 1 if b < QB else 0):
                            pe.transpose(flat(g)[:, t * P:t * P + R], prob[b % 2][0:R, META + t * P:META + (t + 1) * P],
                                         ident[0:R, 0:R])
                        if b < QB:
                            mm = pe.transpose(flat(g)[0:META, 512:512 + R], prob[b % 2][0:R, 0:META], ident[0:R, 0:R])
                        else:
                            mm = pe.matmul(flat(g)[:, 512:512 + R], prob[b % 2][0:R, 0:P], ident[0:R, 0:R],
                                           start=True, stop=True)
                    else:
                        pe.wait_ge(p_dve.sem, p_dve.done("vtm", h0) + i * 2 * len(p_dve.names))
                        pe.wait_ge(tile_free, t_at(g, b) + 1 + i * W2)
                        for t in range(b + 1 if b < QB else 0):
                            pe.matmul(flat(g)[:, 0:R], vt[j][:, t * P:(t + 1) * P], pt[b % 2][:, t * P:t * P + R],
                                      start=t == 0, stop=False)
                        mm = pe.matmul(flat(g)[:, 0:R], vt[j][0:META, 512:512 + P], pt[b % 2][0:META, 512:512 + R],
                                       start=b == QB, stop=True)
                    mm.then_inc(a_pe.sem, a_pe.one(s))

                walk(None, proj, attend, pe)
                pe.wait_ge(tile_free, gO)
                out_pe(pe, uO, gO, split_tiles(hid, range(HEADS)))

            def vv_at(g):
                if g < gX:
                    return g - (P_SEQ.index("sum") - P_SEQ.index("vv"))
                return g - (X_SEQ.index("sum") - X_SEQ.index("vv"))

            def t_at(g, b):
                seq = X_SEQ if g < gX + len(X_SEQ) * (HEADS - 1) else A_SEQ
                return g - (seq.index(("O", b)) - seq.index(("T", b)))

            def dve_(dve):
                norm_dve(dve, n, g0)
                for t in range(6):
                    g = g0 + 1 + t
                    dve.wait_ge(unit_done, u0 + t + 1)
                    dve.tensor_tensor(halves(lat[t]), tile(g), halves(rstd[:]), ALU.mult).then_inc(tile_free, 1)
                dve.wait_ge(consts_in, 32)
                for k in range(2):
                    dve.memset(lquarters[k], 0.0).then_inc(l_dve.sem, l_dve.one(f"clear{k}"))
                dve.wait_ge(l_dve.sem, l_dve.done("clear1"))
                for k, (a0, a1, width) in enumerate(groups):
                    dve.wait_ge(l_pe.sem, l_pe.done(f"sum{k}"))
                    mean_rsqrt(dve, g0 + 7 + k, [SUMS], width, [lquarters[k]], scratch, l_dve, k)
                for k, (a0, a1, width) in enumerate(groups):
                    dve.wait_ge(l_pe.sem, l_pe.done(f"spread{k}"))
                    for t in range(a0, a1):
                        ins = dve.scalar_tensor_tensor(halves(lat[t]), halves(lat[t]), par[:, t:t + 1], tile(g0 + 7 + k),
                                                       ALU.mult, ALU.mult)
                        if t < a1 - 1:
                            ins.then_inc(l_dve.sem, l_dve.one(("norm", t)))
                        else:
                            ins.then_inc(tile_free, 1)
                dve.wait_ge(l_act.sem, l_act.done(("square", 5)))
                dve.tensor_scalar(lat[5], lat[5], par[:, G_KR:G_KR + 1], None, ALU.mult).then_inc(l_dve.sem, l_dve.one("gain"))
                dve.wait_ge(l_dve.sem, l_dve.done("gain"))
                turn(dve, krot, lat[5], scr[:, 1], l_dve, 0)
                for k, name in enumerate(("clearq", "cleark")):
                    dve.memset(quarters[k], 0.0).then_inc(l_dve.sem, l_dve.one(name))
                dve.wait_ge(l_dve.sem, l_dve.done("cleark"))
                dve.wait_ge(l_pool.sem, l_pool.done(("lo", 4)))

                def proj(s, j, h0, i, g):
                    D2 = len(p_dve.names) * 2
                    if s == "qn" or s == "kn":
                        a_ = "sqqn" if s == "qn" else "sqkn"
                        col = G_Q if s == "qn" else G_K
                        dst = qn[j] if s == "qn" else kn[j]
                        dve.wait_ge(p_act.sem, p_act.done(a_, h0) + i * 2 * len(p_act.names))
                        dve.tensor_scalar(halves(dst), tile(g), par[:, col:col + 1], None, ALU.mult).then_inc(tile_free, 1)
                    elif s == "qr":
                        dve.wait_ge(p_act.sem, p_act.done("sqqr", h0) + i * 2 * len(p_act.names))
                        dve.tensor_scalar(halves(rg), tile(g), par[:, G_QR:G_QR + 1], None, ALU.mult).then_inc(tile_free, 1)
                        dve.wait_ge(tile_free, g + 1 + i * W2)
                        turn(dve, qr[j], rg, rt, p_dve, h0, i * D2)
                    elif s == "vv":
                        dve.wait_ge(unit_done, uH + 2 * h0 + 2 + i * 4)
                        dve.tensor_copy(halves(vfm), tile(g)).then_inc(tile_free, 1)
                    elif s == "sum":
                        dve.wait_ge(p_pe.sem, p_pe.done("sum", h0) + i * 2 * len(p_pe.names))
                        dve.tensor_copy(vt[j][:, 0:512], flat(g)[:, 0:512]).then_inc(p_dve.sem, p_dve.one("vt"))
                        dve.tensor_copy(vt[j][0:META, 512:512 + P], flat(g)[0:META, 512:512 + P])\
                           .then_inc(p_dve.sem, p_dve.one("vtm"))
                        mean_rsqrt(dve, g, [SUM_Q, SUM_K], QK, quarters, scratch, p_dve, "f", h0 + 2 * i,
                                   free=g + 1 + i * W2)
                    elif s == "spreadq":
                        dve.wait_ge(p_pe.sem, p_pe.done(s, h0) + i * 2 * len(p_pe.names))
                        dve.tensor_tensor(halves(qr[j])[0:ROPE], halves(qr[j])[0:ROPE], tile(g)[0:ROPE], ALU.mult)\
                           .then_inc(p_dve.sem, p_dve.one("qr"))
                        dve.tensor_tensor(halves(qn[j]), halves(qn[j]), tile(g), ALU.mult).then_inc(tile_free, 1)
                        dve.wait_ge(tile_free, g + 1 + i * W2)
                    else:
                        dve.wait_ge(p_pe.sem, p_pe.done(s, h0) + i * 2 * len(p_pe.names))
                        dve.tensor_copy(halves(fac), tile(g)).then_inc(tile_free, 1)
                        dve.wait_ge(tile_free, g + 1 + i * W2)
                        dve.tensor_tensor(kn[j], kn[j], fac, ALU.mult).then_inc(p_dve.sem, p_dve.one("kn"))
                        dve.tensor_tensor(kr[j][0:ROPE], krot[0:ROPE], fac[0:ROPE], ALU.mult)\
                           .then_inc(p_dve.sem, p_dve.one("kr"))
                        dve.wait_ge(p_dve.sem, p_dve.done("kr", h0) + i * D2)

                def attend(s, j, h0, i, g):
                    k, b = s
                    R, K = rows(b), keys(b)
                    A2 = 2 * len(a_dve.names)
                    if k == "S":
                        st = stat[0:R, 8 * b:8 * b + 4]
                        dve.wait_ge(a_pe.sem, a_pe.done(s, h0) + i * 2 * len(a_pe.names))
                        if b < QB:
                            dve.memset(flat(g)[0:64, K - 64:K], NEG).then_inc(a_dve.sem, a_dve.one(("mask", b)))
                            dve.wait_ge(a_dve.sem, a_dve.done(("mask", b), h0) + i * A2)
                        dve.reduce_max(st[:, 0:1], flat(g)[0:R, 0:K], AX.X).then_inc(a_dve.sem, a_dve.one(("max", b)))
                        dve.wait_ge(a_dve.sem, a_dve.done(("max", b), h0) + i * A2)
                        dve.tensor_scalar(st[:, 1:2], st[:, 0:1], -SCALE, None, ALU.mult)\
                           .then_inc(a_dve.sem, a_dve.one(("bias", b)))
                        dve.wait_ge(a_act.sem, a_act.done(("exp", b), h0) + i * 2 * len(a_act.names))
                        dve.reciprocal(st[:, 3:4], st[:, 2:3]).then_inc(tile_free, 1)
                        dve.wait_ge(tile_free, g + 1 + i * W2)
                        dve.tensor_scalar(prob[b % 2][0:R, 0:K], prob[b % 2][0:R, 0:K], st[:, 3:4], None, ALU.mult)\
                           .then_inc(a_dve.sem, a_dve.one(("prob", b)))
                    elif k == "T":
                        dve.wait_ge(a_pe.sem, a_pe.done(s, h0) + i * 2 * len(a_pe.names))
                        if b < QB:
                            dve.wait_ge(a_act.sem, a_act.done(("copy", b), h0) + i * 2 * len(a_act.names))
                        dve.tensor_copy(pt[b % 2][0:META, 512:512 + R], flat(g)[0:META, 512:512 + R]).then_inc(tile_free, 1)
                    else:
                        q0 = META + b * P if b < QB else 0
                        dve.wait_ge(a_act.sem, a_act.done(("hi", b), h0) + i * 2 * len(a_act.names))
                        hi = hid[:, bass.ds(h0 + 2 * i, 1), 0, q0:q0 + R].rearrange("p a b -> p (a b)")
                        lo = hid[:, bass.ds(h0 + 2 * i, 1), 1, q0:q0 + R].rearrange("p a b -> p (a b)")
                        dve.tensor_tensor(lo, flat(g)[:, 0:R], hi.bitcast(F32), ALU.subtract).then_inc(tile_free, 1)

                walk(None, proj, attend, dve)
                out_dve(dve, n + 1, uO, gO)

            def turn(dve, dst, src, tmp, o, r, off=0):
                dve.tensor_tensor(tmp[0:ROPE], src[ROPE:P], tab[ROPE:P], ALU.mult).then_inc(o.sem, o.one("up"))
                dve.tensor_tensor(dst[0:ROPE], src[0:ROPE], tab[0:ROPE], ALU.mult).then_inc(o.sem, o.one("down"))
                dve.wait_ge(o.sem, o.done("down", r) + off)
                dve.tensor_tensor(dst[0:ROPE], dst[0:ROPE], tmp[0:ROPE], ALU.add).then_inc(o.sem, o.one("turned"))
                dve.wait_ge(o.sem, o.done("turned", r) + off)

            def act_(act):
                act.dma_start(tab, a["mla_tab"]).then_inc(consts_in, 16)
                act.dma_start(par[:, 0:9], a["mla_par"]).then_inc(consts_in, 16)
                for t in range(6):
                    round_unit(act, u0 + t + AHEAD)
                    act.wait_ge(tile_free, g0 + 1 + t + 1)
                    if t < 5:
                        act.activation(lsq[t], lat[t], ACT.Square).then_inc(l_act.sem, l_act.one(("square", t)))
                    else:
                        act.activation(sqkr[0:ROPE], lat[t][0:ROPE], ACT.Square).then_inc(l_act.sem, l_act.one(("square", t)))
                for t in range(5):
                    if t in (2, 4):
                        act.wait_ge(tile_free, g0 + 8 + (t == 4))
                    else:
                        act.wait_ge(l_dve.sem, l_dve.done(("norm", t)))
                    act.activation(xs[:, t, 0], lat[t], ACT.Copy).then_inc(l_act.sem, l_act.one(("hi", t)))

                def proj(s, j, h0, i, g):
                    u = uH + 2 * h0
                    A2 = 2 * len(p_act.names)
                    if s == "qn":
                        round_unit(act, u + AHEAD, i, 4)
                        act.wait_ge(p_pe.sem, p_pe.done(s, h0) + i * 2 * len(p_pe.names))
                        act.activation(halves(sqn), tile(g), ACT.Square).then_inc(p_act.sem, p_act.one("sqqn"))
                    elif s == "qr":
                        act.wait_ge(unit_done, u + 1 + i * 4)
                        act.activation(sqr[0:ROPE].rearrange("p (a b) -> p a b", a=2), tile(g)[0:ROPE], ACT.Square)\
                            .then_inc(p_act.sem, p_act.one("sqqr"))
                    elif s == "kn":
                        round_unit(act, u + 1 + AHEAD, i, 4)
                        act.wait_ge(p_pe.sem, p_pe.done(s, h0) + i * 2 * len(p_pe.names))
                        act.activation(halves(sqk), tile(g), ACT.Square).then_inc(p_act.sem, p_act.one("sqkn"))

                def attend(s, j, h0, i, g):
                    k, b = s
                    R, K = rows(b), keys(b)
                    if k == "S":
                        st = stat[0:R, 8 * b:8 * b + 4]
                        act.wait_ge(a_dve.sem, a_dve.done(("bias", b), h0) + i * 2 * len(a_dve.names))
                        act.wait_ge(a_pe.sem, PROB_READ(b, h0) + i * 2 * len(a_pe.names))
                        act.activation(prob[b % 2][0:R, 0:K], flat(g)[0:R, 0:K], ACT.Exp, bias=st[:, 1:2], scale=SCALE,
                                       accum_out=st[:, 2:3]).then_inc(a_act.sem, a_act.one(("exp", b)))
                    elif k == "T" and b < QB:
                        act.wait_ge(a_pe.sem, a_pe.done(s, h0) + i * 2 * len(a_pe.names))
                        act.activation(pt[b % 2][:, 0:P * (b + 1)], flat(g)[:, 0:P * (b + 1)], ACT.Copy)\
                            .then_inc(a_act.sem, a_act.one(("copy", b)))
                    elif k == "O":
                        q0 = META + b * P if b < QB else 0
                        act.wait_ge(a_pe.sem, a_pe.done(s, h0) + i * 2 * len(a_pe.names))
                        hi = hid[:, bass.ds(h0 + 2 * i, 1), 0, q0:q0 + R].rearrange("p a b -> p (a b)")
                        act.activation(hi, flat(g)[:, 0:R], ACT.Copy).then_inc(a_act.sem, a_act.one(("hi", b)))

                walk(None, proj, attend, act)
                out_act(act, n + 1, uO)

            def PROB_READ(b, h0):
                if b < 2:
                    v = a_pe.done(("T", b + 2 if b else 4), h0 - 1)
                    return max(v, 1)
                return a_pe.done(("T", b - 2), h0)

            def pool_(pool):
                for t in range(6):
                    split_unit(pool, u0 + t + AHEAD)
                for t in range(5):
                    pool.wait_ge(l_act.sem, l_act.done(("hi", t)))
                    pool.tensor_tensor(xs[:, t, 1], lat[t], xs[:, t, 0].bitcast(F32), ALU.subtract)\
                        .then_inc(l_pool.sem, l_pool.one(("lo", t)))
                for u in range(uH, uO):
                    split_unit(pool, u + AHEAD)
                out_pool(pool, n + 1, uO)

            return {"pe": pe_, "dve": dve_, "act": act_, "pool": pool_}

        def hgrn(n, u0, g0):
            C, NC = 16, T // 16
            names = ("q16", "kinv", "kt16", "q32", "k32", "q64", "k64", "q128", "k128", "vfm", "gate", "qraw", "sigq",
                     "fg", "kk", "G", "E", "Ei", "Et", "graw", "sigg", "o", "sqo", "ms", "fac", "masks")
            b_ = {x: work[:, k] for k, x in enumerate(names)}
            vt = work[:, 26:28].rearrange("p a b -> p (a b)")
            kt = scr[:, 0:2].rearrange("p a b -> p (a b)")
            mk = scr[:, 2, 0:512]
            misc = scr[:, 3]
            at_ = [misc[:, 0:128], ub[:, 1, 2:130]]
            state = misc[:, 128:256]
            us = [ub[:, 1, 130:258], ub[:, 1, 258:386]]
            d16, d32, d64, d128 = misc[:, 256:289], misc[:, 290:306], misc[:, 306:314], misc[:, 314:318]
            lb, lb1, g_o = misc[:, 320:328], misc[:, 328:336], misc[:, 336:337]
            lg, le, lm, ls = misc[:, 340:372], misc[:, 372:404], misc[:, 404:412], misc[:, 412:420]
            scan_mask = ub[:, 0, 2:]
            quarters = b_["ms"]

            P_SEQ = ["f", "q", "e1", "e2", "i", "e3", "e4", "g", "e5"]
            A_SEQ = ["VK", "M", ("S", 0), "OM", ("S", 1), ("O", 0), ("S", 2), ("O", 1), ("S", 3), ("O", 2), ("O", 3),
                     "Q", "N", "F"]
            X_SEQ = ["VK", "M", "f'", ("S", 0), "q'", "OM", "e1'", ("S", 1), ("O", 0), ("S", 2), "e2'",
                     ("O", 1), ("S", 3), "i'", ("O", 2), "e3'", ("O", 3), "Q", "e4'", "g'", "N", "F", "e5'"]
            NO_TILE = ("e1", "e2", "e3", "e4", "e5", "Q", "F")

            def numbered(seq, g):
                out = []
                for s in seq:
                    head = s.rstrip("'") if isinstance(s, str) else s
                    out.append((head, isinstance(s, str) and s.endswith("'"), g))
                    g += head not in NO_TILE
                return out, g
            prologue, gX = numbered(P_SEQ, g0 + 1)
            body, gX1 = numbered(X_SEQ, gX)
            PER = gX1 - gX
            assert PER % 4 == 0
            epilogue, gO = numbered(A_SEQ, gX + PER * (HEADS - 1))
            assert gO + DT == g0 + 1 + HGRN_TILES, (gO + DT - g0 - 1)
            uO = u0 + 4 * HEADS
            UNIT_OF = {"f": 0, "q": 1, "i": 2, "g": 3}

            def walk(eng, project_, attend):
                for s, _, g in prologue:
                    project_(s, 0, 0, g)
                with eng.Fori(0, HEADS - 1) as i:
                    for s, next_, g in body:
                        if next_:
                            project_(s, 1, i, g)
                        else:
                            attend(s, 0, i, g)
                for s, _, g in epilogue:
                    attend(s, HEADS - 1, 0, g)

            consts_in = sem("hgrn_consts")
            c_dve = Order(sem("hgrn_c_dve"), ["clear", "m1", "m2", "max", "sub0", "sub1", "sub2", "sub3", "s1", "s2", "sum", "rec",
                                              "lb", "lb1"])
            c_act = Order(sem("hgrn_c_act"), ["exp"])
            p_act = Order(sem("hgrn_p_act"), ["sigf", "sigq", "ln", "E", "Ei", "Et", "q32", "k32", "q64", "k64",
                                              "q128", "k128", "k128m", "sigg"])
            p_dve = Order(sem("hgrn_p_dve"), ["forget", "k", "G", "tail", "q", "q16", "kinv", "kt16",
                                              "d16", "d32", "d64", "d128", "q32", "k32", "q64", "k64", "q128", "k128", "gate"])
            a_pe = Order(sem("hgrn_a_pe"), A_SEQ[:-1])
            a_dve = Order(sem("hgrn_a_dve"),
                          ["vtm", "ktm", ("mk", 0), ("at", 0), "om", ("mk", 1), ("at", 1), ("st", 0), ("mk", 2), ("at", 2),
                           ("st", 1), ("at", 3), ("st", 2), "o3"] + [("f", s) for s in RSQRT[1:]] + ["gated"])
            a_act = Order(sem("hgrn_a_act"), ["vt", "sqo", "hi"])
            a_pool = Order(sem("hgrn_a_pool"), ["lo"], start=1)

            def pe_(pe):
                first_tiles_pe(pe, n, u0, g0)
                x = split_tiles(xs, range(DT))

                def proj(s, r, i, g):
                    if s in NO_TILE or s in ("f", "q") and r == 0:
                        return
                    pe.wait_ge(lo_ready, u0 + 4 * r + UNIT_OF[s] + 1 + i * 4)
                    pe.wait_ge(tile_free, g - 3 + i * PER)
                    project(pe, tile(g), (u0 + UNIT_OF[s]) % RING, 0, x, True, True, unit_done)

                def attend(s, r, i, g):
                    if s == "F":
                        return
                    if s == "Q":
                        pe.wait_ge(a_act.sem, a_act.done("sqo", r + i))
                        sums_pe(pe, g_of(("O", QB - 1), g), SUMS, [(b_["sqo"], P)]).then_inc(a_pe.sem, a_pe.one(s))
                        return
                    pe.wait_ge(tile_free, g - 3 + i * PER)
                    f = flat(g)
                    if s == "VK":
                        pe.wait_ge(p_dve.sem, p_dve.done("k128", r + i))
                        pe.wait_ge(p_act.sem, p_act.done("k128m", r + i))
                        for b in range(QB):
                            c = slice(META + b * P, META + (b + 1) * P)
                            pe.transpose(f[:, b * P:(b + 1) * P], b_["vfm"][:, c], ident[:])
                        for b in range(QB):
                            c = slice(META + b * P, META + (b + 1) * P)
                            mm = pe.transpose(f[:, 512 + b * P:512 + (b + 1) * P], b_["k128"][:, c], ident[:])
                    elif s == "M":
                        pe.transpose(f[0:META, 0:P], b_["vfm"][:, 0:META], ident[:])
                        pe.transpose(f[0:META, P:2 * P], b_["k128"][:, 0:META], ident[:])
                        mm = pe.matmul(f[0:META, 256:256 + META], b_["kinv"][:, 0:META], b_["q16"][:, 0:META],
                                       start=True, stop=True)
                    elif s == "OM":
                        pe.wait_ge(tile_free, g_of("M", g) + 1 + i * PER)
                        pe.matmul(f[:, 0:META], vt[0:META, 512:640], at_[1][0:META, 0:META], start=True, stop=True)
                        mm = pe.matmul(f[:, 512:640], kt[0:META, 512:640], vt[0:META, 512:640], start=True, stop=True)
                    elif s == "N":
                        pe.wait_ge(a_dve.sem, a_dve.done(("f", LAST), r + i))
                        mm = spread_pe(pe, g, quarters)
                    elif s[0] == "S":
                        b = s[1]
                        c = slice(META + b * P, META + (b + 1) * P)
                        for lv, (k_, q_) in enumerate((("kinv", "q16"), ("kt16", "q16"), ("k32", "q32"), ("k64", "q64"))):
                            mm = pe.matmul(f[:, lv * P:(lv + 1) * P], b_[k_][:, c], b_[q_][:, c], start=True, stop=True)
                        if b < QB - 1:
                            pe.wait_ge(tile_free, g_of("VK", g) + 1 + i * PER)
                            mm = pe.matmul(f[:, 512:640], kt[:, b * P:(b + 1) * P], vt[:, b * P:(b + 1) * P],
                                           start=True, stop=True)
                    else:
                        b = s[1]
                        c = slice(META + b * P, META + (b + 1) * P)
                        pe.wait_ge(a_dve.sem, a_dve.done(("at", b), r + i))
                        if b:
                            pe.wait_ge(a_dve.sem, a_dve.done(("st", b - 1), r + i))
                        else:
                            pe.wait_ge(tile_free, g_of("OM", g) + 1 + i * PER)
                        pe.matmul(f[:, 0:P], vt[:, b * P:(b + 1) * P], at_[b % 2], start=True, stop=False)
                        mm = pe.matmul(f[:, 0:P], state, b_["q128"][:, c], start=False, stop=True)
                    mm.then_inc(a_pe.sem, a_pe.one(s))

                walk(pe, proj, attend)
                pe.wait_ge(a_pool.sem, a_pool.done("lo", HEADS - 1))
                out_pe(pe, uO, gO, split_tiles(hid, range(HEADS)))

            def g_of(s, g):
                seq = epilogue if g >= gX + PER * (HEADS - 1) else body
                return [x for t, next_, x in seq if t == s and not next_][0]

            def dve_(dve):
                dve.wait_ge(consts_in, 48)
                dve.memset(quarters, 0.0).then_inc(c_dve.sem, c_dve.one("clear"))
                L4 = [lg[:, 8 * k:8 * k + 8] for k in range(4)]
                E4 = [le[:, 8 * k:8 * k + 8] for k in range(4)]

                def small(name, a0, a1, op, out):
                    dve.tensor_tensor(out, a0, a1, op).then_inc(c_dve.sem, c_dve.one(name))
                    dve.wait_ge(c_dve.sem, c_dve.done(name))
                small("m1", L4[0], L4[1], ALU.max, lm)
                small("m2", lm, L4[2], ALU.max, lm)
                small("max", lm, L4[3], ALU.max, lm)
                for k in range(4):
                    small(f"sub{k}", L4[k], lm, ALU.subtract, L4[k])
                dve.wait_ge(c_act.sem, c_act.done("exp"))
                small("s1", E4[0], E4[1], ALU.add, ls)
                small("s2", ls, E4[2], ALU.add, ls)
                small("sum", ls, E4[3], ALU.add, ls)
                dve.reciprocal(ls, ls).then_inc(c_dve.sem, c_dve.one("rec"))
                dve.wait_ge(c_dve.sem, c_dve.done("rec"))
                small("lb", E4[1], ls, ALU.mult, lb)
                dve.tensor_scalar(lb1, lb, -1.0, 1.0, ALU.mult, ALU.add).then_inc(c_dve.sem, c_dve.one("lb1"))
                dve.wait_ge(c_dve.sem, c_dve.done("lb1"))
                norm_dve(dve, n, g0)

                def step(o, name, r):
                    return o.done(name, r)

                def tt(out, x, y, op, name, o=p_dve):
                    dve.tensor_tensor(out, x, y, op).then_inc(o.sem, o.one(name))

                def v(name, count):
                    return b_[name][:, META:].rearrange("p (a b c) -> p a b c", b=2, c=count)

                def proj(s, r, i, g):
                    R = r + i
                    if s in UNIT_OF:
                        dst = {"f": "fg", "q": "qraw", "i": "vfm", "g": "graw"}[s]
                        dve.wait_ge(unit_done, u0 + 4 * r + UNIT_OF[s] + 1 + i * 4)
                        dve.tensor_tensor(halves(b_[dst]), tile(g), halves(rstd[:]), ALU.mult).then_inc(tile_free, 1)
                    elif s == "e1":
                        dve.wait_ge(p_act.sem, p_act.done("sigf", R))
                        dve.tensor_scalar(b_["fg"], b_["fg"], lb1[:, bass.ds(R, 1)], lb[:, bass.ds(R, 1)], ALU.mult, ALU.add)\
                           .then_inc(p_dve.sem, p_dve.one("forget"))
                        dve.wait_ge(p_dve.sem, p_dve.done("forget", R))
                        dve.tensor_scalar(b_["kk"], b_["fg"], -1.0, 1.0, ALU.mult, ALU.add)\
                           .then_inc(p_dve.sem, p_dve.one("k"))
                    elif s == "e2":
                        dve.wait_ge(p_act.sem, p_act.done("ln", R))
                        dve.tensor_tensor_scan(b_["G"], scan_mask, b_["fg"], 0.0, ALU.mult, ALU.add)\
                           .then_inc(p_dve.sem, p_dve.one("G"))
                        dve.wait_ge(p_dve.sem, p_dve.done("G", R))
                        Gv = b_["G"].rearrange("p (a b) -> p a b", b=C)
                        tt(b_["Et"].rearrange("p (a b) -> p a b", b=C), Gv[:, :, C - 1:C].broadcast_to([P, NC, C]), Gv,
                           ALU.subtract, "tail")
                    elif s == "e3":
                        dve.wait_ge(p_act.sem, p_act.done("Et", R))
                        tt(b_["qraw"], b_["qraw"], b_["sigq"], ALU.mult, "q")
                        dve.wait_ge(p_dve.sem, p_dve.done("q", R))
                        tt(b_["q16"], b_["qraw"], b_["E"], ALU.mult, "q16")
                        tt(b_["kinv"], b_["kk"], b_["Ei"], ALU.mult, "kinv")
                        tt(b_["kt16"], b_["kk"], b_["Et"], ALU.mult, "kt16")
                    elif s == "e5":
                        dve.wait_ge(p_act.sem, p_act.done("sigg", R))
                        tt(b_["gate"], b_["graw"], b_["sigg"], ALU.mult, "gate")
                        dve.wait_ge(p_dve.sem, p_dve.done("gate", R))
                    elif s == "e4":
                        dve.tensor_copy(d16, b_["E"].rearrange("p (a b) -> p a b", b=C)[:, :, C - 1])\
                           .then_inc(p_dve.sem, p_dve.one("d16"))
                        dve.wait_ge(p_dve.sem, p_dve.done("d16", R))
                        pair = lambda d: d.rearrange("p (a b) -> p a b", b=2)
                        dd = [pair(d16[:, 1:33]), pair(d32), pair(d64)]
                        for name, src, dst in (("d32", dd[0], d32), ("d64", dd[1], d64), ("d128", dd[2], d128)):
                            tt(dst, src[:, :, 0], src[:, :, 1], ALU.mult, name)
                            dve.wait_ge(p_dve.sem, p_dve.done(name, R))
                        for lv, (w, src, dst) in enumerate(((16, ("q16", "kt16"), ("q32", "k32")),
                                                            (32, ("q32", "k32"), ("q64", "k64")),
                                                            (64, ("q64", "k64"), ("q128", "k128")))):
                            nb = SEQ // (2 * w)
                            if lv:
                                dve.wait_ge(p_act.sem, p_act.done(src[1], R))
                                dve.wait_ge(p_dve.sem, p_dve.done(src[1], R))
                            tt(v(dst[0], w)[:, :, 1], v(src[0], w)[:, :, 1], dd[lv][:, :, 0:1].broadcast_to([P, nb, w]),
                               ALU.mult, dst[0])
                            tt(v(dst[1], w)[:, :, 0], v(src[1], w)[:, :, 0], dd[lv][:, :, 1:2].broadcast_to([P, nb, w]),
                               ALU.mult, dst[1])

                def attend(s, r, i, g):
                    R = r + i
                    f = flat(g)
                    if s == "VK":
                        dve.wait_ge(a_act.sem, a_act.done("vt", R))
                        dve.tensor_copy(kt[:, 0:512], f[:, 512:1024]).then_inc(tile_free, 1)
                    elif s == "M":
                        dve.wait_ge(a_pe.sem, a_pe.done(s, R))
                        dve.tensor_copy(vt[0:META, 512:640], f[0:META, 0:P]).then_inc(a_dve.sem, a_dve.one("vtm"))
                        dve.tensor_copy(kt[0:META, 512:640], f[0:META, P:2 * P]).then_inc(a_dve.sem, a_dve.one("ktm"))
                        dve.tensor_tensor(at_[1][0:META, 0:META], f[0:META, 256:256 + META], b_["masks"][0:META, 0:META],
                                          ALU.mult).then_inc(tile_free, 1)
                    elif s == "OM":
                        dve.wait_ge(a_pe.sem, a_pe.done(s, R))
                        dve.tensor_copy(b_["o"][:, 0:META], f[:, 0:META]).then_inc(a_dve.sem, a_dve.one("om"))
                        dve.tensor_copy(state, f[:, 512:640]).then_inc(tile_free, 1)
                    elif s == "Q":
                        dve.wait_ge(a_pe.sem, a_pe.done(s, R))
                        gq = g_of(("O", QB - 1), g)
                        mean_rsqrt(dve, gq, [SUMS], P, [quarters], b_["sqo"], a_dve, "f", R, free=gq + 1 + i * PER)
                    elif s == "N":
                        dve.wait_ge(a_pe.sem, a_pe.done(s, R))
                        dve.scalar_tensor_tensor(halves(b_["o"]), halves(b_["o"]), g_o, tile(g), ALU.mult, ALU.mult)\
                           .then_inc(tile_free, 1)
                        dve.wait_ge(tile_free, g + 1 + i * PER)
                    elif s == "F":
                        dve.wait_ge(a_pool.sem, a_pool.done("lo", R) - 1)
                        tt(b_["fac"], b_["o"], b_["gate"], ALU.mult, "gated", a_dve)
                        dve.wait_ge(a_dve.sem, a_dve.done("gated", R))
                    elif s[0] == "S":
                        b = s[1]
                        dve.wait_ge(a_pe.sem, a_pe.done(s, R))
                        if b:
                            dve.wait_ge(a_dve.sem, a_dve.done(("at", b - 1), R))
                        masked = dve.tensor_tensor(mk, f[:, 0:512], b_["masks"][:, 0:512], ALU.mult)
                        if b < QB - 1:
                            masked.then_inc(a_dve.sem, a_dve.one(("mk", b)))
                            dve.wait_ge(a_dve.sem, a_dve.done(("mk", b), R))
                            dve.tensor_copy(us[b % 2], f[:, 512:640]).then_inc(tile_free, 1)
                        else:
                            masked.then_inc(tile_free, 1)
                            dve.wait_ge(tile_free, g + 1 + i * PER)
                        dve.tensor_reduce(at_[b % 2], mk.rearrange("p (l t) -> p t l", t=P), AX.X, ALU.add)\
                           .then_inc(a_dve.sem, a_dve.one(("at", b)))
                    else:
                        b = s[1]
                        c = slice(META + b * P, META + (b + 1) * P)
                        dve.wait_ge(a_pe.sem, a_pe.done(s, R))
                        if b < QB - 1:
                            dve.scalar_tensor_tensor(state, state, d128[:, b:b + 1], us[b % 2], ALU.mult, ALU.add)\
                               .then_inc(a_dve.sem, a_dve.one(("st", b)))
                        out = dve.tensor_copy(b_["o"][:, c], f[:, 0:P])
                        if b < QB - 1:
                            out.then_inc(tile_free, 1)
                        else:
                            out.then_inc(a_dve.sem, a_dve.one("o3"))

                walk(dve, proj, attend)
                out_dve(dve, n + 1, uO, gO)

            def act_(act):
                last_stage_over(act, n)
                act.dma_start(b_["masks"][:, 0:512], a["hgrn_masks"]).then_inc(consts_in, 16)
                act.dma_start(scan_mask, a["hgrn_scan"]).then_inc(consts_in, 16)
                act.dma_start(misc[:, 336:372], a["hgrn_par"]).then_inc(consts_in, 16)
                act.wait_ge(c_dve.sem, c_dve.done("sub3"))
                act.activation(le, lg, ACT.Exp).then_inc(c_act.sem, c_act.one("exp"))

                def f(out, x, func, name, o=p_act, **kw):
                    act.activation(out, x, func, **kw).then_inc(o.sem, o.one(name))

                def v(name, count):
                    return b_[name][:, META:].rearrange("p (a b c) -> p a b c", b=2, c=count)

                def proj(s, r, i, g):
                    R = r + i
                    if s in UNIT_OF:
                        round_unit(act, u0 + 4 * r + UNIT_OF[s] + AHEAD, i, 4)
                    if s in ("f", "q", "g"):
                        act.wait_ge(tile_free, g + 1 + i * PER)
                        src = {"f": "fg", "q": "qraw", "g": "graw"}[s]
                        dst = {"f": "fg", "q": "sigq", "g": "sigg"}[s]
                        f(b_[dst], b_[src], ACT.Sigmoid, "sig" + s)
                    elif s == "e1":
                        act.wait_ge(p_dve.sem, p_dve.done("k", R))
                        f(b_["fg"], b_["fg"], ACT.Ln, "ln")
                    elif s == "e2":
                        act.wait_ge(p_dve.sem, p_dve.done("tail", R))
                        f(b_["E"], b_["G"], ACT.Exp, "E")
                        f(b_["Ei"], b_["G"], ACT.Exp, "Ei", scale=-1.0)
                        f(b_["Et"], b_["Et"], ACT.Exp, "Et")
                    elif s == "e4":
                        act.wait_ge(p_dve.sem, p_dve.done("kt16", R))
                        for w, src, dst in ((16, ("q16", "kt16"), ("q32", "k32")), (32, ("q32", "k32"), ("q64", "k64")),
                                            (64, ("q64", "k64"), ("q128", "k128"))):
                            if w > 16:
                                act.wait_ge(p_dve.sem, p_dve.done(src[1], R))
                                act.wait_ge(p_act.sem, p_act.done(src[1], R))
                            f(v(dst[0], w)[:, :, 0], v(src[0], w)[:, :, 0], ACT.Copy, dst[0])
                            f(v(dst[1], w)[:, :, 1], v(src[1], w)[:, :, 1], ACT.Copy, dst[1])
                        f(b_["k128"][:, 0:META], b_["kt16"][:, 0:META], ACT.Copy, "k128m")

                def attend(s, r, i, g):
                    R = r + i
                    if s == "VK":
                        act.wait_ge(a_pe.sem, a_pe.done(s, R))
                        f(vt[:, 0:512], flat(g)[:, 0:512], ACT.Copy, "vt", a_act)
                    elif s == "Q":
                        act.wait_ge(a_dve.sem, a_dve.done("o3", R))
                        f(b_["sqo"], b_["o"], ACT.Square, "sqo", a_act)
                    elif s == "F":
                        act.wait_ge(a_dve.sem, a_dve.done("gated", R))
                        hi = hid[:, bass.ds(R, 1), 0].rearrange("p a b -> p (a b)")
                        f(hi, b_["fac"], ACT.Copy, "hi", a_act)

                walk(act, proj, attend)
                out_act(act, n + 1, uO)

            def pool_(pool):
                pool.sem_inc(a_pool.sem, 1)

                def proj(s, r, i, g):
                    if s in UNIT_OF:
                        split_unit(pool, u0 + 4 * r + UNIT_OF[s] + AHEAD, i, 4)

                def attend(s, r, i, g):
                    if s == "F":
                        pool.wait_ge(a_act.sem, a_act.done("hi", r + i))
                        hi = hid[:, bass.ds(r + i, 1), 0].rearrange("p a b -> p (a b)")
                        lo = hid[:, bass.ds(r + i, 1), 1].rearrange("p a b -> p (a b)")
                        pool.tensor_tensor(lo, b_["fac"], hi.bitcast(F32), ALU.subtract)\
                            .then_inc(a_pool.sem, a_pool.one("lo"))

                walk(pool, proj, attend)
                out_pool(pool, n + 1, uO)

            return {"pe": pe_, "dve": dve_, "act": act_, "pool": pool_}

        def s5(n, u0, g0):
            if "s5" not in stages:
                return {}
            NPAIR, CH = D // 32, 64
            HP = NPAIR // 2
            NCH = 1 + SEQ // CH
            av = work[:, 0:8]
            flat_work = work[:].rearrange("p a b -> p (a b)")
            cols = [8 * T]

            def take(k):
                cols[0] += k
                return flat_work[:, cols[0] - k:cols[0]]
            Tc, Ts, R0 = (take(NPAIR * CH).rearrange("p (a b) -> p a b", b=CH) for _ in range(3))
            Bl = take(2 * DT * P).rearrange("p (f c s) -> p f c s", c=2, s=P)
            Cl = take(2 * NPAIR * 32).rearrange("p (a c s) -> p a c s", c=2, s=32)
            xr, xi, cr, ci = (take(NPAIR) for _ in range(4))
            assert cols[0] <= NW * T
            tmp = [work2[:, 1024 * k:1024 * (k + 1)] for k in range(8)]
            pairs = lambda t: t.rearrange("p (a b) -> p a b", a=NPAIR)
            chunk = [spare[:, 2048 * k:2048 * (k + 1)].rearrange("p (f q s) -> p f q s", q=4, s=CH) for k in range(2)]
            braw, bbar = [tmp[0], tmp[1]], [tmp[2], tmp[3]]
            scr_ = scr[:].rearrange("p a b -> p (a b)")
            dcol = scr_[:, 2048:2056]
            zs = [(scr_[:, 0:1024], scr_[:, 1024:2048]), (spare[:, 4096:5120], spare[:, 5120:6144])]
            ybuf = [spare[:, 6656 + 512 * k:7168 + 512 * k].rearrange("p (f s) -> p f s", s=CH) for k in range(2)]
            R0m = spare[:, 6144:6656].rearrange("p (a b) -> p a b", b=META)
            lre, lim, ldt, mag, zre, zim, sn, cs, ang, sh, dt, are, kk, rr, pp, t0 = (
                ub[:, 0, 2 + NPAIR * k:2 + NPAIR * (k + 1)] for k in range(16))
            t1 = ub[:, 1, 2:2 + NPAIR]

            LOG2E, LN2_A, LN2_B = 1.4426950408889634, 0.693359375, -2.12194440e-4
            TWO_PI, TWO_PI_A, PI_BELOW = 6.283185307179586, 6.28125, 3.1415925
            ROUND = 12582912.0

            gB = g0 + 1
            gM = gB + 2
            gS = gM + 2
            gO = gS + 6 * (NCH - 1) + 4
            assert gO + 2 * DT == g0 + 1 + S5_TILES, gO + 2 * DT - g0 - 1

            consts_in, lam_in = sem("s5_consts"), sem("s5_lam")
            EXP = ["k", "int", "ra", "rb", "clamp", "two"] + [f"p{k}" for k in range(8)]
            SETUP = [("dt", x) for x in EXP] + ["x"] + [("mag", x) for x in EXP] + \
                ["ang", "turns", "int", "ra", "rb", "clamp", "s2", "cs", "are", "aim", "are1", "m1", "m2", "num_re",
                 "m3", "m4", "num_im", "d1", "d2", "den", "rden", "zre", "zim"] + \
                [("bb", k) for k in range(3)] + ["T0c", "T0s"] + [(x, m) for m in range(5) for x in range(6)] + \
                [(0, 5), (1, 5), (4, 5)] + [("a", m) for m in range(DT)]
            c_dve = Order(sem("s5_c_dve"), SETUP)
            c_act = Order(sem("s5_c_act"), ["sin", "sinh", "negative", "R0", "R0m"])
            c_pool = Order(sem("s5_c_pool"), [("bb", k) for k in range(3)] + [(2, 5), (3, 5), (5, 5), "R0z", "R0mz"])
            c_pe = Order(sem("s5_c_pe"), ["B0", "B1"])
            HALFN = ["xr", "xi", "c0", "c1", "t1", "t3", "wr", "c2", "zr", "c3", "zi", "p1", "p2"]
            h_dve = [Order(sem(f"s5_half{hf}"), HALFN) for hf in range(2)]
            h_pool = [Order(sem(f"s5_half{hf}_pool"), ["wi", "p3", "p4"]) for hf in range(2)]
            bu_pe = [sem(f"s5_bu{hf}") for hf in range(2)]
            y_pe = [sem(f"s5_y{hf}") for hf in range(2)]
            y_read = Order(sem("s5_y_read"), [(hf, f) for hf in range(2) for f in range(3)])
            gelu_made, gelu_done = sem("s5_gelu"), sem("s5_gelu_copied")
            g_act = Order(sem("s5_g_act"), [("hi", m) for m in range(DT)])
            g_dve = Order(sem("s5_g_dve"), [("lo", m) for m in range(DT)])
            chunk_in = sem("s5_chunk_in")
            chunk_zero = sem("s5_chunk_zero")
            o_act = sem("s5_gate")

            def inputs(t, k, i):
                if k == 0:
                    return av[:, t, 0:META]
                at_ = META + CH * (k - 1)
                return av[:, t, at_:at_ + CH] if isinstance(i, int) else av[:, t, bass.ds(i * (2 * CH) + at_, CH)]

            def walk(eng, bu, y):
                def step(k, i, g):
                    bu(1, k, i, g)
                    if k < NCH - 1:
                        bu(0, k + 1, i, g + 2)
                        g += 2
                    y(0, k, i, g + 2)
                    y(1, k, i, g + 3)
                bu(0, 0, 0, gM)
                for k in range(2):
                    step(k, 0, gS + 6 * k)
                with eng.Fori(0, (NCH - 3) // 2) as i:
                    for k in (2, 3):
                        step(k, i, gS + 6 * k)
                step(NCH - 1, 0, gS + 6 * (NCH - 1))

            def pe_(pe):
                norm_sum_pe(pe, n, g0)
                norm_spread_pe(pe, n, g0)
                for x, made in enumerate((c_dve, c_pool)):
                    pe.wait_ge(made.sem, made.done(("bb", 2)))
                    pe.wait_ge(tile_free, gB + x - 3)
                    for f in range(DT):
                        mm = pe.transpose(flat(gB + x)[:, f * P:(f + 1) * P], bbar[x][:, f * P:(f + 1) * P], ident[:])
                    mm.then_inc(c_pe.sem, c_pe.one(f"B{x}"))
                pe.wait_ge(tile_free, gB + 2)
                pe.wait_ge(c_dve.sem, c_dve.done(("a", DT - 1)))
                pe.wait_ge(consts_in, 48)
                pe.wait_ge(c_act.sem, c_act.done("negative"))

                def bu(hf, k, i, g):
                    N = META if k == 0 else CH
                    pe.wait_ge(chunk_in, 4 * k + 4 + i * 8)
                    for part in range(2):
                        pe.wait_ge(tile_free, g + part - 3 + i * 12)
                        for f in range(4):
                            out = flat(g + part)[:, f * 256:(f + 1) * 256].rearrange("p (a b) -> p a b", b=CH)
                            mm = pe.matmul(out[:, :, 0:N], Bl[:, hf * 4 + f, part, :], chunk[k % 2][:, hf * 4 + f, :, 0:N],
                                           start=True, stop=True)
                    mm.then_inc(bu_pe[hf], 1)

                def y(hf, k, i, g):
                    N = META if k == 0 else CH
                    pe.wait_ge(tile_free, g - 3 + i * 12)
                    pe.wait_ge(h_dve[hf].sem, h_dve[hf].done("p2", k + i * 2))
                    pe.wait_ge(h_pool[hf].sem, h_pool[hf].done("p4", k + i * 2))
                    for q in range(HP):
                        pair = hf * HP + q
                        r0 = 32 * (pair % 4)
                        for x in range(4):
                            mm = pe.matmul(flat(g)[r0:r0 + 32, (q // 4) * CH:(q // 4) * CH + N],
                                           Cl[:, pair, x // 2, :], tmp[4 * hf + x][:, q * N:(q + 1) * N],
                                           start=x == 0, stop=x == 3, tile_position=(0, r0))
                    mm.then_inc(y_pe[hf], 1)

                walk(pe, bu, y)
                for m in range(2 * DT):
                    pe.wait_ge(lo_ready, u0 + m + 1)
                    pe.wait_ge(tile_free, gO + m - 3)
                    project(pe, tile(gO + m), (u0 + m) % RING, 0, split_tiles(hid, range(DT)), True, True, unit_done,
                            {k: (g_dve.sem, g_dve.done(("lo", k))) for k in range(DT) if m == 0})

            def setup_dve(dve):
                def did(name, ins):
                    ins.then_inc(c_dve.sem, c_dve.one(name))
                    dve.wait_ge(c_dve.sem, c_dve.done(name))

                def tt(name, out, x, y, op):
                    did(name, dve.tensor_tensor(out, x, y, op))

                def ts(name, out, x, s1, s2, op1, op2):
                    did(name, dve.tensor_scalar(out, x, s1, s2, op1, *([op2] if op2 else [])))

                def stt(name, out, x, s, y, op1, op2):
                    did(name, dve.scalar_tensor_tensor(out, x, s, y, op1, op2))

                def exp(v, out, x):
                    ts((v, "k"), kk, x, LOG2E, ROUND, ALU.mult, ALU.add)
                    ts((v, "int"), kk, kk, ROUND, None, ALU.subtract, None)
                    stt((v, "ra"), rr, kk, -LN2_A, x, ALU.mult, ALU.add)
                    stt((v, "rb"), rr, kk, -LN2_B, rr, ALU.mult, ALU.add)
                    ts((v, "clamp"), kk, kk, -127.0, 128.0, ALU.max, ALU.min)
                    ts((v, "two"), t0.bitcast(mybir.dt.int32), kk, 2.0 ** 23, 127 * 2.0 ** 23, ALU.mult, ALU.add)
                    c, fact = [], 1.0
                    for k in range(1, 8):
                        fact *= k
                        c.append(1.0 / fact)
                    ts((v, "p0"), pp, rr, c[6], None, ALU.mult, None)
                    for k in range(1, 7):
                        stt((v, f"p{k}"), pp, pp, c[6 - k], rr, ALU.add, ALU.mult)
                    stt((v, "p7"), out, pp, 1.0, t0, ALU.add, ALU.mult)

                dve.wait_ge(lam_in, 16)
                exp("dt", dt, ldt)
                tt("x", t1, lre, dt, ALU.mult)
                exp("mag", mag, t1)
                tt("ang", ang, lim, dt, ALU.mult)
                ts("turns", kk, ang, 1.0 / TWO_PI, ROUND, ALU.mult, ALU.add)
                ts("int", kk, kk, ROUND, None, ALU.subtract, None)
                stt("ra", ang, kk, -TWO_PI_A, ang, ALU.mult, ALU.add)
                stt("rb", ang, kk, -(TWO_PI - TWO_PI_A), ang, ALU.mult, ALU.add)
                ts("clamp", ang, ang, -PI_BELOW, PI_BELOW, ALU.max, ALU.min)
                dve.wait_ge(c_act.sem, c_act.done("sinh"))
                tt("s2", cs, sh, sh, ALU.mult)
                ts("cs", cs, cs, -2.0, 1.0, ALU.mult, ALU.add)
                tt("are", are, mag, cs, ALU.mult)
                tt("aim", t1, mag, sn, ALU.mult)
                ts("are1", are, are, 1.0, None, ALU.subtract, None)
                tt("m1", zre, are, lre, ALU.mult)
                tt("m2", t0, t1, lim, ALU.mult)
                tt("num_re", zre, zre, t0, ALU.add)
                tt("m3", zim, t1, lre, ALU.mult)
                tt("m4", t0, are, lim, ALU.mult)
                tt("num_im", zim, zim, t0, ALU.subtract)
                tt("d1", t0, lre, lre, ALU.mult)
                tt("d2", t1, lim, lim, ALU.mult)
                tt("den", t0, t0, t1, ALU.add)
                did("rden", dve.reciprocal(t0, t0))
                tt("zre", zre, zre, t0, ALU.mult)
                tt("zim", zim, zim, t0, ALU.mult)

            def wide(v, k):
                return v.rearrange("p (a b) -> p a b", b=1).broadcast_to([P, NPAIR, k])

            def input_matrix(eng, o, x, temp):
                for k, (out, in0, in1, op) in enumerate(((pairs(bbar[x]), pairs(braw[x]), wide(zre, 32), ALU.mult),
                                                         (pairs(temp), pairs(braw[1 - x]), wide(zim, 32), ALU.mult),
                                                         (bbar[x], bbar[x], temp, ALU.add if x else ALU.subtract))):
                    eng.tensor_tensor(out, in0, in1, op).then_inc(o.sem, o.one(("bb", k)))
                    eng.wait_ge(o.sem, o.done(("bb", k)))

            def double(eng, o, m, steps):
                N = 1 << m
                a_, b_, c_, d_ = (pairs(tmp[x])[:, :, 0:N] for x in (5, 6, 7, 4))
                cN, sN = (t[:, :, N - 1:N].broadcast_to([P, NPAIR, N]) for t in (Tc, Ts))
                c0, s0, c1, s1 = Tc[:, :, 0:N], Ts[:, :, 0:N], Tc[:, :, N:2 * N], Ts[:, :, N:2 * N]
                ops = ((a_, c0, cN, ALU.mult), (b_, s0, sN, ALU.mult), (c_, s0, cN, ALU.mult), (d_, c0, sN, ALU.mult),
                       (c1, a_, b_, ALU.subtract), (s1, c_, d_, ALU.add))
                for k in steps:
                    out, in0, in1, op = ops[k]
                    eng.tensor_tensor(out, in0, in1, op).then_inc(o.sem, o.one((k, m)))
                    if k in (1, 3, 4, 5):
                        eng.wait_ge(o.sem, o.done((k, m)))

            def dve_(dve):
                norm_dve(dve, n, g0)
                dve.wait_ge(consts_in, 48)
                input_matrix(dve, c_dve, 0, tmp[5])
                for name, t, src in (("T0c", Tc, cs), ("T0s", Ts, sn)):
                    dve.tensor_copy(t[:, :, 0], src).then_inc(c_dve.sem, c_dve.one(name))
                dve.wait_ge(c_dve.sem, c_dve.done("T0s"))
                for m in range(5):
                    double(dve, c_dve, m, range(6))
                double(dve, c_dve, 5, (0, 1, 4))
                dve.wait_ge(c_pe.sem, c_pe.done("B0"))
                dve.tensor_copy(Bl[:, :, 0, :], flat(gB).rearrange("p (f s) -> p f s", s=P)).then_inc(tile_free, 1)
                dve.wait_ge(c_pe.sem, c_pe.done("B1"))
                dve.tensor_copy(Bl[:, :, 1, :], flat(gB + 1).rearrange("p (f s) -> p f s", s=P)).then_inc(tile_free, 1)
                dve.wait_ge(tile_free, gB + 2)
                for m in range(DT):
                    dve.scalar_tensor_tensor(av[:, m], h[:, m], gains[:, first + n, m:m + 1], rstd[:], ALU.mult, ALU.mult)\
                       .then_inc(c_dve.sem, c_dve.one(("a", m)))
                dve.wait_ge(c_dve.sem, c_dve.done(("a", DT - 1)))
                dve.wait_ge(c_pool.sem, c_pool.done("R0mz"))

                def bu(hf, k, i, g):
                    o, r, N = h_dve[hf], k + i * 2, META if k == 0 else CH
                    e = HP * N
                    v3 = lambda x: x.rearrange("p (a b) -> p a b", b=N)
                    T1, T2, T3, T4 = (v3(tmp[4 * hf + x][:, 0:e]) for x in range(4))
                    wr, wi = (z_[:, 0:e] for z_ in zs[hf])
                    hs = slice(hf * HP, (hf + 1) * HP)
                    tc, ts_ = Tc[:, hs, 0:N], Ts[:, hs, 0:N]
                    re, im = (flat(g + x).rearrange("p (a b) -> p a b", b=CH)[:, :, 0:N] for x in range(2))
                    decay = (R0m if k == 0 else R0)[:, hs].rearrange("p a b -> p (a b)")

                    def one(ins, name):
                        ins.then_inc(o.sem, o.one(name))
                    if k > 0:
                        dve.wait_ge(y_pe[hf], k + i * 2)
                        L = META if k == 1 else CH
                        last = [tmp[4 * hf + x][:, 0:HP * L].rearrange("p (a b) -> p a b", b=L)[:, :, L - 1]
                                for x in range(4)]
                        one(dve.tensor_tensor(xr[:, hs], last[0], last[1], ALU.add), "xr")
                        one(dve.tensor_tensor(xi[:, hs], last[2], last[3], ALU.add), "xi")
                    else:
                        one(dve.memset(xr[:, hs], 0.0), "xr")
                        one(dve.memset(xi[:, hs], 0.0), "xi")
                    dve.wait_ge(o.sem, o.done("xi", r))
                    one(dve.tensor_tensor(cr[:, hs], xr[:, hs], mag[:, hs], ALU.mult), "c0")
                    one(dve.tensor_tensor(ci[:, hs], xi[:, hs], mag[:, hs], ALU.mult), "c1")
                    dve.wait_ge(bu_pe[hf], k + 1 + i * 2)
                    one(dve.tensor_tensor(T1, re, tc, ALU.mult), "t1")
                    dve.tensor_tensor(T4, re, ts_, ALU.mult).then_inc(tile_free, 1)
                    one(dve.tensor_tensor(T3, im, tc, ALU.mult), "t3")
                    dve.tensor_tensor(T2, im, ts_, ALU.mult).then_inc(tile_free, 1)
                    dve.wait_ge(tile_free, g + 2 + i * 12)
                    one(dve.tensor_tensor(v3(wr), T1, T2, ALU.add), "wr")
                    dve.wait_ge(o.sem, o.done("wr", r))
                    one(dve.tensor_tensor(v3(wr)[:, :, 0], v3(wr)[:, :, 0], cr[:, hs], ALU.add), "c2")
                    dve.wait_ge(o.sem, o.done("c2", r))
                    one(dve.tensor_tensor_scan(wr, decay, wr, 0.0, ALU.mult, ALU.add), "zr")
                    dve.wait_ge(h_pool[hf].sem, h_pool[hf].done("wi", r))
                    one(dve.tensor_tensor(v3(wi)[:, :, 0], v3(wi)[:, :, 0], ci[:, hs], ALU.add), "c3")
                    dve.wait_ge(o.sem, o.done("c3", r))
                    one(dve.tensor_tensor_scan(wi, decay, wi, 0.0, ALU.mult, ALU.add), "zi")
                    one(dve.tensor_tensor(T1, tc, v3(wr), ALU.mult), "p1")
                    dve.wait_ge(o.sem, o.done("zi", r))
                    one(dve.scalar_tensor_tensor(T2, ts_, -1.0, v3(wi), ALU.mult, ALU.mult), "p2")

                def y(hf, k, i, g):
                    N = META if k == 0 else CH
                    dve.wait_ge(y_pe[hf], k + 1 + i * 2)
                    if k >= 2:
                        dve.wait_ge(gelu_done, k - 1 + i * 2)
                    for f in range(4):
                        t = hf * 4 + f
                        ins = dve.scalar_tensor_tensor(ybuf[k % 2][:, t, 0:N], inputs(t, k, i), dcol[:, t:t + 1],
                                                       flat(g)[:, f * CH:f * CH + N], ALU.mult, ALU.add)
                        if f < 3:
                            ins.then_inc(y_read.sem, y_read.one((hf, f)))
                        else:
                            ins.then_inc(tile_free, 1)

                walk(dve, bu, y)
                for m in range(DT):
                    dve.wait_ge(g_act.sem, g_act.done(("hi", m)))
                    dve.tensor_tensor(hid[:, m, 1], av[:, m], hid[:, m, 0].bitcast(F32), ALU.subtract)\
                       .then_inc(g_dve.sem, g_dve.one(("lo", m)))
                for m in range(DT):
                    val, gate = gO + 2 * m, gO + 2 * m + 1
                    gated = work[:, 10]
                    dve.wait_ge(o_act, m + 1)
                    if m >= 1:
                        dve.wait_ge(tile_free, val)
                    dve.tensor_tensor(halves(gated), tile(val), halves(work[:, 8 + m % 2]), ALU.mult).then_inc(tile_free, 1)
                    dve.wait_ge(tile_free, val + 1)
                    dve.tensor_tensor(h[:, m], h[:, m], gated, ALU.add).then_inc(tile_free, 1)
                    dve.wait_ge(tile_free, gate + 1)
                    tail_dve_(dve, n + 1, m)

            def setup_act(act):
                act.wait_ge(c_dve.sem, c_dve.done("clamp"))
                act.activation(sn, ang, ACT.Sin).then_inc(c_act.sem, c_act.one("sin"))
                act.activation(sh, ang, ACT.Sin, scale=0.5).then_inc(c_act.sem, c_act.one("sinh"))

            def load_lam(act):
                act.dma_start(ub[:, 0, 2:2 + 3 * NPAIR], a["s5_lam"]).then_inc(lam_in, 16)

            def act_(act):
                last_stage_over(act, n)
                act.dma_start(work2[:, 0:2048], a["s5_b"]).then_inc(consts_in, 16)
                act.dma_start(Cl.rearrange("p a c s -> p (a c s)"), a["s5_c"]).then_inc(consts_in, 16)
                act.dma_start(dcol, a["s5_d"]).then_inc(consts_in, 16)
                act.wait_ge(consts_in, 48)
                act.activation(Cl[:, :, 1, :], Cl[:, :, 1, :], ACT.Copy, scale=-1.0).then_inc(c_act.sem, c_act.one("negative"))
                act.activation(R0, wide(mag, CH), ACT.Copy).then_inc(c_act.sem, c_act.one("R0"))
                act.activation(R0m, wide(mag, META), ACT.Copy).then_inc(c_act.sem, c_act.one("R0m"))

                def bu(hf, k, i, g):
                    if hf == 1:
                        return
                    if k == 0:
                        act.wait_ge(c_dve.sem, c_dve.done(("a", DT - 1)))
                        act.wait_ge(chunk_zero, 1)
                    if k >= 2:
                        act.wait_ge(bu_pe[1], k - 1 + i * 2)
                    N = META if k == 0 else CH
                    at_ = META + CH * (k - 1) if k else 0
                    for q in range(4):
                        rows = slice(32 * q, 32 * q + 32)
                        src = av[rows, :, at_:at_ + N] if isinstance(i, int) else \
                            av[rows, :, bass.ds(i * (2 * CH) + at_, N)]
                        act.activation(chunk[k % 2][rows, :, q, 0:N], src, ACT.Copy).then_inc(chunk_in, 1)

                def y(hf, k, i, g):
                    if hf == 0:
                        return
                    N = META if k == 0 else CH
                    at_ = META + CH * (k - 1) if k else 0
                    act.wait_ge(tile_free, g + 1 + i * 12)
                    y_ = ybuf[k % 2][:, :, 0:N]
                    act.activation(y_, y_, ACT.Gelu_apprx_tanh).then_inc(gelu_made, 1)
                    act.wait_ge(gelu_made, k + 1 + i * 2)
                    x = av[:, :, at_:at_ + N] if isinstance(i, int) else av[:, :, bass.ds((i + i) * CH + at_, N)]
                    act.activation(x, y_, ACT.Copy).then_inc(gelu_done, 1)

                walk(act, bu, y)
                act.wait_ge(gelu_done, NCH)
                for m in range(DT):
                    act.activation(hid[:, m, 0], av[:, m], ACT.Copy).then_inc(g_act.sem, g_act.one(("hi", m)))
                for m in range(DT):
                    round_unit(act, u0 + 2 * m + AHEAD)
                    if m >= 2:
                        act.wait_ge(tile_free, gO + 2 * m - 3)
                    act.wait_ge(unit_done, u0 + 2 * m + 2)
                    act.activation(halves(work[:, 8 + m % 2]), tile(gO + 2 * m + 1), ACT.Sigmoid).then_inc(o_act, 1)
                    round_unit(act, u0 + 2 * m + 1 + AHEAD)
                    tail_act_(act, n + 1, m)

            def pool_(pool):
                last_stage_over(pool, n)
                pool.wait_ge(consts_in, 48)
                input_matrix(pool, c_pool, 1, spare[:, 4096:5120])
                pool.memset(spare[:, 0:4096], 0.0).then_inc(chunk_zero, 1)
                pool.wait_ge(c_dve.sem, c_dve.done((5, 4)))
                double(pool, c_pool, 5, (2, 3, 5))
                for name, t in (("R0", R0), ("R0m", R0m)):
                    pool.wait_ge(c_act.sem, c_act.done(name))
                    pool.memset(t[:, :, 0], 0.0).then_inc(c_pool.sem, c_pool.one(name + "z"))

                def bu(hf, k, i, g):
                    N, r, order = META if k == 0 else CH, k + i * 2, h_pool[hf]
                    e = HP * N
                    v3 = lambda x: x.rearrange("p (a b) -> p a b", b=N)
                    T3, T4 = (tmp[4 * hf + x][:, 0:e] for x in (2, 3))
                    wr, wi = (z_[:, 0:e] for z_ in zs[hf])
                    hs = slice(hf * HP, (hf + 1) * HP)
                    steps = (("wi", "t3", wi, T3, T4, ALU.subtract), ("p3", "zr", v3(T3), Ts[:, hs, 0:N], v3(wr), ALU.mult),
                             ("p4", "zi", v3(T4), Tc[:, hs, 0:N], v3(wi), ALU.mult))
                    for name, after, out, x, y_, op in steps:
                        pool.wait_ge(h_dve[hf].sem, h_dve[hf].done(after, r))
                        if name == "wi":
                            pool.wait_ge(tile_free, g + 1 + i * 12)
                        if name == "p3":
                            pool.wait_ge(order.sem, order.done("wi", r))
                        pool.tensor_tensor(out, x, y_, op).then_inc(order.sem, order.one(name))

                walk(pool, bu, lambda *_: None)
                for m in range(DT):
                    split_unit(pool, u0 + 2 * m + AHEAD)
                    split_unit(pool, u0 + 2 * m + 1 + AHEAD)
                    tail_pool_(pool, n + 1, m)

            return {"pe": pe_, "dve": dve_, "act": act_, "pool": pool_,
                    "setup": (load_lam, setup_act, setup_dve)}

        def ret(n, u0, g0):
            if "ret" not in stages:
                return {}
            flat_work = work[:].rearrange("p a b -> p (a b)")
            qrot, krot = [work[:, 0], work[:, 1]], [work[:, 2], work[:, 3]]
            ra, rb, rc, rd = (work[:, k] for k in range(4, 8))
            tab = work[:, 8:12]
            vfm = [work[:, 12 + t] for t in range(4)]
            vtok = flat_work[:, 16 * T:16 * T + 2560].rearrange("p (b d) -> p b d", d=RDV)
            gn = flat_work[:, 16 * T + 2560:16 * T + 2576]
            st_ = flat_work[:, 21 * T:25 * T]
            starts = (0, 512, 896, 1152)
            st = [st_[:, s:s + SEQ - b * P] for b, s in enumerate(starts)]
            stm = st_[0:META, 1280:1280 + T]
            mask = work[:, 25]
            fac, mu = work[:, 26], work[:, 27]
            o = [spare[:, (8 + t) * T:(9 + t) * T] for t in range(4)]
            gate = [spare[:, (12 + t) * T:(13 + t) * T] for t in range(4)]
            PROJ = ["q0", "q1", "k0", "k1"] + [f"v{t}" for t in range(4)] + [f"g{t}" for t in range(4)]
            UNIT = {s: k for k, s in enumerate(PROJ)}
            HEAD = ["VA", "VB", "VM", "SM", "S01", "S23", "q0'", "q1'", "O0", "O1", "O2", "O3", "k0'", "k1'", "MEAN",
                    "v0'", "v1'", "VAR", "v2'", "v3'", "g0'", "g1'", "g2'", "g3'"]
            ALONE = [s for s in HEAD if s[-1] != "'"]
            PER = len(HEAD) + DT
            assert PER % 4 == 0
            END = ["VA", "VB", "VM", "SM", "S01", "S23", "w0", "w1", "O0", "O1", "O2", "O3", "w2", "w3", "MEAN", "w4", "w5",
                   "VAR", "w6", "w7"]
            gX = g0 + 1 + len(PROJ)
            gE = gX + PER * (RH - 1) - DT
            gO = gE + len(END)
            assert gO + DT == g0 + 1 + RET_TILES, gO + DT - g0 - 1
            uX, uO = u0 + 12, u0 + 12 + 16 * (RH - 1)

            def walk(eng, project_, attend, out):
                for k, s in enumerate(PROJ):
                    project_(s, 0, 0, u0 + k, g0 + 1 + k)
                def sums(i):
                    for k, s in enumerate(HEAD):
                        if s[-1] == "'":
                            project_(s[:-1], 1, i, uX + UNIT[s[:-1]], gX + k)
                        else:
                            attend(s, 0, i, gX + k, HEAD)
                with eng.Fori(0, RH - 2) as i:
                    sums(i)
                    for m in range(DT):
                        out(m, 0, i, uX + 12 + m // 2, gX + len(HEAD) + m)
                sums(RH - 2)
                for k, s in enumerate(END):
                    if s[0] == "w":
                        m = int(s[1])
                        out(m, 0, RH - 2, uX + 12 + m // 2, gE + k - (RH - 2) * PER)
                    else:
                        attend(s, RH - 1, 0, gE + k, END)
                for m in range(DT):
                    out(m, RH - 1, 0, uO + m // 2, gO + m)

            consts_in, tab_in = sem("ret_consts"), sem("ret_tab")
            p_dve = Order(sem("ret_p_dve"), [c + x for c in "qk" for x in ("c", "d", "1", "a", "b", "2")])
            p_act = Order(sem("ret_p_act"), [f"silu{t}" for t in range(4)])
            a_pe = Order(sem("ret_a_pe"), ALONE + ["SPREAD"])
            a_act = Order(sem("ret_a_act"), ["VA", "VB"] + [f"sq{t}" for t in range(4)] +
                          [f"hi{t}" for t in range(4)])
            a_dve = Order(sem("ret_a_dve"), ["SM", "S0", "S2"] + [f"o{t}" for t in range(4)] + ["s0", "s1", "s2"] +
                          [f"d{t}" for t in range(4)] + ["clear", "v0", "v1", "v2"] + [("f", s) for s in RSQRT] +
                          ["n0", "n1", "n2"] + [f"z{t}" for t in range(4)])
            a_pool = Order(sem("ret_a_pool"), [f"lo{t}" for t in range(4)])
            out_even = sem("ret_out_even")

            def pe_(pe):
                first_tiles_pe(pe, n, u0, g0)
                x = split_tiles(xs, range(DT))

                def proj(s, r, i, u, g):
                    if s in ("q0", "q1") and r == 0:
                        return
                    pe.wait_ge(lo_ready, u + 1 + i * 16)
                    pe.wait_ge(tile_free, g - 3 + i * PER)
                    project(pe, tile(g), u % RING, 0, x, True, True, unit_done)
                    if r and s == "v2":
                        spread(i, g - 1)

                def spread(R, g):
                    pe.wait_ge(a_dve.sem, a_dve.done(("f", LAST), R))
                    spread_pe(pe, g, fac).then_inc(a_pe.sem, a_pe.one("SPREAD"))

                def attend(s, r, i, g, seq):
                    R = r + i
                    pe.wait_ge(tile_free, g - 3 + i * PER)
                    f = flat(g)
                    if s in ("VA", "VB"):
                        for b in range(2):
                            blk = b + 2 * (s == "VB")
                            for t in range(4):
                                mm = pe.transpose(f[:, b * 512 + t * P:b * 512 + (t + 1) * P],
                                                  vfm[t][:, META + blk * P:META + (blk + 1) * P], ident[:])
                    elif s == "VM":
                        for t in range(4):
                            mm = pe.transpose(f[0:META, t * P:(t + 1) * P], vfm[t][:, 0:META], ident[:])
                    elif s == "SM":
                        pe.wait_ge(p_dve.sem, p_dve.done("k2", R))
                        for c, q0, q1 in ((0, META, T), (512, 0, META)):
                            for t in range(2):
                                mm = pe.matmul(f[0:META, c:c + q1 - q0], krot[t][:, 0:META], qrot[t][:, q0:q1],
                                               start=t == 0, stop=t == 1)
                    elif s[0] == "S":
                        for j in range(2):
                            b = int(s[1 + j])
                            k0 = META + b * P
                            for t in range(2):
                                mm = pe.matmul(f[:, j * 512:j * 512 + T - k0], krot[t][:, k0:k0 + P], qrot[t][:, k0:T],
                                               start=t == 0, stop=t == 1)
                    elif s[0] == "O":
                        t = int(s[1])
                        d = slice(t * P, (t + 1) * P)
                        if t == 0:
                            pe.wait_ge(tile_free, g_of("S23", g, seq) + 1 + i * PER)
                        pe.matmul(f[:, 512:512 + META], vtok[0:META, 4, d], stm[:, SEQ:T], start=True, stop=True)
                        pe.matmul(f[:, 0:SEQ], vtok[0:META, 4, d], stm[:, 0:SEQ], start=True, stop=False)
                        for b in range(QB):
                            mm = pe.matmul(f[:, b * P:SEQ], vtok[:, b, d], st[b], start=False, stop=b == QB - 1)
                    elif s == "MEAN":
                        pe.wait_ge(a_dve.sem, a_dve.done("s2", R))
                        for q in range(2):
                            mm = pe.matmul(tile(g)[:, q], ones[:], fac[:, q * HALF:(q + 1) * HALF], start=True, stop=True)
                    else:
                        pe.wait_ge(a_dve.sem, a_dve.done("v2", R))
                        mm = sums_pe(pe, g, SUMS, [(scr[:, 0], P)])
                    mm.then_inc(a_pe.sem, a_pe.one(s))

                def out(m, r, i, u, g):
                    split = {k: (a_pool.sem, a_pool.done(f"lo{k}", r + i)) for k in range(4) if m == 0}
                    if m % 2 == 0:
                        pe.wait_ge(lo_ready, u + 1 + i * 16)
                    pe.wait_ge(tile_free, g - 3 + i * PER)
                    project(pe, tile(g), u % RING, 4 * (m % 2), split_tiles(hid, range(4)), True, True,
                            unit_done if m % 2 else out_even, split)
                    if m == DT - 1 and isinstance(i, int) and r == 0:
                        spread(RH - 1, g + i * PER - (END.index("w7") - END.index("VAR")))

                walk(pe, proj, attend, out)

            def g_of(s, g, seq):
                return g - (seq.index("O0") - seq.index(s))

            def dve_(dve):
                norm_dve(dve, n, g0)

                def one(order, name, ins):
                    ins.then_inc(order.sem, order.one(name))

                def rope(c, out, r):
                    j = 2 * (c == "k")
                    one(p_dve, c + "c", dve.tensor_tensor(rc, ra, tab[:, j], ALU.mult))
                    one(p_dve, c + "d", dve.tensor_tensor(rd, rb, tab[:, j + 1], ALU.mult))
                    dve.wait_ge(p_dve.sem, p_dve.done(c + "d", r))
                    one(p_dve, c + "1", dve.tensor_tensor(out[0], rc, rd, ALU.subtract))
                    one(p_dve, c + "a", dve.tensor_tensor(ra, ra, tab[:, j + 1], ALU.mult))
                    one(p_dve, c + "b", dve.tensor_tensor(rb, rb, tab[:, j], ALU.mult))
                    dve.wait_ge(p_dve.sem, p_dve.done(c + "b", r))
                    one(p_dve, c + "2", dve.tensor_tensor(out[1], ra, rb, ALU.add))
                    dve.wait_ge(p_dve.sem, p_dve.done(c + "2", r))

                def proj(s, r, i, u, g):
                    R = r + i
                    dst = {"q0": ra, "q1": rb, "k0": ra, "k1": rb}.get(s)
                    if dst is None:
                        dst = (vfm if s[0] == "v" else gate)[int(s[1])]
                    dve.wait_ge(unit_done, u + 1 + i * 16)
                    if s == "q0":
                        dve.wait_ge(tab_in, 16 * r + 16 + i * 16)
                    dve.tensor_tensor(halves(dst), tile(g), halves(rstd[:]), ALU.mult).then_inc(tile_free, 1)
                    if s in ("q1", "k1"):
                        dve.wait_ge(tile_free, g + 1 + i * PER)
                    if s == "q1":
                        rope("q", qrot, R)
                    elif s == "k1" and r == 0:
                        rope("k", krot, R)

                def attend(s, r, i, g, seq):
                    R = r + i
                    f = flat(g)
                    dve.wait_ge(a_pe.sem, a_pe.done(s, R))
                    if s in ("VA", "VB"):
                        dve.wait_ge(a_act.sem, a_act.done(s, R))
                        dve.tensor_copy(vtok[:, 1 + 2 * (s == "VB")], f[:, 512:1024]).then_inc(tile_free, 1)
                    elif s == "VM":
                        dve.tensor_copy(vtok[0:META, 4], f[0:META, 0:512]).then_inc(tile_free, 1)
                    elif s == "SM":
                        one(a_dve, "SM", dve.tensor_copy(stm[:, 0:SEQ], f[0:META, 0:512]))
                        dve.tensor_tensor(stm[:, SEQ:T], f[0:META, 512:512 + META], mask[0:META, 0:META], ALU.mult)\
                           .then_inc(tile_free, 1)
                    elif s[0] == "S":
                        b = int(s[1])
                        w = SEQ - b * P
                        one(a_dve, f"S{b}", dve.tensor_tensor(st[b], f[:, 0:w], mask[:, 0:w], ALU.mult))
                        dve.tensor_tensor(st[b + 1], f[:, 512:512 + w - P], mask[:, 0:w - P], ALU.mult).then_inc(tile_free, 1)
                    elif s[0] == "O":
                        t = int(s[1])
                        one(a_dve, f"o{t}", dve.tensor_copy(o[t][:, 0:META], f[:, 512:512 + META]))
                        dve.tensor_copy(o[t][:, META:], f[:, 0:SEQ]).then_inc(tile_free, 1)
                        if t == 3:
                            dve.wait_ge(tile_free, g + 1 + i * PER)
                            for k in range(3):
                                one(a_dve, f"s{k}", dve.tensor_tensor(fac, o[0] if k == 0 else fac, o[k + 1], ALU.add))
                                dve.wait_ge(a_dve.sem, a_dve.done(f"s{k}", R))
                    elif s == "MEAN":
                        dve.tensor_scalar(halves(mu), tile(g), 1.0 / RDV, None, ALU.mult).then_inc(tile_free, 1)
                        dve.wait_ge(tile_free, g + 1 + i * PER)
                        for t in range(4):
                            one(a_dve, f"d{t}", dve.tensor_tensor(o[t], o[t], mu, ALU.subtract))
                        if r == 0:
                            rope("k", krot, 1 + i)
                    else:
                        mean_rsqrt(dve, g, [SUMS], RDV, [fac], ub[:, 1, 2:], a_dve, "f", R)
                        finish(dve, R, g, i)

                def squares(R):
                    dve.memset(fac, 0.0).then_inc(a_dve.sem, a_dve.one("clear"))
                    for k in range(3):
                        dve.wait_ge(a_act.sem, a_act.done(f"sq{k + 1}", R))
                        one(a_dve, f"v{k}", dve.tensor_tensor(scr[:, 0], scr[:, 0], scr[:, k + 1], ALU.add))
                        dve.wait_ge(a_dve.sem, a_dve.done(f"v{k}", R))

                def finish(dve, R, g, i):
                    dve.wait_ge(p_act.sem, p_act.done("silu3", R))
                    dve.wait_ge(a_pe.sem, a_pe.done("SPREAD", R))
                    for t in range(4):
                        col = gn[:, 4 * R + t:4 * R + t + 1] if isinstance(R, int) else gn[:, bass.ds(R * 4 + t, 1)]
                        ins = dve.scalar_tensor_tensor(halves(o[t]), halves(o[t]), col, tile(g), ALU.mult, ALU.mult)
                        if t < 3:
                            one(a_dve, f"n{t}", ins)
                        else:
                            ins.then_inc(tile_free, 1)
                    dve.wait_ge(tile_free, g + 1 + i * PER)
                    for t in range(4):
                        one(a_dve, f"z{t}", dve.tensor_tensor(o[t], o[t], gate[t], ALU.mult))
                    dve.wait_ge(a_dve.sem, a_dve.done("z3", R))

                def out(m, r, i, u, g):
                    if m % 2:
                        dve.wait_ge(unit_done, u + 1 + i * 16)
                    else:
                        dve.wait_ge(out_even, 4 * r + m // 2 + 1 + i * 4)
                    dve.tensor_tensor(halves(h[:, m]), tile(g), halves(h[:, m]), ALU.add).then_inc(tile_free, 1)
                    if r:
                        dve.wait_ge(tile_free, g + 1)
                        tail_dve_(dve, n + 1, m)

                def proj_(s, r, i, u, g):
                    proj(s, r, i, u, g)
                    if r and s == "v0":
                        squares(i)

                def out_(m, r, i, u, g):
                    out(m, r, i, u, g)
                    if m == 4 and isinstance(i, int) and r == 0:
                        squares(RH - 1)

                dve.wait_ge(consts_in, 32)
                walk(dve, proj_, attend, out_)

            def act_(act):
                last_stage_over(act, n)
                act.dma_start(mask, a["ret_mask"]).then_inc(consts_in, 16)
                act.dma_start(gn, a["ret_gn"]).then_inc(consts_in, 16)
                act.dma_start(tab, a["ret_tab"][0]).then_inc(tab_in, 16)

                def f(out, x, func, name, order=a_act, **kw):
                    act.activation(out, x, func, **kw).then_inc(order.sem, order.one(name))

                def proj(s, r, i, u, g):
                    round_unit(act, u + AHEAD, i, 16)
                    if s[0] == "g":
                        t = int(s[1])
                        act.wait_ge(tile_free, g + 1 + i * PER)
                        f(gate[t], gate[t], ACT.Silu, f"silu{t}", p_act)
                    if r and s == "v3":
                        highs(i)

                def highs(R):
                    for t in range(4):
                        act.wait_ge(a_dve.sem, a_dve.done(f"z{t}", R))
                        f(hid[:, t, 0], o[t], ACT.Copy, f"hi{t}")

                def attend(s, r, i, g, seq):
                    R = r + i
                    if s in ("VA", "VB"):
                        act.wait_ge(a_pe.sem, a_pe.done(s, R))
                        f(vtok[:, 2 * (s == "VB")], flat(g)[:, 0:512], ACT.Copy, s)
                        if s == "VA" and r == 0:
                            act.wait_ge(p_dve.sem, p_dve.done("k2", R))
                            act.dma_start(tab, a["ret_tab"][bass.ds(i + 1, 1)].rearrange("a p c t -> p (a c) t"))\
                               .then_inc(tab_in, 16)
                    elif s == "MEAN":
                        for t in range(4):
                            act.wait_ge(a_dve.sem, a_dve.done(f"d{t}", R))
                            f(scr[:, t], o[t], ACT.Square, f"sq{t}")

                def out(m, r, i, u, g):
                    if m % 2 == 0:
                        round_unit(act, u + AHEAD, i, 16)
                    if m == DT - 1 and isinstance(i, int) and r == 0:
                        highs(RH - 1)
                    if r:
                        tail_act_(act, n + 1, m)

                walk(act, proj, attend, out)

            def pool_(pool):
                def lows(R):
                    for t in range(4):
                        pool.wait_ge(a_act.sem, a_act.done(f"hi{t}", R))
                        pool.tensor_tensor(hid[:, t, 1], o[t], hid[:, t, 0].bitcast(F32), ALU.subtract)\
                            .then_inc(a_pool.sem, a_pool.one(f"lo{t}"))

                def proj(s, r, i, u, g):
                    split_unit(pool, u + AHEAD, i, 16)
                    if r and s == "v3":
                        lows(i)

                def out(m, r, i, u, g):
                    if m % 2 == 0:
                        split_unit(pool, u + AHEAD, i, 16)
                    if m == DT - 1 and isinstance(i, int) and r == 0:
                        lows(RH - 1)
                    if r:
                        tail_pool_(pool, n + 1, m)

                walk(pool, proj, lambda *_: None, out)

            return {"pe": pe_, "dve": dve_, "act": act_, "pool": pool_}
        makers = {"mla": mla, "hgrn": hgrn, "s5": s5, "ret": ret}
        mixer = {n: makers[kind](n, u0, g0) for n, (kind, name, u0, g0) in enumerate(at) if kind != "ffn"}

        block = ctx.enter_context(nc.Block())

        @block.sync
        def _(sp):
            sp.dma_start(gains[:], a["gains"]).then_inc(gains_in, 16)
            for m in range(DT):
                sp.dma_start(h[:, m], a["h0"][m * P:(m + 1) * P]).then_inc(h_in[m], 16)
                if m % 2 == 0:
                    load_unit(sp, m // 2)
            for name, t in (("ones", ones), ("pick", pick), ("ident", ident)):
                sp.dma_start(t[:], a[name]).then_inc(consts, 16)
            laps = n_units // RING
            with sp.Fori(1, laps) as i:
                for s in range(RING):
                    load_unit(sp, s, i, RING)
            for u in range(laps * RING, n_units):
                load_unit(sp, u)
            kind, name, u0, g0 = at[-1]
            for m in range(DT):
                sp.wait_ge(tile_free, g0 + LAST_TILES[kind] + m + 1)
                if kind != "ffn" or DEBUG:
                    sp.wait_ge(tail_pool.sem, tail_pool.done("lo", 8 * len(at) + m))
                sp.dma_start(a["out"][m * P:(m + 1) * P], h[:, m, META if a["out"].shape[1] == SEQ else 0:]).then_inc(out_written, 16)
            sp.wait_ge(out_written, 16 * DT)

        @block.tensor
        def _(pe):
            for n, (kind, name, u0, g0) in enumerate(at):
                if kind == "ffn":
                    ffn_pe(pe, n, int(name[3]) - layer0, u0, g0)
                else:
                    mixer[n]["pe"](pe)

        @block.vector
        def _(dve):
            dve.sem_inc(tile_free, 4)
            dve.memset(sqsum[:], 0.0).then_inc(sum_cleared, 1)
            dve.memset(ub[:, :, 0:2], 0.0).then_inc(pads, 1)
            if setup_of(0):
                setup_of(0)[2](dve)
            dve.wait_ge(gains_in, 16)
            for m in range(DT):
                dve.wait_ge(h_in[m], 16)
                tail_dve_(dve, 0, m)
            for n, (kind, name, u0, g0) in enumerate(at):
                last = n == len(at) - 1 and not DEBUG
                if kind == "ffn":
                    ffn_dve(dve, n, int(name[3]) - layer0, u0, g0, last)
                else:
                    mixer[n]["dve"](dve)

        @block.scalar
        def _(act):
            act.dma_start(convp[:], a["convp"][layer0]).then_inc(convp_landed, 16)
            if setup_of(0):
                setup_of(0)[0](act)
                setup_of(0)[1](act)
            for m in range(DT):
                if m in (0, 2, 4):
                    round_unit(act, m // 2)
                tail_act_(act, 0, m)
            for n, (kind, name, u0, g0) in enumerate(at):
                last = n == len(at) - 1 and not DEBUG
                if kind == "ffn":
                    ffn_act(act, n, int(name[3]) - layer0, u0, g0, last)
                    if not last and n + 1 < len(at):
                        act.dma_start(convp[:], a["convp"][int(name[3]) + 1]).then_inc(convp_landed, 16)
                else:
                    mixer[n]["act"](act)

        @block.gpsimd
        def _(pool):
            pool.sem_inc(up_pool.sem, 1)
            for m in range(DT):
                if m in (0, 2, 4):
                    split_unit(pool, m // 2)
                tail_pool_(pool, 0, m)
            for n, (kind, name, u0, g0) in enumerate(at):
                last = n == len(at) - 1 and not DEBUG
                if kind == "ffn":
                    ffn_pool(pool, n, int(name[3]) - layer0, u0, g0, last)
                else:
                    mixer[n]["pool"](pool)

def _mla_units(z):
    import numpy as np
    down = np.asarray(z["mla_w_down"][0])
    k1, k2 = np.split(down[:, QL + KVL:], 2, 1)
    down = _blocks(np.concatenate([down[:, :QL + KVL], k1, k2, k2, k1], 1))
    out = [_unit(b) for b in down]
    uq = np.asarray(z["mla_w_uq"][0]).reshape(QL, HEADS, QK)
    ukv = np.asarray(z["mla_w_ukv"][0]).reshape(KVL, HEADS, NOPE + VDIM)
    for h in range(HEADS):
        q1, q2 = np.split(uq[:, h, NOPE:], 2, 1)
        q = _blocks(np.concatenate([uq[:, h, :NOPE], q1, q2, q2, q1], 1))
        out.append(_unit(list(q[0]) + list(q[1])))
        kv = _blocks(ukv[:, h])
        out.append(_unit(list(kv[0]) + list(kv[1])))
    return out + [_unit(b) for b in _blocks(z["mla_w_o"][0])]


def _rope(dim):
    import numpy as np
    inv = (1.0 / (np.float32(10000.0) ** (np.arange(0, dim, 2, dtype=np.float32) / np.float32(dim)))).astype(np.float32)
    ang = inv[:, None] * np.arange(T, dtype=np.float32)[None]
    return np.cos(ang.astype(np.float64)), np.sin(ang.astype(np.float64))


def _mla_arrays(z):
    import numpy as np
    c, s = _rope(ROPE)

    def head(g):
        g1, g2 = np.split(np.asarray(g)[NOPE:], 2)
        return [np.asarray(g)[:NOPE], np.concatenate([g1, g2, g2, g1])]

    cols = [_cols(z["mla_cq_norm_g"][0]), _cols(z["mla_ckv_norm_g"][0])]
    cols += [v[:, None] for v in head(z["mla_q_head_g"][0]) + head(z["mla_k_head_g"][0])]
    return {"mla_tab": np.concatenate([c, c, -s, s]), "mla_par": np.concatenate(cols, 1)}


def _hgrn_units(z):
    import numpy as np
    q, f, i, g = (_blocks(w) for w in np.split(np.asarray(z["hgrn_w_in"][0]), 4, 1))
    out = []
    for h in range(HEADS):
        out += [_unit(f[h]), _unit(q[h]), _unit(i[h]), _unit(g[h])]
    return out + [_unit(b) for b in _blocks(z["hgrn_w_o"][0])]


def _hgrn_arrays(z):
    import numpy as np
    j, i = np.arange(P)[:, None], np.arange(P)[None]
    masks = [(j // 16 == i // 16) & (j <= i)]
    for w in (16, 32, 64):
        masks.append((j // (2 * w) == i // (2 * w)) & (j // w + 1 == i // w))
    scan = np.broadcast_to((np.arange(T) % 16 != 0)[None], (P, T))
    logits = np.asarray(z["hgrn_lb_logits"]).reshape(DEPTH, HEADS, P).transpose(2, 0, 1).reshape(P, -1)
    par = np.concatenate([_cols(z["hgrn_o_norm_g"][0]), np.zeros((P, 3)), logits], 1)
    return {"hgrn_masks": np.concatenate(masks, 1), "hgrn_scan": scan, "hgrn_par": par}



def _s5_units(z):
    w = _blocks(z["s5_w_glu"][0])
    return [_unit(w[m + DT * x]) for m in range(DT) for x in range(2)]


def _s5_arrays(z):
    import numpy as np
    G, NPAIR, K = D // 16, D // 32, 16

    def states(v):
        v = np.asarray(v)
        v = v.reshape((NPAIR, 2) + v.shape[1:])
        return np.moveaxis(v, 0, 2).reshape((P, NPAIR) + v.shape[3:])

    def paired(v):
        v, out = states(v), np.zeros((P, NPAIR, 2, K), np.float32)
        for g in range(2):
            out[g * S5P:(g + 1) * S5P, :, g] = v[g * S5P:(g + 1) * S5P]
        return out.reshape(P, NPAIR, 2 * K)

    dt = np.broadcast_to(np.asarray(z["s5_log_dt"][0])[:, None], (G, S5P))
    lam = np.concatenate([states(v) for v in (z["s5_lam_re"][0], z["s5_lam_im"][0], dt)], 1)
    b = np.concatenate([paired(z[k][0]).reshape(P, -1) for k in ("s5_b_re", "s5_b_im")], 1)
    c = np.stack([paired(np.asarray(z[k][0]).transpose(0, 2, 1)) for k in ("s5_c_re", "s5_c_im")], 2)
    return {"s5_lam": lam, "s5_b": b, "s5_c": c.reshape(P, -1), "s5_d": _cols(z["s5_d"][0])}



def _ret_units(z):
    import numpy as np
    w = np.asarray(z["ret_w_in"][0])
    q, k, v, g = (_blocks(x) for x in np.split(w, [RH * RDK, 2 * RH * RDK, 2 * RH * RDK + RH * RDV], 1))
    wo = _blocks(z["ret_w_o"][0])
    proj = [[_unit(b) for b in list(q[2 * h:2 * h + 2]) + list(k[2 * h:2 * h + 2]) +
             list(v[4 * h:4 * h + 4]) + list(g[4 * h:4 * h + 4])] for h in range(RH)]
    outs = [[_unit(list(wo[m, 4 * h:4 * h + 4]) + list(wo[m + 1, 4 * h:4 * h + 4])) for m in range(0, DT, 2)]
            for h in range(RH)]
    out = proj[0]
    for h in range(RH):
        out = out + (proj[h + 1] if h + 1 < RH else []) + outs[h]
    return out


def _ret_arrays(z):
    import numpy as np
    c, s = _rope(RDK)
    t = np.arange(T, dtype=np.float64)
    tabs = []
    for h in range(RH):
        up = (1.0 - 2.0 ** (-5 - h)) ** t
        down = RDK ** -0.5 / up
        tabs.append(np.stack([c * up, s * up, c * down, s * down], 1))
    mask = np.arange(T)[None] >= np.arange(P)[:, None]
    return {"ret_tab": np.stack(tabs), "ret_mask": mask, "ret_gn": _cols(z["ret_gn_g"][0])}


HOST_UNITS = {"mla": _mla_units, "hgrn": _hgrn_units, "s5": _s5_units,
              "ret": _ret_units}
HOST_ARRAYS = {"mla": _mla_arrays, "hgrn": _hgrn_arrays, "s5": _s5_arrays,
               "ret": _ret_arrays}
DEBUG = False


def _blocks(w):
    import numpy as np
    K, M = w.shape
    return np.asarray(w).reshape(K // P, P, M // P, P).transpose(2, 0, 1, 3)


def _unit(blocks):
    import numpy as np
    u = np.zeros((P, BLK * P), np.float32)
    for k, b in enumerate(blocks):
        u[:, k * P:(k + 1) * P] = b
    return u


def _cols(v):
    import numpy as np
    return np.ascontiguousarray(np.asarray(v).reshape(-1, P).T)


def _stream(stages, z):
    out = []
    for s in stages:
        kind = "ffn" if s[:3] == "ffn" else s
        if kind == "ffn":
            n = int(s[3])
            up, down = _blocks(z["ffn_w_up"][n]), _blocks(z["ffn_w_down"][n])
            for k in range(KT):
                out += [_unit(up[k]), _unit(up[KT + k])]
            for m in range(DT):
                k0 = 0
                for nb in DOWN:
                    out.append(_unit(down[m][k0:k0 + nb]))
                    k0 += nb
        else:
            out += HOST_UNITS[kind](z)
    return out


def arrays(z, stages, h0):
    import numpy as np
    f = lambda v: np.ascontiguousarray(v, dtype=np.float32)
    r = {"stream": f(np.stack(_stream(stages, z))), "h0": f(h0),
         "ones": f(np.ones((P, P))), "ident": f(np.eye(P)),
         "pick": f(np.broadcast_to((np.arange(P) % 32 == 0)[:, None], (P, P)))}
    g = [_cols(np.asarray(z[k])[n]) for n in range(DEPTH) for k in ("norm_mix_g", "norm_ffn_g")]
    r["gains"] = f(np.stack(g, 1))
    cw, cb = np.asarray(z["ffn_conv_w"]), np.asarray(z["ffn_conv_b"])
    cp = np.stack([cw[:, 0], cw[:, 1], cw[:, 2], cb], -1)
    cp = cp.reshape(DEPTH, 2, KT, P, 4).transpose(0, 3, 2, 1, 4).reshape(DEPTH, P, 2 * KT, 4)
    r["convp"] = f(cp)
    for s in stages:
        kind = "ffn" if s[:3] == "ffn" else s
        if kind != "ffn":
            r.update({k: f(v) for k, v in HOST_ARRAYS[kind](z).items()})
    return r


def kernel(**inputs):
    import numpy as _np
    import concourse.bacc as _bacc
    from concourse import mybir as _mybir
    from concourse.bass_utils import run_bass_kernel_spmd as _run

    z = {k: _np.asarray(v) for k, v in inputs.items()}
    h0 = _np.concatenate([z["meta_tokens"], z["x"][0]], 0).T
    given = arrays(z, SUBLAYERS, h0)
    nc = _bacc.Bacc("TRN2", target_bir_lowering=False, num_devices=1)
    a = {k: nc.dram_tensor("in_" + k, v.shape, _mybir.dt.from_np(v.dtype), kind="ExternalInput").ap()
         for k, v in given.items()}
    a["out"] = nc.dram_tensor("out_0", (D, SEQ), F32, kind="ExternalOutput").ap()
    trunk(nc, a, SUBLAYERS)
    r = _run(nc, [{"in_" + k: v for k, v in given.items()}], core_ids=[0])
    return _np.ascontiguousarray(r.results[0]["out_0"].T)[None]
```
